# Optimizing a Trainium2 kernel written in Bass

```python
import math
import jax, jax.numpy as jnp
from jax import lax
import numpy as np

D_MODEL = 1024
BATCH = 1
SEQ = 512
DEPTH = 2

MEM_LEN = 256
D_MIX = D_MODEL
NORM_EPS = 1e-6
DA_HEADS = 4
DA_HALF = D_MIX // (4 * DA_HEADS)
DA_VDIM = 2 * DA_HALF
DA_QK = DA_HEADS * 2 * DA_HALF
DA_V = DA_HEADS * DA_VDIM
Q_BLOCK = 128
SSD_HEADS = 4
SSD_INNER = D_MIX // 4
SSD_HEAD_DIM = SSD_INNER // SSD_HEADS
SSD_GROUPS = 2
SSD_STATE = 128
SSD_CONV = 4
SSD_CHUNK = 128
SSD_CONV_DIM = SSD_INNER + 2 * SSD_GROUPS * SSD_STATE
GDN_HEADS = 4
GDN_V = D_MIX // 4
GDN_DV = GDN_V // GDN_HEADS
GDN_DK = GDN_DV
GDN_QK = GDN_HEADS * GDN_DK
GDN_CONV = 4
GDN_CHUNK = 64
GDN_CONV_DIM = 2 * GDN_QK + GDN_V
IN_SIZES = (DA_QK, DA_QK, DA_V, SSD_INNER, SSD_CONV_DIM, SSD_HEADS, GDN_CONV_DIM, GDN_V, GDN_HEADS, GDN_HEADS)
P_IN = 2 * DA_QK + DA_V + SSD_INNER + SSD_CONV_DIM + SSD_HEADS + GDN_CONV_DIM + GDN_V + 2 * GDN_HEADS
X_HEADS = 4
X_HEAD_DIM = D_MODEL // X_HEADS
D_FF = -(-8 * D_MODEL // (3 * 256)) * 256

kernel_name = 'hymba_style_diffattn_ssd_gdn_hybrid'

def rms_norm(x, g, eps=NORM_EPS):
    xf = x.astype(jnp.float32)
    y = xf * lax.rsqrt(jnp.mean(xf * xf, axis=-1, keepdims=True) + eps)
    return (y * g.astype(jnp.float32)).astype(x.dtype)

def l2_norm(x, eps=1e-6):
    xf = x.astype(jnp.float32)
    return xf * lax.rsqrt(jnp.sum(xf * xf, axis=-1, keepdims=True) + eps)

def causal_depthwise_conv(x, w):
    k = w.shape[0]
    return lax.conv_general_dilated(
        x, w.astype(x.dtype)[:, None, :], window_strides=(1,), padding=[(k - 1, 0)],
        dimension_numbers=('NWC', 'WIO', 'NWC'), feature_group_count=x.shape[-1])

def diff_attention(q, k, v, lam, q_g, k_g, sub_g, lambda_init):
    bsz, seq, nh, _, dh = q.shape
    q = rms_norm(q, q_g)
    k = rms_norm(k, k_g)
    nb = seq // Q_BLOCK
    qb = jnp.moveaxis(q.reshape(bsz, nb, Q_BLOCK, nh, 2, dh), 1, 0)
    kpos = jnp.arange(seq)
    scale = dh ** -0.5

    def block(args):
        qblk, i = args
        qpos = i * Q_BLOCK + jnp.arange(Q_BLOCK)
        s = jnp.einsum('bqhcd,bkhcd->bhcqk', qblk, k).astype(jnp.float32) * scale
        s = jnp.where((kpos[None, :] <= qpos[:, None])[None, None, None], s, -jnp.inf)
        p = jax.nn.softmax(s, axis=-1)
        w = p[:, :, 0] - lam * p[:, :, 1]
        return jnp.einsum('bhqk,bkhe->bqhe', w.astype(v.dtype), v)

    o = lax.map(block, (qb, jnp.arange(nb)))
    o = jnp.moveaxis(o, 0, 1).reshape(bsz, seq, nh, 2 * dh)
    o = rms_norm(o, sub_g) * (1.0 - lambda_init)
    return o.reshape(bsz, seq, nh * 2 * dh)

def ssd_chunked(x, dt, a_neg, bm, cm):
    bsz, seq, nh, hp = x.shape
    n = bm.shape[-1]
    t = SSD_CHUNK
    nc = seq // t
    xd = (x * dt[..., None]).reshape(bsz, nc, t, nh, hp)
    bc = bm.reshape(bsz, nc, t, nh, n)
    cc = cm.reshape(bsz, nc, t, nh, n)
    a_cum = jnp.cumsum((dt * a_neg).reshape(bsz, nc, t, nh), axis=2)
    tril = jnp.arange(t)[:, None] >= jnp.arange(t)[None, :]
    seg = a_cum[:, :, :, None, :] - a_cum[:, :, None, :, :]
    lmat = jnp.exp(jnp.where(tril[None, None, :, :, None], seg, -jnp.inf))
    scores = jnp.einsum('bclhn,bcshn->bclsh', cc, bc) * lmat
    y_diag = jnp.einsum('bclsh,bcshp->bclhp', scores, xd)
    decay_states = jnp.exp(a_cum[:, :, -1:, :] - a_cum)
    states = jnp.einsum('bclhn,bclh,bclhp->bchpn', bc, decay_states, xd)
    chunk_decay = jnp.exp(a_cum[:, :, -1, :])

    def step(h, inp):
        st, dec = inp
        return h * dec[:, :, None, None] + st, h

    h0 = jnp.zeros((bsz, nh, hp, n), jnp.float32)
    _, h_prev = lax.scan(step, h0, (jnp.moveaxis(states, 1, 0), jnp.moveaxis(chunk_decay, 1, 0)))
    h_prev = jnp.moveaxis(h_prev, 0, 1)
    y_off = jnp.einsum('bclhn,bchpn,bclh->bclhp', cc, h_prev, jnp.exp(a_cum))
    return (y_diag + y_off).reshape(bsz, seq, nh, hp)

def ssd_mixer(z, xbc, dt_raw, conv_w, conv_b, dt_bias, a_log, d_skip, norm_g):
    bsz, seq, _ = z.shape
    xbc = jax.nn.silu(causal_depthwise_conv(xbc, conv_w) + conv_b.astype(xbc.dtype))
    xs, bm, cm = jnp.split(xbc, [SSD_INNER, SSD_INNER + SSD_GROUPS * SSD_STATE], axis=-1)
    xs = xs.astype(jnp.float32).reshape(bsz, seq, SSD_HEADS, SSD_HEAD_DIM)
    rep = SSD_HEADS // SSD_GROUPS
    bm = jnp.repeat(bm.astype(jnp.float32).reshape(bsz, seq, SSD_GROUPS, SSD_STATE), rep, axis=2)
    cm = jnp.repeat(cm.astype(jnp.float32).reshape(bsz, seq, SSD_GROUPS, SSD_STATE), rep, axis=2)
    dt = jax.nn.softplus(dt_raw.astype(jnp.float32) + dt_bias.astype(jnp.float32))
    a_neg = -jnp.exp(a_log.astype(jnp.float32))
    y = ssd_chunked(xs, dt, a_neg, bm, cm) + d_skip.astype(jnp.float32)[:, None] * xs
    y = y.reshape(bsz, seq, SSD_INNER) * jax.nn.silu(z.astype(jnp.float32))
    gsz = SSD_INNER // SSD_GROUPS
    y = rms_norm(y.reshape(bsz, seq, SSD_GROUPS, gsz), norm_g.reshape(SSD_GROUPS, gsz))
    return y.reshape(bsz, seq, SSD_INNER).astype(z.dtype)

def gated_delta_chunked(q, k, v, g, beta):
    bsz, seq, nh, dk = q.shape
    dv = v.shape[-1]
    t = GDN_CHUNK
    nc = seq // t
    to_c = lambda a: a.reshape(bsz, nc, t, nh, a.shape[-1]).transpose(0, 3, 1, 2, 4)
    q = to_c(q * dk ** -0.5)
    k = to_c(k)
    v = to_c(v)
    beta = beta.reshape(bsz, nc, t, nh).transpose(0, 3, 1, 2)
    g = jnp.cumsum(g.reshape(bsz, nc, t, nh).transpose(0, 3, 1, 2), axis=-1)
    tril = jnp.arange(t)[:, None] >= jnp.arange(t)[None, :]
    strict = jnp.arange(t)[:, None] > jnp.arange(t)[None, :]
    decay = jnp.exp(jnp.where(tril, g[..., :, None] - g[..., None, :], -jnp.inf))
    k_beta = k * beta[..., None]
    v_beta = v * beta[..., None]
    a_low = jnp.where(strict, jnp.einsum('bhcid,bhcjd->bhcij', k_beta, k) * decay, 0.0)
    eye = jnp.broadcast_to(jnp.eye(t, dtype=jnp.float32), a_low.shape)
    t_inv = lax.linalg.triangular_solve(eye + a_low, eye, left_side=True, lower=True)
    u = jnp.einsum('bhcij,bhcjd->bhcid', t_inv, v_beta)
    w = jnp.einsum('bhcij,bhcjd->bhcid', t_inv, k_beta * jnp.exp(g)[..., None])
    attn = jnp.where(tril, jnp.einsum('bhcid,bhcjd->bhcij', q, k) * decay, 0.0)
    qg = q * jnp.exp(g)[..., None]
    kg = k * jnp.exp(g[..., -1:] - g)[..., None]
    g_last = jnp.exp(g[..., -1])

    def step(state, inp):
        qg_i, kg_i, u_i, w_i, attn_i, gl_i = inp
        v_new = u_i - jnp.einsum('bhtk,bhkv->bhtv', w_i, state)
        o = jnp.einsum('bhtk,bhkv->bhtv', qg_i, state) + jnp.einsum('bhts,bhsv->bhtv', attn_i, v_new)
        state = state * gl_i[..., None, None] + jnp.einsum('bhtk,bhtv->bhkv', kg_i, v_new)
        return state, o

    s0 = jnp.zeros((bsz, nh, dk, dv), jnp.float32)
    mv = lambda a: jnp.moveaxis(a, 2, 0)
    _, o = lax.scan(step, s0, (mv(qg), mv(kg), mv(u), mv(w), mv(attn), mv(g_last)))
    return o.transpose(1, 0, 3, 2, 4).reshape(bsz, seq, nh, dv)

def gdn_mixer(qkv, z, b_raw, a_raw, conv_w, a_log, dt_bias, norm_g):
    bsz, seq, _ = z.shape
    qkv = jax.nn.silu(causal_depthwise_conv(qkv, conv_w))
    q, k, v = jnp.split(qkv, [GDN_QK, 2 * GDN_QK], axis=-1)
    q = l2_norm(q.reshape(bsz, seq, GDN_HEADS, GDN_DK))
    k = l2_norm(k.reshape(bsz, seq, GDN_HEADS, GDN_DK))
    v = v.astype(jnp.float32).reshape(bsz, seq, GDN_HEADS, GDN_DV)
    beta = jax.nn.sigmoid(b_raw.astype(jnp.float32))
    g = -jnp.exp(a_log.astype(jnp.float32)) * jax.nn.softplus(a_raw.astype(jnp.float32) + dt_bias.astype(jnp.float32))
    o = gated_delta_chunked(q, k, v, g, beta)
    o = rms_norm(o, norm_g) * jax.nn.silu(z.astype(jnp.float32).reshape(bsz, seq, GDN_HEADS, GDN_DV))
    return o.reshape(bsz, seq, GDN_V).astype(z.dtype)

def mem_cross_attention(h, mem_n, w_q, w_kv, q_g, k_g, w_o):
    bsz, seq, _ = h.shape
    q = rms_norm((h @ w_q).reshape(bsz, seq, X_HEADS, X_HEAD_DIM), q_g)
    k, v = jnp.split(mem_n @ w_kv, 2, axis=-1)
    k = rms_norm(k.reshape(bsz, -1, X_HEADS, X_HEAD_DIM), k_g)
    v = v.reshape(bsz, -1, X_HEADS, X_HEAD_DIM)
    s = jnp.einsum('bshd,bmhd->bhsm', q, k).astype(jnp.float32) * X_HEAD_DIM ** -0.5
    p = jax.nn.softmax(s, axis=-1)
    o = jnp.einsum('bhsm,bmhd->bshd', p.astype(v.dtype), v).reshape(bsz, seq, D_MODEL)
    return o @ w_o

def swiglu(h, w_gate_up, w_down):
    gate, up = jnp.split(h @ w_gate_up, 2, axis=-1)
    return (jax.nn.silu(gate) * up) @ w_down

def setup_inputs(seed: int = 0) -> dict:
    key = jax.random.key(seed)
    ks = jax.random.split(key, 40)
    L = DEPTH
    f32 = jnp.float32
    nrm = lambda k, shape, s: jax.random.normal(k, shape, f32) * s
    gain = lambda k, shape: 1.0 + 0.02 * jax.random.normal(k, shape, f32)

    def dt_bias_init(k, shape):
        dt = jnp.exp(jax.random.uniform(k, shape, f32) * (math.log(0.1) - math.log(1e-3)) + math.log(1e-3))
        return dt + jnp.log(-jnp.expm1(-dt))

    return {
        'x': jax.random.normal(ks[0], (BATCH, SEQ, D_MODEL), f32),
        'mem': jax.random.normal(ks[1], (BATCH, MEM_LEN, D_MODEL), f32),
        'norm_mix_g': gain(ks[2], (L, D_MODEL)),
        'w_in': nrm(ks[3], (L, D_MODEL, P_IN), D_MODEL ** -0.5),
        'w_out': nrm(ks[4], (L, D_MIX, D_MODEL), D_MIX ** -0.5),
        'da_q_norm_g': gain(ks[5], (L, DA_HALF)),
        'da_k_norm_g': gain(ks[6], (L, DA_HALF)),
        'da_lambda_q1': nrm(ks[7], (L, DA_HALF), 0.1),
        'da_lambda_k1': nrm(ks[8], (L, DA_HALF), 0.1),
        'da_lambda_q2': nrm(ks[9], (L, DA_HALF), 0.1),
        'da_lambda_k2': nrm(ks[10], (L, DA_HALF), 0.1),
        'da_sub_norm_g': gain(ks[11], (L, DA_VDIM)),
        'ssd_conv_w': nrm(ks[12], (L, SSD_CONV, SSD_CONV_DIM), SSD_CONV ** -0.5),
        'ssd_conv_b': nrm(ks[13], (L, SSD_CONV_DIM), 0.1),
        'ssd_dt_bias': dt_bias_init(ks[14], (L, SSD_HEADS)),
        'ssd_A_log': jnp.log(jax.random.uniform(ks[15], (L, SSD_HEADS), f32, 1.0, 16.0)),
        'ssd_D': 1.0 + 0.1 * jax.random.normal(ks[16], (L, SSD_HEADS), f32),
        'ssd_norm_g': gain(ks[17], (L, SSD_INNER)),
        'gdn_conv_w': nrm(ks[18], (L, GDN_CONV, GDN_CONV_DIM), GDN_CONV ** -0.5),
        'gdn_A_log': jnp.log(jax.random.uniform(ks[19], (L, GDN_HEADS), f32, 1.0, 16.0)),
        'gdn_dt_bias': dt_bias_init(ks[20], (L, GDN_HEADS)),
        'gdn_norm_g': gain(ks[21], (L, GDN_DV)),
        'norm_x_g': gain(ks[22], (L, D_MODEL)),
        'norm_mem_g': gain(ks[23], (L, D_MODEL)),
        'w_cq': nrm(ks[24], (L, D_MODEL, D_MODEL), D_MODEL ** -0.5),
        'w_ckv': nrm(ks[25], (L, D_MODEL, 2 * D_MODEL), D_MODEL ** -0.5),
        'xq_norm_g': gain(ks[26], (L, X_HEAD_DIM)),
        'xk_norm_g': gain(ks[27], (L, X_HEAD_DIM)),
        'w_co': nrm(ks[28], (L, D_MODEL, D_MODEL), D_MODEL ** -0.5),
        'norm_ffn_g': gain(ks[29], (L, D_MODEL)),
        'w_gate_up': nrm(ks[30], (L, D_MODEL, 2 * D_FF), D_MODEL ** -0.5),
        'w_down': nrm(ks[31], (L, D_FF, D_MODEL), D_FF ** -0.5),
    }

def reference(x, mem, norm_mix_g, w_in, w_out, da_q_norm_g, da_k_norm_g, da_lambda_q1, da_lambda_k1,
              da_lambda_q2, da_lambda_k2, da_sub_norm_g, ssd_conv_w, ssd_conv_b, ssd_dt_bias, ssd_A_log,
              ssd_D, ssd_norm_g, gdn_conv_w, gdn_A_log, gdn_dt_bias, gdn_norm_g, norm_x_g, norm_mem_g,
              w_cq, w_ckv, xq_norm_g, xk_norm_g, w_co, norm_ffn_g, w_gate_up, w_down):
    bsz, seq, _ = x.shape
    offsets = np.cumsum(IN_SIZES)[:-1].tolist()
    f32 = jnp.float32
    for l in range(DEPTH):
        lambda_init = 0.8 - 0.6 * math.exp(-0.3 * l)
        h = rms_norm(x, norm_mix_g[l])
        proj = h @ w_in[l]
        qa, ka, va, z_s, xbc_s, dt_s, qkv_g, z_g, b_g, a_g = jnp.split(proj, offsets, axis=-1)
        lam = (jnp.exp(jnp.sum(da_lambda_q1[l].astype(f32) * da_lambda_k1[l].astype(f32)))
               - jnp.exp(jnp.sum(da_lambda_q2[l].astype(f32) * da_lambda_k2[l].astype(f32))) + lambda_init)
        o_a = diff_attention(qa.reshape(bsz, seq, DA_HEADS, 2, DA_HALF),
                             ka.reshape(bsz, seq, DA_HEADS, 2, DA_HALF),
                             va.reshape(bsz, seq, DA_HEADS, DA_VDIM),
                             lam, da_q_norm_g[l], da_k_norm_g[l], da_sub_norm_g[l], lambda_init).astype(x.dtype)
        o_b = ssd_mixer(z_s, xbc_s, dt_s, ssd_conv_w[l], ssd_conv_b[l], ssd_dt_bias[l], ssd_A_log[l],
                        ssd_D[l], ssd_norm_g[l])
        o_c = gdn_mixer(qkv_g, z_g, b_g, a_g, gdn_conv_w[l], gdn_A_log[l], gdn_dt_bias[l], gdn_norm_g[l])
        x = x + jnp.concatenate([o_a, o_b, o_c], axis=-1) @ w_out[l]
        x = x + mem_cross_attention(rms_norm(x, norm_x_g[l]), rms_norm(mem, norm_mem_g[l]),
                                    w_cq[l], w_ckv[l], xq_norm_g[l], xk_norm_g[l], w_co[l])
        x = x + swiglu(rms_norm(x, norm_ffn_g[l]), w_gate_up[l], w_down[l])
    return x


_drawn_inputs = setup_inputs


def setup_inputs(seed=0):
    import zlib

    import numpy as np

    out = dict(_drawn_inputs(seed))
    spreads = {}
    factors = {'da_q_norm_g': 4.247,
     'da_k_norm_g': 4.639,
     'da_lambda_q2': 4.35,
     'da_sub_norm_g': 4.035,
     'ssd_norm_g': 4.733,
     'gdn_norm_g': 7.463,
     'norm_x_g': 8.0,
     'norm_mem_g': 8.0,
     'xq_norm_g': 8.0,
     'xk_norm_g': 8.0,
     'norm_ffn_g': 3.267}
    for name, (base, spread) in spreads.items():
        noise = np.random.default_rng([zlib.crc32(name.encode()), seed]).standard_normal(out[name].shape)
        drawn = base * np.exp(spread * noise) if base else spread * noise
        out[name] = __import__('jax').numpy.asarray(drawn.astype(out[name].dtype))
    for name, factor in factors.items():
        out[name] = (out[name] * factor).astype(out[name].dtype)
    return out
```

```python
import math
from contextlib import ExitStack

import numpy as np
import concourse.bass as bass
from concourse import mybir

P = 128
D_MODEL, SEQ, DEPTH, MEM = 1024, 512, 2, 256
EPS = 1e-6
KT = D_MODEL // P
CH = 128
NC = SEQ // CH
DA_H, DA_D, DA_V = 4, 64, 128
S_H, S_D = 4, 64
G_H, G_D = 4, 64
X_H, X_D = 4, 256
D_FF = 2816
FT = D_FF // P
FH = FT // 2
NLEV = 7

F32, F32R, BF16 = mybir.dt.float32, mybir.dt.float32r, mybir.dt.bfloat16
ACT = mybir.ActivationFunctionType
ALU = mybir.AluOpType
AX = mybir.AxisListType

LN_EXP = "natural_log_exp_and_others"

B_IN, N_IN = 0, 28
B_OUT, N_OUT = 28, 8
B_KV, N_KV = 36, 16
B_CQ, N_CQ = 52, 8
B_CO, N_CO = 60, 8
B_FF = 68
N_GU, N_DN = 2 * FH, 8
NB = B_FF + 2 * (N_GU + N_DN)
PAIRS_A = (B_FF + 2 * N_GU) // 2
PAIRS_D = N_DN
WA, WD = KT * P, FH * P

H_MIX, H_IN, H_MEM, H_X, H_CA, H_FF = 8, 0, 16, 24, 32, 40

EA_IN, EA_KV, EA_CQ = 0, 28, 44
ED_OUT, ED_CO, ED_DN = 0, 8, 16

PC = {}
_at = 0
for _n, _w in (("g_mix", 8), ("g_x", 8), ("g_mem", 8), ("g_ffn", 8), ("qg", 1), ("kg", 1), ("subg", 1),
               ("cw", 48), ("cb", 12), ("dtb", 8), ("alog", 8), ("dsk", 4), ("sng", 2), ("gng", 2),
               ("xqg", 2), ("xkg", 2), ("laminit", 1), ("onemin", 1), ("lamv", 256)):
    PC[_n] = (_at, _at + _w)
    _at += _w
NPRM = _at
CC = {n: (i * P, (i + 1) * P) for i, n in enumerate(("idn", "ones", "blk", "tri", "negq", "negd"))}
CC["lev"] = (6 * P, (6 + NLEV) * P)
NCON = (6 + NLEV) * P

PER_LAYER = {
    "act_step": 28, "blk_done": 128, "c_n": 16, "c_nm": 8, "c_p": 16, "c_pt": 8, "c_pv": 8, "c_rs": 8, "c_s": 8,
    "c_sq": 16, "c_ssm": 16, "c_t": 8, "c_w": 8, "conv": 12, "convs": 12, "cv_ev": 4, "cv_tr": 4, "da_nm": 16,
    "da_o": 4, "da_p": 32, "da_pv": 16, "da_s": 16, "da_t": 16, "da_w": 16, "da_wt": 16, "dve_step": 157,
    "evac_a": 52, "evac_d": 32, "f_h2": 22, "f_hi": 22, "f_lo": 22, "f_sg": 22, "g3_ev": 6, "g3_tr": 6, "g_a":
    1, "g_cum": 1, "g_dk": 1, "g_edk": 1, "g_ex": 1, "g_ln": 2, "g_ps": 1, "g_v": 2, "gd_at": 4, "gd_att": 4,
    "gd_d": 4, "gd_dec": 16, "gd_kq": 4, "gn_n": 4, "gn_rs": 1, "gn_ss": 1, "go_n": 1, "go_rs": 1, "go_ss": 1,
    "go_tr": 2, "gt_ev": 8, "gt_tr": 4, "h_f32": 40, "h_hi": 48, "h_lo": 48, "lam_exp": 2, "lam_sum": 1, "lvl":
    24, "m1_ev": 24, "m1_mm": 24, "nrm_mm": 24, "nrm_rs": 3, "nrm_sq": 24, "o_ev": 4, "o_mm": 4, "on_rs": 4,
    "on_sq": 4, "on_ss": 4, "prm_in": 32, "qk_n": 8, "qk_rs": 8, "qk_sq": 8, "qk_ss": 8, "raw_in0": 512,
    "raw_in1": 512, "s_cb": 4, "s_d": 4, "s_dec": 16, "s_ev": 4, "s_h": 3, "s_hst": 3, "s_rs": 1, "s_ss": 1,
    "s_st": 4, "s_tr": 4, "s_x": 8, "s_y": 4, "s_ya": 4, "s_yn": 1, "so_tr": 2, "st": 3, "st_mm": 3, "t_upd":
    20, "ti_0": 4, "ti_ev": 4, "ti_tr": 4, "tt_upd": 24, "tx_mm": 24, "v_ev": 4, "v_tr": 4, "vn": 4, "vn_mm": 4,
    "w_ev": 2, "w_hi": 128, "w_lo": 128, "w_mm": 2, "wsm_hi": 1, "wsm_lo": 1, "z_ev": 2, "z_tr": 2, "zg_ev": 2,
    "zg_tr": 2
}


START = {"w_lo": 3, "blk_done": 2, "evac_a": 2, "evac_d": 2, "f_sg": 1, "f_h2": 1, "f_hi": 1, "f_lo": 1, "h_lo": 1}


class Signal:

    def __init__(self, nc, ctx, name, trips):
        self.sem = ctx.enter_context(nc.semaphore(name))
        self.name, self.n, self.trips = name, 0, trips
        self.per_layer, self.start = PER_LAYER.get(name, 0), START.get(name, 0)

    def up(self, by=1):
        self.n += by * self.trips[0]
        return self.sem

    def at(self, l, v):
        return l * self.per_layer + (v + self.start)


def trunk(nc, x_d, mem_d, wa_d, wd_d, wsm_d, prm_d, con_d, out_d, strict=True):
    ctx = ExitStack()
    nc.disable_value_cache = True
    with ctx:
        trips = [1]
        signals = {}

        def signal(name):
            signals[name] = Signal(nc, ctx, name, trips)
            return signals[name]

        s_act_step = signal("act_step")
        s_blk_done = signal("blk_done")
        s_c_bf = signal("c_bf")
        s_c_n = signal("c_n")
        s_c_nm = signal("c_nm")
        s_c_p = signal("c_p")
        s_c_pt = signal("c_pt")
        s_c_pv = signal("c_pv")
        s_c_rs = signal("c_rs")
        s_c_s = signal("c_s")
        s_c_sq = signal("c_sq")
        s_c_ssm = signal("c_ssm")
        s_c_t = signal("c_t")
        s_c_w = signal("c_w")
        s_const_in = signal("const_in")
        s_conv = signal("conv")
        s_convs = signal("convs")
        s_cv_ev = signal("cv_ev")
        s_cv_tr = signal("cv_tr")
        s_da_nm = signal("da_nm")
        s_da_o = signal("da_o")
        s_da_p = signal("da_p")
        s_da_pv = signal("da_pv")
        s_da_s = signal("da_s")
        s_da_t = signal("da_t")
        s_da_w = signal("da_w")
        s_da_wt = signal("da_wt")
        s_dve_step = signal("dve_step")
        s_evac_a = signal("evac_a")
        s_evac_d = signal("evac_d")
        s_f_h2 = signal("f_h2")
        s_f_hi = signal("f_hi")
        s_f_lo = signal("f_lo")
        s_f_sg = signal("f_sg")
        s_g3_ev = signal("g3_ev")
        s_g3_tr = signal("g3_tr")
        s_g_a = signal("g_a")
        s_g_cum = signal("g_cum")
        s_g_dk = signal("g_dk")
        s_g_edk = signal("g_edk")
        s_g_ex = signal("g_ex")
        s_g_ln = signal("g_ln")
        s_g_ps = signal("g_ps")
        s_g_v = signal("g_v")
        s_gd_at = signal("gd_at")
        s_gd_att = signal("gd_att")
        s_gd_d = signal("gd_d")
        s_gd_dec = signal("gd_dec")
        s_gd_kq = signal("gd_kq")
        s_gn_n = signal("gn_n")
        s_gn_rs = signal("gn_rs")
        s_gn_ss = signal("gn_ss")
        s_go_n = signal("go_n")
        s_go_rs = signal("go_rs")
        s_go_ss = signal("go_ss")
        s_go_tr = signal("go_tr")
        s_gt_ev = signal("gt_ev")
        s_gt_tr = signal("gt_tr")
        s_h_f32 = signal("h_f32")
        s_h_hi = signal("h_hi")
        s_h_lo = signal("h_lo")
        s_lam_exp = signal("lam_exp")
        s_lam_sum = signal("lam_sum")
        s_lvl = signal("lvl")
        s_m1_ev = signal("m1_ev")
        s_m1_mm = signal("m1_mm")
        s_m_ev = signal("m_ev")
        s_m_tr = signal("m_tr")
        s_mem_in = signal("mem_in")
        s_mem_n = signal("mem_n")
        s_mem_rs = signal("mem_rs")
        s_mem_sq = signal("mem_sq")
        s_nrm_mm = signal("nrm_mm")
        s_nrm_rs = signal("nrm_rs")
        s_nrm_sq = signal("nrm_sq")
        s_o_ev = signal("o_ev")
        s_o_mm = signal("o_mm")
        s_on_rs = signal("on_rs")
        s_on_sq = signal("on_sq")
        s_on_ss = signal("on_ss")
        s_prm_in = signal("prm_in")
        s_qk_n = signal("qk_n")
        s_qk_rs = signal("qk_rs")
        s_qk_sq = signal("qk_sq")
        s_qk_ss = signal("qk_ss")
        s_s_cb = signal("s_cb")
        s_s_d = signal("s_d")
        s_s_dec = signal("s_dec")
        s_s_ev = signal("s_ev")
        s_s_h = signal("s_h")
        s_s_hst = signal("s_hst")
        s_s_rs = signal("s_rs")
        s_s_ss = signal("s_ss")
        s_s_st = signal("s_st")
        s_s_tr = signal("s_tr")
        s_s_x = signal("s_x")
        s_s_y = signal("s_y")
        s_s_ya = signal("s_ya")
        s_s_yn = signal("s_yn")
        s_setup = signal("setup")
        s_so_tr = signal("so_tr")
        s_st = signal("st")
        s_st_mm = signal("st_mm")
        s_t_upd = signal("t_upd")
        s_ti_0 = signal("ti_0")
        s_ti_ev = signal("ti_ev")
        s_ti_tr = signal("ti_tr")
        s_tt_upd = signal("tt_upd")
        s_tx_mm = signal("tx_mm")
        s_v_ev = signal("v_ev")
        s_v_setup = signal("v_setup")
        s_v_tr = signal("v_tr")
        s_vn = signal("vn")
        s_vn_mm = signal("vn_mm")
        s_w_ev = signal("w_ev")
        s_w_hi = signal("w_hi")
        s_w_lo = signal("w_lo")
        s_w_mm = signal("w_mm")
        s_wsm_hi = signal("wsm_hi")
        s_wsm_lo = signal("wsm_lo")
        s_x_in = signal("x_in")
        s_x_tr = signal("x_tr")
        s_x_turned = signal("x_turned")
        s_y_out = signal("y_out")
        s_y_ready = signal("y_ready")
        s_y_tr = signal("y_tr")
        s_z_ev = signal("z_ev")
        s_z_tr = signal("z_tr")
        s_zg_ev = signal("zg_ev")
        s_zg_tr = signal("zg_tr")
        s_raw_in = [signal("raw_in0"), signal("raw_in1")]
        base = (nc.sbuf_base + 31) // 32 * 32
        total = (nc.sbuf_usable_end - base) // 4
        cur = [0]

        def at(name, off, shape, dt=F32):
            return nc.alloc_sbuf_tensor_at(name, [P] + list(shape), dt, offset=base + 4 * off)

        def new(name, shape, dt=F32):
            n = int(np.prod(shape))
            words = n if dt != BF16 else (n + 1) // 2
            words = (words + 7) // 8 * 8
            t = at(name, cur[0], shape, dt)
            cur[0] += words
            return t

        xT = new("xT", [KT, SEQ])
        h_hi = new("h_hi", [KT, SEQ], F32R)
        h_lo = new("h_lo", [KT, SEQ], F32R)
        memn = new("memn", [KT, MEM])
        raw = new("raw", [2, 2 * WD])
        w_hi = [new(f"w_hi{i}", [FH, P], F32R) for i in range(2)]
        w_lo = [new(f"w_lo{i}", [FH, P], F32R) for i in range(2)]
        con = new("con", [NCON])
        idb, negq, negd = (new(n, [P], BF16) for n in ("idb", "negq", "negd"))
        prm = new("prm", [NPRM])
        wsm = new("wsm", [KT, 12])
        wsm_hi = new("wsm_hi", [KT, 12], F32R)
        wsm_lo = new("wsm_lo", [KT, 12], F32R)
        eps, seed = new("eps", [2]), new("seed", [sum(START.values())])
        htmp = new("htmp", [2, SEQ])
        sq = new("sq", [2, SEQ])
        rs = new("rs", [2, SEQ])
        lp, lsum, lexp, nlam = new("lp", [2, 64]), new("lsum", [2]), new("lexp", [2]), new("nlam", [2])
        ag, sg1 = new("ag", [8]), new("sg1", [1])
        mx, sm, rr = new("mx", [16, 2]), new("sm", [16, 2]), new("rr", [16, 2])
        gv, gb, g1, sp, ga = (new(n, [NC, w]) for n, w in (("gv", 8), ("gb", 4), ("g1", 8), ("sp", 8), ("ga", 8)))
        beta = new("beta", [NC, 4])
        cums, ex = new("cums", [2, NC, 8]), new("ex", [2, NC, 8])
        ncum, edk = new("ncum", [NC, 8]), new("edk", [NC, 8])
        ss8, ss16, ss32 = new("ss8", [8]), new("ss16", [16]), new("ss32", [NC, 8])
        A0 = cur[0]
        assert A0 + 14336 + 6912 <= total, (A0, total)
        FR = A0 + 14336
        projT = at("projT", A0, [28, SEQ])
        vtok = at("vtok", FR, [NC, DA_H, DA_V])
        prob = at("prob", FR + 2048, [2, 2, SEQ])
        wgt = at("wgt", FR + 4096, [2, SEQ])
        wgtT = at("wgtT", FR + 5120, [2, SEQ])
        convT = at("convT", A0, [6, SEQ])
        xd = at("xd", A0 + 5120, [NC, S_H, S_D])
        btok = at("btok", A0 + 4096, [NC, 2, P])
        ysq = at("ysq", A0 + 3072, [NC, 256])
        xdd = at("xdd", FR, [NC, S_H, S_D])
        xskip = at("xskip", FR + 1024, [NC, S_H, S_D])
        dec = at("dec", FR + 2048, [2, 4, P])
        scoT = at("scoT", FR + 3072, [2, 4, P])
        hst = at("hst", FR + 4096, [2, S_H, S_D])
        ysd = at("ysd", FR + 4608, [NC, S_H, S_D])
        ytmp = at("ytmp", FR + 5632, [S_H, S_D])
        zst = at("zst", FR + 5888, [NC, 256])
        convG = at("convG", A0, [6, SEQ])
        qktok = at("qktok", A0 + 3072, [NC, 2, G_H, G_D])
        gvtok = at("gvtok", A0 + 5120, [NC, G_H, G_D])
        kE = at("kE", A0 + 11264, [NC, G_H, G_D])
        kgt = at("kgt", A0 + 12288, [NC, G_H, G_D])
        qE = at("qE", A0 + 13312, [NC, G_H, G_D])
        gsq = at("gsq", FR, [NC, 2, G_H, G_D])
        tr3 = at("tr3", A0 + 8192, [3, 2, SEQ])
        aT = at("aT", FR, [NC, G_H, P])
        attT = at("attT", FR + 2048, [NC, G_H, P])
        tri_i = at("tri_i", FR + 4096, [NC, G_H, P])
        tri_t = at("tri_t", A0, [NC, G_H, P])
        decG = at("decG", A0 + 2048, [2, 4, P])
        lvlA = at("lvlA", A0 + 2048, [2, 4, P])
        m1 = at("m1", A0 + 8192, [NC, G_H, P])
        wTn = at("wTn", A0 + 3072, [2, SEQ])
        otok = at("otok", A0 + 6144, [NC, G_H, G_D])
        stS = at("stS", FR + 6144, [2, 2, G_D])
        vnew = at("vnew", FR + 6400, [2, G_H, G_D])
        zgt = at("zgt", A0 + 11264, [NC, 256])
        osq = at("osq", A0 + 12288, [NC, 256])
        qcT = at("qcT", A0, [KT, SEQ])
        kvT = at("kvT", A0 + 4096, [16, MEM])
        vmt = at("vmt", A0 + 8192, [2, D_MODEL])
        pT = at("pT", A0 + 10240, [2, 2, SEQ])
        pc = at("pc", A0 + 12288, [2, 2, MEM])
        f_hi = at("f_hi", A0, [FH, SEQ], F32R)
        f_lo = at("f_lo", A0 + 5632, [FH, SEQ], F32R)
        sgate = at("sgate", A0 + 11264, [SEQ])
        h2 = at("h2", A0 + 11776, [SEQ])
        xtok = at("xtok", A0, [NC, D_MODEL])
        mtok = at("mtok", A0 + 4096, [2, D_MODEL])
        mjunk = at("mjunk", A0 + 6144, [2, D_MODEL])

        bank = [ctx.enter_context(nc.psum_tensor(f"bank{i}", [P, 512], F32)) for i in range(4)]
        hi_banks = ctx.enter_context(nc.psum_tensor("hi_banks", [P, 4, 512], F32))
        bk = [b[:] for b in bank] + [hi_banks[:, i, :] for i in range(4)]

        def col(name, i=0, n=1):
            a = PC[name][0] + i
            return prm[:, a:a + n]

        def cst(name):
            return con[:, CC[name][0]:CC[name][1]]

        def lev(i):
            a = CC["lev"][0] + i * P
            return con[:, a:a + P]

        def bcl(ap, n):
            return ap.unsqueeze(len(ap.shape)).to_broadcast(list(ap.shape) + [n])

        def bcm(ap, n):
            return ap.unsqueeze(1).to_broadcast([ap.shape[0], n] + list(ap.shape[1:]))

        block = ctx.enter_context(nc.Block())

        @block.sync
        def _(sp_):
            sp_.dma_start(con[:], con_d).then_inc(s_const_in.sem, 16)
            sp_.dma_start(xtok[:], x_d.rearrange("(c p) d -> p c d", p=P)).then_inc(s_x_in.sem, 16)
            sp_.dma_start(mtok[:], mem_d.rearrange("(c p) d -> p c d", p=P)).then_inc(s_mem_in.sem, 16)

            with sp_.Fori(0, DEPTH) as l:

                def load(p, slot, src, width):
                    sp_.wait_ge(s_w_lo.sem, s_w_lo.at(l, 2 * p - 2))
                    sp_.dma_start(raw[:, slot, 0:2 * width], src.rearrange("a p n -> p (a n)")).then_inc(s_raw_in[slot].up(16), 16)

                def run(p0, n, src_d, per, q0, width):
                    trips[0] = n // 2
                    with sp_.Fori(0, n // 2) as i:
                        for j in range(2):
                            load(p0 + 2 * i + j, (p0 + j) % 2,
                                 src_d[bass.ds(l * per + 2 * i + (q0 + j), 1), :, :], width)
                    trips[0] = 1
                    if n % 2:
                        load(p0 + n - 1, (p0 + n - 1) % 2, src_d[bass.ds(l * per + (q0 + n - 1), 1), :, :], width)

                p = qa = B_FF // 2
                run(0, p, wa_d, PAIRS_A, 0, WA)
                for half in range(2):
                    run(p, N_GU // 2, wa_d, PAIRS_A, qa, WA)
                    p, qa = p + N_GU // 2, qa + N_GU // 2
                    run(p, N_DN // 2, wd_d, PAIRS_D, half * N_DN // 2, WD)
                    p += N_DN // 2
            for c in range(NC):
                sp_.wait_ge(s_y_ready.sem, 2 * c + 2)
                sp_.dma_start(out_d.rearrange("(c p) d -> c p d", p=P)[c], xtok[:, c, :]).then_inc(s_y_out.sem, 16)
            sp_.wait_ge(s_y_out.sem, 16 * NC)

        @block.gpsimd
        def _(pool):
            with pool.Fori(0, DEPTH) as l:
                pool.wait_ge(s_evac_d.sem, s_evac_d.at(l, 0))
                pool.dma_start(prm[:], prm_d[bass.ds(l, 1), :, :].rearrange("a p n -> p (a n)")).then_inc(s_prm_in.up(16), 16)
                pool.dma_start(wsm[:].rearrange("p k n -> p (k n)"),
                                     wsm_d[bass.ds(l, 1), :, :].rearrange("a p n -> p (a n)")).then_inc(s_prm_in.up(16), 16)

        def pair_loop(eng, p0, n, body):
            body(0, p0 % 2, p0 // 2 + 1, True)
            rounds = (n - 1) // 2
            if rounds:
                trips[0] = rounds
                with eng.Fori(0, rounds) as i:
                    for j in (1, 2):
                        body(2 * i + j, (p0 + j) % 2, (p0 + j) // 2 + 1 + i, False)
                trips[0] = 1
            if (n - 1) % 2:
                body(n - 1, (p0 + n - 1) % 2, (p0 + n - 1) // 2 + 1, False)

        @block.scalar
        def _(act):
            def link(l, ins):
                ins.then_inc(s_act_step.up(), 1)
                act.wait_ge(s_act_step.sem, s_act_step.at(l, s_act_step.n))

            act.preload_act_table_set(LN_EXP)
            act.wait_ge(s_mem_in.sem, 16)
            act.wait_ge(s_setup.sem, 1)
            for c in range(2):
                act.activation(mjunk[:, c, :], mtok[:, c, :], ACT.Square,
                               accum_out=ss8[:, c:c + 1]).then_inc(s_mem_sq.sem, 1)
            act.wait_ge(s_mem_sq.sem, 2)
            act.activation(ss8[:, 2:4], ss8[:, 0:2], ACT.Ln, bias=eps[:, 0:1], scale=1.0 / D_MODEL
                           ).then_inc(s_mem_sq.sem, 1)
            act.wait_ge(s_mem_sq.sem, 3)
            act.activation(ss8[:, 4:6], ss8[:, 2:4], ACT.Exp, scale=-0.5).then_inc(s_mem_rs.sem, 1)

            act.wait_ge(s_x_turned.sem, 8)

            with act.Fori(0, DEPTH) as l:

                def rsqrt(out, in_, scale, e, done):
                    link(l, act.activation(out, in_, ACT.Ln, bias=eps[0:in_.shape[0], e:e + 1], scale=scale))
                    act.activation(out, out, ACT.Exp, scale=-0.5).then_inc(done.up(), 1)

                def split_hi(n, w=SEQ, src=None, free=None):
                    if free is not None:
                        act.wait_ge(s_blk_done.sem, s_blk_done.at(l, free))
                    if src is None:
                        act.wait_ge(s_h_f32.sem, s_h_f32.at(l, n + 1 - (KT if n >= H_FF else 0)))
                        src = htmp[:, n % 2, 0:w]
                    act.activation(h_hi[:, n % KT, 0:w], src, ACT.Copy).then_inc(s_h_hi.up(), 1)

                def dense(b0, n, K, evac):
                    width = K * P

                    def body(q, slot, loads, first):
                        for j in range(2):
                            act.wait_ge(s_blk_done.sem, s_blk_done.at(l, 2 * q + (b0 + j - 1)))
                            if j == 0:
                                act.wait_ge(s_raw_in[slot].sem, s_raw_in[slot].at(l, 16 * loads))
                            act.activation(w_hi[j][:, 0:K, :].rearrange("p k n -> p (k n)"), raw[:, slot, j * width:(j + 1) * width], ACT.Copy).then_inc(s_w_hi.up(), 1)
                            if not first and evac is not None:
                                evac(2 * q + (j - 2))
                    pair_loop(act, b0 // 2, n // 2, body)
                    if evac is not None:
                        for o in (n - 2, n - 1):
                            evac(o)

                def copy_out(b0, dst, w):
                    def evac(o):
                        act.wait_ge(s_blk_done.sem, s_blk_done.at(l, o + (b0 + 1)))
                        act.activation(dst[:, bass.ds(o, 1), 0:w].rearrange("p a n -> p (a n)"), bk[o_parity(o)][:, 0:w], ACT.Copy).then_inc(s_evac_a.up(), 1)
                    return evac

                par = [0]

                def o_parity(o):
                    par[0] ^= 1
                    return par[0] ^ 1

                def norm(idx, ready):
                    for k in range(KT):
                        n = idx * KT + k
                        ready(k)
                        if n >= 2:
                            act.wait_ge(s_nrm_mm.sem, s_nrm_mm.at(l, n - 1))
                        act.activation(sq[:, k % 2, :], xT[:, k, :], ACT.Square).then_inc(s_nrm_sq.up(), 1)
                    act.wait_ge(s_nrm_mm.sem, s_nrm_mm.at(l, (idx + 1) * KT))
                    rsqrt(rs[:, 0, :], bk[2], 1.0 / D_MODEL, 0, s_nrm_rs)

                act.preload_act_table_set(LN_EXP)
                act.wait_ge(s_prm_in.sem, s_prm_in.at(l, 32))
                act.wait_ge(s_lam_sum.sem, s_lam_sum.at(l, 1))
                act.activation(lexp[:], lsum[:], ACT.Exp).then_inc(s_lam_exp.up(), 1)
                act.activation(ag[:], col("alog", 0, 8), ACT.Exp).then_inc(s_lam_exp.up(), 1)
                act.activation(wsm_hi[:].rearrange("p k n -> p (k n)"), wsm[:].rearrange("p k n -> p (k n)"), ACT.Copy).then_inc(s_wsm_hi.up(), 1)

                norm(0, lambda k: None if k else act.wait_ge(s_evac_d.sem, s_evac_d.at(l, 0)))
                for k in range(KT):
                    split_hi(H_IN + k, free=None if k else 0)
                dense(B_IN, N_IN, KT, copy_out(B_IN, projT, SEQ))

                for t in range(8):
                    if t == 0:
                        act.wait_ge(s_evac_a.sem, s_evac_a.at(l, N_IN))
                    if t >= 2:
                        act.wait_ge(s_qk_ss.sem, s_qk_ss.at(l, t - 1))
                    act.activation(sq[:, t % 2, :], projT[:, t, :], ACT.Square).then_inc(s_qk_sq.up(), 1)
                    if t >= 1:
                        act.wait_ge(s_qk_ss.sem, s_qk_ss.at(l, t))
                        if t >= 3:
                            act.wait_ge(s_qk_n.sem, s_qk_n.at(l, t - 2))
                        rsqrt(rs[:, (t - 1) % 2, :], bk[2 + (t - 1) % 2], 1.0 / DA_D, 0, s_qk_rs)
                act.wait_ge(s_qk_ss.sem, s_qk_ss.at(l, 8))
                act.wait_ge(s_qk_n.sem, s_qk_n.at(l, 6))
                rsqrt(rs[:, 1, :], bk[3], 1.0 / DA_D, 0, s_qk_rs)
                for c in range(NC):
                    act.wait_ge(s_v_tr.sem, s_v_tr.at(l, c + 1))
                    act.activation(vtok[:, c].rearrange("p h e -> p (h e)"), bk[4 + c % 2], ACT.Copy).then_inc(s_v_ev.up(), 1)

                def da_exp(n):
                    nk = (n % NC + 1) * P
                    act.wait_ge(s_da_nm.sem, s_da_nm.at(l, n + 1))
                    if n >= 2:
                        act.wait_ge(s_da_w.sem, s_da_w.at(l, n - 1))
                    for c in range(2):
                        act.activation(prob[:, n % 2, c, 0:nk], bk[4 + 2 * (n % 2) + c][:, 0:nk], ACT.Exp, bias=mx[:, n, c:c + 1], scale=DA_D ** -0.5, accum_out=sm[:, n, c:c + 1]).then_inc(s_da_p.up(), 1)

                def da_turned(n):
                    nk = (n % NC + 1) * P
                    act.wait_ge(s_da_t.sem, s_da_t.at(l, n + 1))
                    if n >= 2:
                        act.wait_ge(s_da_pv.sem, s_da_pv.at(l, n - 1))
                    act.activation(wgtT[:, n % 2, 0:nk], bk[2 + n % 2][:, 0:nk], ACT.Copy).then_inc(s_da_wt.up(), 1)
                    if n % NC == 0 and n > 0:
                        da_out(n // NC - 1)

                def da_out(h):
                    act.wait_ge(s_da_pv.sem, s_da_pv.at(l, NC * (h + 1)))
                    act.activation(projT[:, h, :], bk[h % 2], ACT.Copy).then_inc(s_da_o.up(), 1)

                ND = DA_H * NC
                for n in range(ND):
                    da_exp(n)
                    if n >= 1:
                        da_turned(n - 1)
                da_turned(ND - 1)
                da_out(DA_H - 1)
                act.wait_ge(s_da_o.sem, s_da_o.at(l, DA_H))
                for h in range(2):
                    act.activation(sq[:, h % 2, :], projT[:, h, :], ACT.Square).then_inc(s_on_sq.up(), 1)
                for h in range(DA_H):
                    act.wait_ge(s_on_ss.sem, s_on_ss.at(l, h + 1))
                    if h >= 2:
                        act.wait_ge(s_h_f32.sem, s_h_f32.at(l, H_MIX + h - 1))
                    rsqrt(rs[:, h % 2, :], bk[2 + h % 2], 1.0 / DA_V, 0, s_on_rs)
                    if h + 2 < DA_H:
                        act.activation(sq[:, h % 2, :], projT[:, h + 2, :], ACT.Square).then_inc(s_on_sq.up(), 1)
                    split_hi(H_MIX + h)

                act.wait_ge(s_g_v.sem, s_g_v.at(l, 2))
                link(l, act.activation(g1[:], gv[:], ACT.Abs))
                link(l, act.activation(g1[:], g1[:], ACT.Exp, scale=-1.0))
                act.activation(g1[:], g1[:], ACT.Ln, bias=1.0).then_inc(s_g_ln.up(), 1)
                act.activation(gb[:], gb[:], ACT.Exp, scale=-1.0).then_inc(s_g_ln.up(), 1)
                act.wait_ge(s_g_dk.sem, s_g_dk.at(l, 1))
                act.activation(ex[:].rearrange("p a c h -> p (a c h)"), cums[:].rearrange("p a c h -> p (a c h)"), ACT.Exp).then_inc(s_g_ex.up(), 1)
                act.activation(edk[:], edk[:], ACT.Exp).then_inc(s_g_edk.up(), 1)

                for t in range(6):
                    act.wait_ge(s_conv.sem, s_conv.at(l, t + 1))
                    act.activation(convT[:, t, :], convT[:, t, :], ACT.Silu).then_inc(s_convs.up(), 1)
                for c in range(NC):
                    act.wait_ge(s_s_tr.sem, s_s_tr.at(l, c + 1))
                    act.activation(btok[:, c].rearrange("p g n -> p (g n)"), bk[4 + c % 2][:, 0:256], ACT.Copy).then_inc(s_s_ev.up(), 1)
                for i in range(2):
                    act.wait_ge(s_z_tr.sem, s_z_tr.at(l, i + 1))
                    act.activation(zst[:, 2 * i:2 * i + 2].rearrange("p c n -> p (c n)"), bk[2 + i], ACT.Silu).then_inc(s_z_ev.up(), 1)
                act.preload_act_table_set(LN_EXP)
                for c in range(NC):
                    act.wait_ge(s_s_d.sem, s_s_d.at(l, c + 1))
                    if c >= 2:
                        act.wait_ge(s_s_st.sem, s_s_st.at(l, c - 1))
                    for h in range(S_H):
                        act.activation(dec[:, c % 2, h, :], bk[4 + c % 2][:, h * P:(h + 1) * P], ACT.Exp, bias=ncum[:, c, h:h + 1]).then_inc(s_s_dec.up(), 1)
                act.wait_ge(s_s_ss.sem, s_s_ss.at(l, 1))
                rsqrt(ss8[:], ss8[:], 1.0 / P, 0, s_s_rs)
                for f in range(2):
                    split_hi(H_MIX + 4 + f)

                for t in range(6):
                    act.wait_ge(s_conv.sem, s_conv.at(l, 7 + t))
                    act.activation(convG[:, t, :], convG[:, t, :], ACT.Silu).then_inc(s_convs.up(), 1)
                for c in range(NC):
                    act.wait_ge(s_gt_tr.sem, s_gt_tr.at(l, c + 1))
                    act.activation(qktok[:, c].rearrange("p a h d -> p (a h d)"), bk[2 + c % 2], ACT.Copy).then_inc(s_gt_ev.up(), 1)
                    act.activation(gvtok[:, c].rearrange("p h d -> p (h d)"), bk[4 + c % 2][:, 0:256], ACT.Copy).then_inc(s_gt_ev.up(), 1)
                act.preload_act_table_set(LN_EXP)
                act.wait_ge(s_gn_ss.sem, s_gn_ss.at(l, 1))
                rsqrt(ss32[:], ss32[:], 1.0, 0, s_gn_rs)
                for i in range(6):
                    act.wait_ge(s_g3_tr.sem, s_g3_tr.at(l, i + 1))
                    act.activation(tr3[:, i // 2, i % 2, :], bk[2 + i % 2], ACT.Copy).then_inc(s_g3_ev.up(), 1)
                for c in range(NC):
                    act.wait_ge(s_gd_d.sem, s_gd_d.at(l, c + 1))
                    if c >= 2:
                        act.wait_ge(s_gd_at.sem, s_gd_at.at(l, c - 1))
                    for h in range(G_H):
                        act.activation(decG[:, c % 2, h, :], bk[4 + c % 2][:, h * P:(h + 1) * P], ACT.Exp, bias=ncum[:, c, 4 + h:5 + h]).then_inc(s_gd_dec.up(), 1)
                for c in range(NC):
                    act.wait_ge(s_ti_tr.sem, s_ti_tr.at(l, c + 1))
                    act.activation(tri_i[:, c].rearrange("p h n -> p (h n)"), bk[2 + c % 2], ACT.Copy).then_inc(s_ti_ev.up(), 1)
                for v in range(NLEV - 1):
                    for c in range(NC):
                        n = v * NC + c
                        act.wait_ge(s_m1_mm.sem, s_m1_mm.at(l, n + 1))
                        if v:
                            act.wait_ge(s_tx_mm.sem, s_tx_mm.at(l, n - NC + 1))
                        act.activation(m1[:, c].rearrange("p h n -> p (h n)"), bk[2 + c % 2], ACT.Copy).then_inc(s_m1_ev.up(), 1)
                for p_ in range(2):
                    act.wait_ge(s_w_mm.sem, s_w_mm.at(l, p_ + 1))
                    act.activation(wTn[:, p_, :], bk[2 + p_], ACT.Copy, scale=-1.0).then_inc(s_w_ev.up(), 1)
                for c in range(NC):
                    act.wait_ge(s_o_mm.sem, s_o_mm.at(l, c + 1))
                    act.activation(otok[:, c].rearrange("p (a r) d -> p r a d", r=2), hi_banks[:, 2:4, 0:P].rearrange("p r (a d) -> p r a d", a=2), ACT.Copy).then_inc(s_o_ev.up(), 1)
                for i in range(2):
                    act.wait_ge(s_zg_tr.sem, s_zg_tr.at(l, i + 1))
                    act.activation(zgt[:, 2 * i:2 * i + 2].rearrange("p c n -> p (c n)"), bk[2 + i], ACT.Silu).then_inc(s_zg_ev.up(), 1)
                act.preload_act_table_set(LN_EXP)
                act.wait_ge(s_go_ss.sem, s_go_ss.at(l, 1))
                rsqrt(ss16[:], ss16[:], 1.0 / G_D, 0, s_go_rs)
                for f in range(2):
                    split_hi(H_MIX + 6 + f)

                dense(B_OUT, N_OUT, KT, None)
                for k in range(KT):
                    split_hi(H_MEM + k, MEM, free=B_OUT + N_OUT)
                dense(B_KV, N_KV, KT, copy_out(B_KV, kvT, MEM))
                norm(1, lambda k: act.wait_ge(s_evac_d.sem, s_evac_d.at(l, ED_OUT + k + 1)))
                for k in range(KT):
                    split_hi(H_X + k, free=B_KV + N_KV)
                dense(B_CQ, N_CQ, KT, copy_out(B_CQ, qcT, SEQ))
                act.wait_ge(s_evac_a.sem, s_evac_a.at(l, EA_CQ + N_CQ))
                for n in range(16):
                    if n >= 2:
                        act.wait_ge(s_c_ssm.sem, s_c_ssm.at(l, n - 1))
                    w = SEQ if n < 8 else MEM
                    act.activation(sq[:, n % 2, 0:w], qcT[:, n, :] if n < 8 else kvT[:, n - 8, :], ACT.Square).then_inc(s_c_sq.up(), 1)
                    if n % 2 == 1:
                        m = n // 2
                        act.wait_ge(s_c_ssm.sem, s_c_ssm.at(l, n + 1))
                        if m >= 2:
                            act.wait_ge(s_c_n.sem, s_c_n.at(l, 2 * m - 2))
                        rsqrt(rs[:, m % 2, 0:w], bk[2 + m % 2][:, 0:w], 1.0 / X_D, 0, s_c_rs)
                for i in range(4):
                    act.wait_ge(s_cv_tr.sem, s_cv_tr.at(l, i + 1))
                    act.activation(vmt[:, i // 2, (i % 2) * 512:(i % 2 + 1) * 512], bk[2 + i % 2], ACT.Copy).then_inc(s_cv_ev.up(), 1)

                def c_exp(n):
                    act.wait_ge(s_c_nm.sem, s_c_nm.at(l, n + 1))
                    if n >= 2:
                        act.wait_ge(s_c_t.sem, s_c_t.at(l, n - 1))
                    for i in range(2):
                        act.activation(pc[:, n % 2, i, :], bk[4 + n % 2][:, i * MEM:(i + 1) * MEM], ACT.Exp, bias=mx[:, n, i:i + 1], scale=X_D ** -0.5, accum_out=sm[:, n, i:i + 1]).then_inc(s_c_p.up(), 1)

                def c_turned(n):
                    h, qp = n // 2, n % 2
                    act.wait_ge(s_c_t.sem, s_c_t.at(l, n + 1))
                    if h >= 2 and qp == 0:
                        act.wait_ge(s_c_pv.sem, s_c_pv.at(l, 2 * (h - 1)))
                    act.activation(pT[:, h % 2, :, qp * 256:(qp + 1) * 256], bk[6 + n % 2].rearrange("p (m q) -> p m q", m=2), ACT.Copy).then_inc(s_c_pt.up(), 1)
                    if qp == 0 and h > 0:
                        c_out(h - 1)

                def c_out(h):
                    for e in range(2):
                        act.wait_ge(s_c_pv.sem, s_c_pv.at(l, 2 * h + e + 1))
                        split_hi(H_CA + 2 * h + e, src=bk[e], free=B_CQ + N_CQ)

                for n in range(8):
                    c_exp(n)
                    if n >= 1:
                        c_turned(n - 1)
                c_turned(7)
                c_out(3)
                dense(B_CO, N_CO, KT, None)
                norm(2, lambda k: act.wait_ge(s_evac_d.sem, s_evac_d.at(l, ED_CO + k + 1)))
                for k in range(KT):
                    split_hi(H_FF + k, free=B_CO + N_CO)
                act.preload_act_table(ACT.Silu)
                b = B_FF
                for half in range(2):

                    f0 = half * FH

                    def body(q, slot, loads, first, b=b, f0=f0):
                        for j in range(2):
                            act.wait_ge(s_blk_done.sem, s_blk_done.at(l, 2 * q + (b + j - 1)))
                            if j == 0:
                                act.wait_ge(s_raw_in[slot].sem, s_raw_in[slot].at(l, 16 * loads))
                            act.activation(w_hi[j][:, 0:KT, :].rearrange("p k n -> p (k n)"), raw[:, slot, j * WA:(j + 1) * WA], ACT.Copy).then_inc(s_w_hi.up(), 1)
                            if not first:
                                ffn_out(q - 1, j, b, f0)

                    def ffn_out(i, j, b, f0):
                        if j == 0:
                            act.wait_ge(s_blk_done.sem, s_blk_done.at(l, 2 * i + (b + 1)))
                            act.wait_ge(s_f_h2.sem, s_f_h2.at(l, i + f0))
                            act.activation(sgate[:], bk[0], ACT.Silu).then_inc(s_f_sg.up(), 1)
                        else:
                            act.wait_ge(s_f_h2.sem, s_f_h2.at(l, i + (f0 + 1)))
                            act.activation(f_hi[:, bass.ds(i, 1), :].rearrange("p a n -> p (a n)"), h2[:], ACT.Copy).then_inc(s_f_hi.up(), 1)
                    pair_loop(act, b // 2, FH, body)
                    for j in range(2):
                        ffn_out(FH - 1, j, b, f0)
                    b += N_GU
                    dense(b, N_DN, FH, None)
                    b += N_DN

            for c in range(NC):
                for i in range(2):
                    n = 2 * c + i
                    act.wait_ge(s_y_tr.sem, n + 1)
                    act.activation(xtok[:, c, i * 512:(i + 1) * 512], bk[2 + n % 2], ACT.Copy
                                   ).then_inc(s_y_ready.sem, 1)

        @block.vector
        def _(dve):
            def tt(out, a, b, op):
                return dve.tensor_tensor(out, a, b, op)

            def stt(out, a, s, b, op0, op1):
                return dve.scalar_tensor_tensor(out=out, in0=a, scalar=s, in1=b, op0=op0, op1=op1)

            MUL, ADD, SUB = ALU.mult, ALU.add, ALU.subtract

            def first(ins):
                ins.then_inc(s_v_setup.sem, 1)
                setup_n[0] += 1
                dve.wait_ge(s_v_setup.sem, setup_n[0])
            setup_n = [0]
            first(dve.memset(eps[:, 0:1], EPS))
            dve.memset(eps[:, 1:2], 0.0).then_inc(s_setup.sem, 1)
            for i, name in enumerate([n for n in START for _ in range(START[n])]):
                dve.memset(seed[:, i:i + 1], 0.0).then_inc(signals[name].sem, 1)
            dve.wait_ge(s_const_in.sem, 16)
            first(dve.tensor_copy(idb[:], cst("idn")))
            first(dve.tensor_copy(negq[:], cst("negq")))
            dve.tensor_copy(negd[:], cst("negd")).then_inc(s_c_bf.sem, 1)
            for n in range(8):
                dve.wait_ge(s_x_tr.sem, n + 1)
                c, i = n // 2, n % 2
                dve.tensor_copy(xT[:, 4 * i:4 * i + 4, c * P:(c + 1) * P],
                                bk[2 + n % 2].rearrange("p (k n) -> p k n", k=4)).then_inc(s_x_turned.sem, 1)
            dve.wait_ge(s_mem_rs.sem, 1)
            for c in range(2):
                dve.tensor_scalar(mjunk[:, c, :], mtok[:, c, :], ss8[:, 4 + c:5 + c], None, MUL
                                  ).then_inc(s_mem_n.sem, 1)
            for n in range(4):
                dve.wait_ge(s_m_tr.sem, n + 1)
                c, i = n // 2, n % 2
                dve.tensor_copy(memn[:, 4 * i:4 * i + 4, c * P:(c + 1) * P],
                                bk[4 + n % 2].rearrange("p (k n) -> p k n", k=4)).then_inc(s_m_ev.sem, 1)
            dve.wait_ge(s_m_ev.sem, 4)
            dve.wait_ge(s_x_turned.sem, 8)

            with dve.Fori(0, DEPTH) as l:
                def own(ins, s):
                    ins.then_inc(s.up(), 1)
                    dve.wait_ge(s.sem, s.at(l, s.n))

                def link(ins):
                    own(ins, s_dve_step)

                def split_lo(n, w=SEQ, src=None):
                    dve.wait_ge(s_h_hi.sem, s_h_hi.at(l, n + 1))
                    tt(h_lo[:, n % KT, 0:w], htmp[:, n % 2, 0:w] if src is None else src,
                             h_hi[:, n % KT, 0:w].bitcast(F32), SUB).then_inc(s_h_lo.up(), 1)

                def free_htmp(n):
                    if n >= 2:
                        dve.wait_ge(s_h_lo.sem, s_h_lo.at(l, n - 1))
                    else:
                        dve.wait_ge(s_h_lo.sem, s_h_lo.at(l, 0))

                def scaled(first_n, count, make):
                    for k in range(count):
                        free_htmp(first_n + k)
                        make(k, htmp[:, (first_n + k) % 2, :]).then_inc(s_h_f32.up(), 1)
                        if k >= 1:
                            split_lo(first_n + k - 1)
                    split_lo(first_n + count - 1)

                def norm_out(idx, first_n, g):
                    dve.wait_ge(s_nrm_rs.sem, s_nrm_rs.at(l, idx + 1))
                    scaled(first_n, KT, lambda k, o: stt(o, xT[:, k, :], col(g, k), rs[:, 0, :], MUL, MUL))

                def dense(b0, n, K, evac):
                    width = K * P

                    def body(q, slot, loads, first_):
                        for j in range(2):
                            dve.wait_ge(s_w_hi.sem, s_w_hi.at(l, 2 * q + (b0 + j + 1)))
                            tt(w_lo[j][:, 0:K, :].rearrange("p k n -> p (k n)"),
                                     raw[:, slot, j * width:(j + 1) * width],
                                     w_hi[j][:, 0:K, :].rearrange("p k n -> p (k n)").bitcast(F32), SUB).then_inc(s_w_lo.up(), 1)
                            if not first_ and evac is not None:
                                evac(2 * q + (j - 2), j)
                    pair_loop(dve, b0 // 2, n // 2, body)
                    if evac is not None:
                        for j in range(2):
                            evac(n - 2 + j, j)

                def add_out(b0):
                    def evac(o, j):
                        dve.wait_ge(s_blk_done.sem, s_blk_done.at(l, o + (b0 + 1)))
                        dst = xT[:, bass.ds(o, 1), :].rearrange("p a n -> p (a n)")
                        tt(dst, bk[j], dst, ADD).then_inc(s_evac_d.up(), 1)
                    return evac

                dve.wait_ge(s_prm_in.sem, s_prm_in.at(l, 32))
                lv = col("lamv", 0, 256).rearrange("p (a b n) -> p a b n", a=2, b=2)
                link(tt(lp[:], lv[:, :, 0, :], lv[:, :, 1, :], MUL))
                dve.reduce_sum(lsum[:], lp[:], AX.X).then_inc(s_lam_sum.up(), 1)
                link(tt(sg1[:], col("subg"), col("onemin"), MUL))
                dve.wait_ge(s_lam_exp.sem, s_lam_exp.at(l, 1))
                link(tt(nlam[:, 0:1], lexp[:, 1:2], lexp[:, 0:1], SUB))
                link(tt(nlam[:, 1:2], nlam[:, 0:1], col("laminit"), SUB))
                dve.wait_ge(s_wsm_hi.sem, s_wsm_hi.at(l, 1))
                tt(wsm_lo[:].rearrange("p k n -> p (k n)"), wsm[:].rearrange("p k n -> p (k n)"),
                         wsm_hi[:].rearrange("p k n -> p (k n)").bitcast(F32), SUB).then_inc(s_wsm_lo.up(), 1)

                norm_out(0, H_IN, "g_mix")
                dense(B_IN, N_IN, KT, None)

                dve.wait_ge(s_g_ps.sem, s_g_ps.at(l, 1))
                gp = bk[3][:, 0:48].rearrange("p (c n) -> p c n", c=NC)
                tt(gv[:], gp[:, :, 0:8], bcm(col("dtb", 0, 8), NC), ADD).then_inc(s_g_v.up(), 1)
                dve.tensor_copy(gb[:], gp[:, :, 8:12]).then_inc(s_g_v.up(), 1)

                for t in range(8):
                    dve.wait_ge(s_qk_rs.sem, s_qk_rs.at(l, t + 1))
                    stt(projT[:, t, :], projT[:, t, :], col("qg" if t < 4 else "kg"), rs[:, t % 2, :],
                              MUL, MUL).then_inc(s_qk_n.up(), 1)

                def da_max(n):
                    nk = (n % NC + 1) * P
                    i = n % 2
                    dve.wait_ge(s_da_s.sem, s_da_s.at(l, n + 1))
                    link(dve.reduce_max(rr[:, n, :], hi_banks[:, 2 * i:2 * i + 2, 0:nk], AX.X))
                    dve.tensor_scalar(mx[:, n, :], rr[:, n, :], -(DA_D ** -0.5), None, MUL).then_inc(s_da_nm.up(), 1)

                def da_weigh(n):
                    nk = (n % NC + 1) * P
                    dve.wait_ge(s_da_p.sem, s_da_p.at(l, 2 * n + 2))
                    link(dve.reciprocal(rr[:, n, :], sm[:, n, :]))
                    link(tt(rr[:, n, 1:2], rr[:, n, 1:2], nlam[:, 1:2], MUL))
                    if n >= 2:
                        dve.wait_ge(s_da_t.sem, s_da_t.at(l, n - 1))
                    w = wgt[:, n % 2, 0:nk]
                    link(dve.tensor_scalar(w, prob[:, n % 2, 0, 0:nk], rr[:, n, 0:1], None, MUL))
                    stt(w, prob[:, n % 2, 1, 0:nk], rr[:, n, 1:2], w, MUL, ADD).then_inc(s_da_w.up(), 1)

                ND = DA_H * NC
                for n in range(ND):
                    da_max(n)
                    if n >= 1:
                        da_weigh(n - 1)
                da_weigh(ND - 1)
                for h in range(DA_H):
                    n = H_MIX + h
                    dve.wait_ge(s_on_rs.sem, s_on_rs.at(l, h + 1))
                    free_htmp(n)
                    stt(htmp[:, n % 2, :], projT[:, h, :], sg1[:, 0:1], rs[:, h % 2, :], MUL, MUL).then_inc(s_h_f32.up(), 1)
                    if h >= 1:
                        split_lo(n - 1)
                split_lo(H_MIX + DA_H - 1)

                dve.wait_ge(s_g_ln.sem, s_g_ln.at(l, 2))
                link(stt(sp[:], gv[:], 0.0, g1[:], ALU.max, ADD))
                stt(ga[:], sp[:], -1.0, bcm(ag[:], NC), MUL, MUL).then_inc(s_g_a.up(), 1)
                link(dve.tensor_scalar(gb[:], gb[:], 1.0, None, ADD))
                link(dve.reciprocal(beta[:], gb[:]))
                dve.wait_ge(s_g_cum.sem, s_g_cum.at(l, 1))
                link(dve.tensor_copy(cums[:].rearrange("p a c h -> p (a c h)"), bk[3][:, 64:128]))
                link(dve.tensor_scalar(ncum[:], cums[:, 0], -1.0, None, MUL))
                tt(edk[:], cums[:, 1], cums[:, 0], SUB).then_inc(s_g_dk.up(), 1)

                def conv(t, src, dst):
                    w = lambda j: col("cw", 4 * t + j)
                    link(dve.tensor_scalar(dst, src, w(3), col("cb", t), MUL, ADD))
                    for j in (1, 2):
                        link(stt(dst[:, j:SEQ], src[:, 0:SEQ - j], w(3 - j), dst[:, j:SEQ], MUL, ADD))
                    stt(dst[:, 3:SEQ], src[:, 0:SEQ - 3], w(0), dst[:, 3:SEQ], MUL, ADD).then_inc(s_conv.up(), 1)

                for t in range(6):
                    conv(t, projT[:, 16 + t, :], convT[:, t, :])
                dve.wait_ge(s_g_edk.sem, s_g_edk.at(l, 1))
                for c in range(NC):
                    dve.wait_ge(s_s_tr.sem, s_s_tr.at(l, c + 1))
                    xp = bk[2 + c % 2][:, 0:256].rearrange("p (h d) -> p h d", h=S_H)
                    link(tt(xd[:, c], xp, bcl(sp[:, c, 0:4], S_D), MUL))
                    tt(xskip[:, c], xp, bcl(col("dsk", 0, 4), S_D), MUL).then_inc(s_s_x.up(), 1)
                    tt(xdd[:, c], xd[:, c], bcl(edk[:, c, 0:4], S_D), MUL).then_inc(s_s_x.up(), 1)

                def s_scores(c):
                    dve.wait_ge(s_s_dec.sem, s_s_dec.at(l, 4 * c + 4))
                    dve.wait_ge(s_s_cb.sem, s_s_cb.at(l, c + 1))
                    if c >= 2:
                        dve.wait_ge(s_s_y.sem, s_s_y.at(l, c - 1))
                    tt(scoT[:, c % 2].rearrange("p (g h) n -> p g h n", g=2),
                             dec[:, c % 2].rearrange("p (g h) n -> p g h n", g=2),
                             bk[6][:, 0:256].rearrange("p (g n) -> p g n", g=2).unsqueeze(2).to_broadcast([P, 2, 2, P]),
                             MUL).then_inc(s_s_st.up(), 1)

                def s_state(c):
                    dve.wait_ge(s_s_h.sem, s_s_h.at(l, c + 1))
                    ph = bk[c % 2][:, 0:256].rearrange("p (h d) -> p h d", h=S_H)
                    if c >= 1:
                        link(tt(hst[:, (c + 1) % 2], hst[:, c % 2], bcl(ex[:, 1, c, 0:4], S_D), MUL))
                        own(tt(hst[:, (c + 1) % 2], hst[:, (c + 1) % 2], ph, ADD), s_s_hst)
                    else:
                        own(dve.tensor_copy(hst[:, 1], ph), s_s_hst)

                def s_out(c):
                    dve.wait_ge(s_s_y.sem, s_s_y.at(l, c + 1))
                    yp = bk[7][:, 0:256].rearrange("p (h d) -> p h d", h=S_H)
                    yo = bk[7][:, 256:512].rearrange("p (h d) -> p h d", h=S_H)
                    if c:
                        link(tt(ytmp[:], yo, bcl(ex[:, 0, c, 0:4], S_D), MUL))
                        link(tt(ytmp[:], ytmp[:], xskip[:, c], ADD))
                        own(tt(ysd[:, c], ytmp[:], yp, ADD), s_s_ya)
                    else:
                        own(tt(ysd[:, c], xskip[:, c], yp, ADD), s_s_ya)

                dve.wait_ge(s_s_x.sem, s_s_x.at(l, 8))
                dve.wait_ge(s_g_ex.sem, s_g_ex.at(l, 1))
                for c in range(NC):
                    s_scores(c)
                    if c < NC - 1:
                        s_state(c)
                    s_out(c)
                dve.wait_ge(s_z_ev.sem, s_z_ev.at(l, 2))
                yf = ysd[:].rearrange("p c h d -> p (c h d)")
                link(tt(yf, yf, zst[:].rearrange("p c n -> p (c n)"), MUL))
                link(tt(ysq[:].rearrange("p c n -> p (c n)"), yf, yf, MUL))
                dve.reduce_sum(ss8[:], ysq[:].rearrange("p c (g n) -> p (c g) n", g=2), AX.X).then_inc(s_s_ss.up(), 1)
                dve.wait_ge(s_s_rs.sem, s_s_rs.at(l, 1))
                y8 = ysd[:].rearrange("p c (g h) d -> p (c g) (h d)", g=2)
                tt(y8, y8, bcl(ss8[:], P), MUL).then_inc(s_s_yn.up(), 1)
                for f in range(2):
                    n = H_MIX + 4 + f
                    dve.wait_ge(s_so_tr.sem, s_so_tr.at(l, f + 1))
                    free_htmp(n)
                    dve.tensor_scalar(htmp[:, n % 2, :], bk[2 + f], col("sng", f), None, MUL).then_inc(s_h_f32.up(), 1)
                for f in range(2):
                    split_lo(H_MIX + 4 + f)

                for t in range(6):
                    conv(6 + t, projT[:, 22 + t, :], convG[:, t, :])
                dve.wait_ge(s_gt_ev.sem, s_gt_ev.at(l, 8))
                flat = lambda a: a.rearrange("p c a h d -> p (c a h d)")
                link(tt(flat(gsq[:]), flat(qktok[:]), flat(qktok[:]), MUL))
                dve.reduce_sum(ss32[:].rearrange("p c n -> p (c n)"),
                                     gsq[:].rearrange("p c a h d -> p (c a h) d"), AX.X).then_inc(s_gn_ss.up(), 1)
                dve.wait_ge(s_gn_rs.sem, s_gn_rs.at(l, 1))
                link(dve.tensor_scalar(ss32[:, :, 0:4], ss32[:, :, 0:4], G_D ** -0.5, None, MUL))
                qk3 = qktok[:].rearrange("p c a h d -> p (c a h) d")
                own(tt(qk3, qk3, bcl(ss32[:].rearrange("p c n -> p (c n)"), G_D), MUL), s_gn_n)
                tt(qE[:], qktok[:, :, 0], bcl(ex[:, 0, :, 4:8], G_D), MUL).then_inc(s_gn_n.up(), 1)
                tt(kE[:], qktok[:, :, 1], bcl(ex[:, 0, :, 4:8], G_D), MUL).then_inc(s_gn_n.up(), 1)
                tt(kgt[:], qktok[:, :, 1], bcl(edk[:, :, 4:8], G_D), MUL).then_inc(s_gn_n.up(), 1)
                for c in range(NC):
                    dve.wait_ge(s_gd_dec.sem, s_gd_dec.at(l, 4 * c + 4))
                    dve.wait_ge(s_gd_kq.sem, s_gd_kq.at(l, c + 1))
                    D4 = decG[:, c % 2]
                    by_row = lambda a: a.rearrange("p (a r) n -> p r a n", r=2)
                    kkqk = hi_banks[:, 2:4, :].rearrange("p r (k a n) -> p k r a n", k=2, a=2)
                    own(tt(by_row(attT[:, c]), by_row(D4), kkqk[:, 1], MUL), s_gd_att)
                    link(tt(D4, D4, bcl(beta[:, c, :], P), MUL))
                    own(tt(by_row(aT[:, c]), by_row(D4), kkqk[:, 0], MUL), s_gd_at)
                for c in range(NC):
                    link(tt(tri_t[:, c], aT[:, c], bcm(lev(0), G_H), MUL))
                    own(tt(tri_t[:, c], bcm(cst("idn"), G_H), tri_t[:, c], SUB), s_ti_0)
                for v in range(NLEV - 1):
                    def mask(c, v=v):
                        n = v * NC + c
                        if n >= 2:
                            dve.wait_ge(s_m1_mm.sem, s_m1_mm.at(l, n - 1))
                        tt(lvlA[:, c % 2], aT[:, c], bcm(lev(v + 1), G_H), MUL).then_inc(s_lvl.up(), 1)
                    mask(0)
                    mask(1)
                    for c in range(NC):
                        n = v * NC + c
                        if v < NLEV - 2:
                            dve.wait_ge(s_tx_mm.sem, s_tx_mm.at(l, n + 1))
                            own(tt(tri_i[:, c], tri_i[:, c], bk[4 + c % 2].rearrange("p (h n) -> p h n", h=G_H), SUB), s_t_upd)
                        dve.wait_ge(s_tx_mm.sem, s_tx_mm.at(l, n + 1))
                        own(tt(tri_t[:, c], tri_t[:, c], bk[6 + c % 2].rearrange("p (h n) -> p h n", h=G_H), SUB), s_tt_upd)
                        if c + 2 < NC:
                            mask(c + 2)
                for c in range(NC):
                    dve.wait_ge(s_vn_mm.sem, s_vn_mm.at(l, c + 1))
                    if c >= 2:
                        dve.wait_ge(s_o_mm.sem, s_o_mm.at(l, c - 1))
                        dve.wait_ge(s_st_mm.sem, s_st_mm.at(l, c - 1))
                    tt(vnew[:, c % 2].rearrange("p (a r) d -> p r a d", r=2),
                             hi_banks[:, 0:2, 0:P].rearrange("p r (a d) -> p r a d", a=2),
                             bcl(beta[:, c, :].rearrange("p (a r) -> p r a", r=2), G_D), MUL).then_inc(s_vn.up(), 1)
                    if c < NC - 1:
                        dve.wait_ge(s_st_mm.sem, s_st_mm.at(l, c + 1))
                        new_, old = (c + 1) % 2, c % 2
                        if c == 0:
                            dve.tensor_copy(stS[:, new_].rearrange("p a d -> p (a d)"), bk[0][:, 0:P]).then_inc(s_st.up(), 1)
                        else:
                            for p_ in range(2):
                                for hh in range(2):
                                    r = slice(64 * hh, 64 * hh + 64)
                                    last = stt(stS[r, new_, p_, :], stS[r, old, p_, :],
                                               ex[r, 1, c, 4 + 2 * p_ + hh:5 + 2 * p_ + hh],
                                               bk[c % 2][r, p_ * 64:p_ * 64 + 64], MUL, ADD)
                                    if p_ + hh < 2:
                                        last.then_inc(s_dve_step.up(), 1)
                            last.then_inc(s_st.up(), 1)
                        dve.wait_ge(s_st.sem, s_st.at(l, c + 1))
                        dve.wait_ge(s_dve_step.sem, s_dve_step.at(l, s_dve_step.n))
                dve.wait_ge(s_o_ev.sem, s_o_ev.at(l, NC))
                dve.wait_ge(s_zg_ev.sem, s_zg_ev.at(l, 2))
                of = otok[:].rearrange("p c h d -> p (c h d)")
                link(tt(osq[:].rearrange("p c n -> p (c n)"), of, of, MUL))
                dve.reduce_sum(ss16[:], osq[:].rearrange("p c (h d) -> p (c h) d", h=G_H), AX.X).then_inc(s_go_ss.up(), 1)
                dve.wait_ge(s_go_rs.sem, s_go_rs.at(l, 1))
                link(tt(of, of, zgt[:].rearrange("p c n -> p (c n)"), MUL))
                o16 = otok[:].rearrange("p c h d -> p (c h) d")
                tt(o16, o16, bcl(ss16[:], G_D), MUL).then_inc(s_go_n.up(), 1)
                for f in range(2):
                    n = H_MIX + 6 + f
                    dve.wait_ge(s_go_tr.sem, s_go_tr.at(l, f + 1))
                    free_htmp(n)
                    dve.tensor_scalar(htmp[:, n % 2, :], bk[2 + f], col("gng", f), None, MUL).then_inc(s_h_f32.up(), 1)
                for f in range(2):
                    split_lo(H_MIX + 6 + f)

                dense(B_OUT, N_OUT, KT, add_out(B_OUT))
                for k in range(KT):
                    n = H_MEM + k
                    free_htmp(n)
                    dve.tensor_scalar(htmp[:, n % 2, 0:MEM], memn[:, k, :], col("g_mem", k), None, MUL).then_inc(s_h_f32.up(), 1)
                    if k >= 1:
                        split_lo(n - 1, MEM)
                split_lo(H_MEM + KT - 1, MEM)
                dense(B_KV, N_KV, KT, None)
                norm_out(1, H_X, "g_x")
                dense(B_CQ, N_CQ, KT, None)
                for m in range(8):
                    dve.wait_ge(s_c_rs.sem, s_c_rs.at(l, m + 1))
                    for f in range(2):
                        n = 2 * m + f
                        w = SEQ if n < 8 else MEM
                        t = qcT[:, n, :] if n < 8 else kvT[:, n - 8, :]
                        stt(t, t, col("xqg" if n < 8 else "xkg", f), rs[:, m % 2, 0:w], MUL, MUL).then_inc(s_c_n.up(), 1)

                def c_max(n):
                    dve.wait_ge(s_c_s.sem, s_c_s.at(l, n + 1))
                    link(dve.reduce_max(rr[:, n, :], bk[4 + n % 2].rearrange("p (i m) -> p i m", i=2), AX.X))
                    dve.tensor_scalar(mx[:, n, :], rr[:, n, :], -(X_D ** -0.5), None, MUL).then_inc(s_c_nm.up(), 1)

                def c_scale(n):
                    dve.wait_ge(s_c_p.sem, s_c_p.at(l, 2 * n + 2))
                    link(dve.reciprocal(rr[:, n, :], sm[:, n, :]))
                    tt(pc[:, n % 2], pc[:, n % 2], bcl(rr[:, n, :], MEM), MUL).then_inc(s_c_w.up(), 1)

                for n in range(8):
                    c_max(n)
                    if n >= 1:
                        c_scale(n - 1)
                    if n >= 3 and n % 2 == 1:
                        h = (n - 3) // 2
                        for e in range(2):
                            split_lo(H_CA + 2 * h + e, src=bk[e])
                c_scale(7)
                for e in range(2):
                    split_lo(H_CA + 6 + e, src=bk[e])
                dense(B_CO, N_CO, KT, add_out(B_CO))
                norm_out(2, H_FF, "g_ffn")
                b = B_FF
                for half in range(2):
                    f0 = half * FH

                    def ffn_out(i, j, b, f0):
                        if j == 0:
                            return
                        dve.wait_ge(s_f_sg.sem, s_f_sg.at(l, i + (f0 + 1)))
                        dve.wait_ge(s_blk_done.sem, s_blk_done.at(l, 2 * i + (b + 2)))
                        dve.wait_ge(s_f_hi.sem, s_f_hi.at(l, i + f0))
                        dve.wait_ge(s_f_lo.sem, s_f_lo.at(l, i + f0))
                        tt(h2[:], sgate[:], bk[1], MUL).then_inc(s_f_h2.up(), 1)
                        dve.wait_ge(s_f_hi.sem, s_f_hi.at(l, i + (f0 + 1)))
                        tt(f_lo[:, bass.ds(i, 1), :].rearrange("p a n -> p (a n)"), h2[:],
                                 f_hi[:, bass.ds(i, 1), :].rearrange("p a n -> p (a n)").bitcast(F32), SUB).then_inc(s_f_lo.up(), 1)

                    def body(q, slot, loads, first_, b=b, f0=f0):
                        for j in range(2):
                            dve.wait_ge(s_w_hi.sem, s_w_hi.at(l, 2 * q + (b + j + 1)))
                            tt(w_lo[j][:, 0:KT, :].rearrange("p k n -> p (k n)"),
                                     raw[:, slot, j * WA:(j + 1) * WA],
                                     w_hi[j][:, 0:KT, :].rearrange("p k n -> p (k n)").bitcast(F32), SUB).then_inc(s_w_lo.up(), 1)
                            if not first_:
                                ffn_out(q - 1, j, b, f0)
                    pair_loop(dve, b // 2, FH, body)
                    ffn_out(FH - 1, 1, b, f0)
                    b += N_GU
                    dense(b, N_DN, FH, add_out(b))
                    b += N_DN

        @block.tensor
        def _(pe):
            def mm(out, lhsT, rhs, start=True, stop=True):
                return pe.matmul(out, lhsT, rhs, start=start, stop=stop)

            idn, ones, blk, tri = cst("idn"), cst("ones"), cst("blk"), cst("tri")

            pe.wait_ge(s_const_in.sem, 16)
            pe.wait_ge(s_x_in.sem, 16)
            for n in range(8):
                c, i = n // 2, n % 2
                if n >= 2:
                    pe.wait_ge(s_x_turned.sem, n - 1)
                for k in range(4):
                    last = pe.transpose(bk[2 + n % 2][:, k * P:(k + 1) * P], xtok[:, c, (4 * i + k) * P:(4 * i + k + 1) * P], idn)
                last.then_inc(s_x_tr.sem, 1)
            pe.wait_ge(s_mem_n.sem, 2)
            for n in range(4):
                c, i = n // 2, n % 2
                if n >= 2:
                    pe.wait_ge(s_m_ev.sem, n - 1)
                for k in range(4):
                    last = pe.transpose(bk[4 + n % 2][:, k * P:(k + 1) * P], mjunk[:, c, (4 * i + k) * P:(4 * i + k + 1) * P], idn)
                last.then_inc(s_m_tr.sem, 1)
            pe.wait_ge(s_c_bf.sem, 1)

            with pe.Fori(0, DEPTH) as l:
                def product(j, K, hi, lo, w):
                    for k in range(K):
                        mm(bk[j][:, 0:w], w_hi[j][:, k, :], hi[:, k, 0:w], k == 0, False)
                        mm(bk[j][:, 0:w], w_hi[j][:, k, :], lo[:, k, 0:w], False, False)
                        last = mm(bk[j][:, 0:w], w_lo[j][:, k, :], hi[:, k, 0:w], False, k == K - 1)
                    last.then_inc(s_blk_done.up(), 1)

                def dense(b0, n, K, hi, lo, w, free, e0, *needs):
                    trips[0] = n // 2
                    with pe.Fori(0, n // 2) as i:
                        for j in range(2):
                            if j == 0:
                                for s, v in needs:
                                    pe.wait_ge(s.sem, s.at(l, v))
                            pe.wait_ge(s_w_lo.sem, s_w_lo.at(l, 2 * i + (b0 + j + 1)))
                            pe.wait_ge(free.sem, free.at(l, 2 * i + (e0 + j - 1)))
                            product(j, K, hi, lo, w)
                    trips[0] = 1

                def norm(idx):
                    for k in range(KT):
                        pe.wait_ge(s_nrm_sq.sem, s_nrm_sq.at(l, idx * KT + k + 1))
                        mm(bk[2], ones, sq[:, k % 2, :], k == 0, k == KT - 1).then_inc(s_nrm_mm.up(), 1)

                norm(0)
                pe.wait_ge(s_wsm_lo.sem, s_wsm_lo.at(l, 1))
                pe.wait_ge(s_h_lo.sem, s_h_lo.at(l, H_IN + KT))
                for c in range(NC):
                    o = bk[3][:, 12 * c:12 * c + 12]
                    for k in range(KT):
                        hh, hl = h_hi[:, k, c * P:(c + 1) * P], h_lo[:, k, c * P:(c + 1) * P]
                        mm(o, hh, wsm_hi[:, k, :], k == 0, False)
                        mm(o, hh, wsm_lo[:, k, :], False, False)
                        last = mm(o, hl, wsm_hi[:, k, :], False, k == KT - 1)
                last.then_inc(s_g_ps.up(), 1)
                dense(B_IN, N_IN, KT, h_hi, h_lo, SEQ, s_evac_a, EA_IN)

                pe.wait_ge(s_g_v.sem, s_g_v.at(l, 2))
                for t in range(8):
                    pe.wait_ge(s_qk_sq.sem, s_qk_sq.at(l, t + 1))
                    if t >= 2:
                        pe.wait_ge(s_qk_rs.sem, s_qk_rs.at(l, t - 1))
                    mm(bk[2 + t % 2], blk, sq[:, t % 2, :]).then_inc(s_qk_ss.up(), 1)
                for c in range(NC):
                    if c >= 2:
                        pe.wait_ge(s_v_ev.sem, s_v_ev.at(l, c - 1))
                    for h in range(DA_H):
                        last = pe.transpose(bk[4 + c % 2][:, h * P:(h + 1) * P], projT[:, 8 + h, c * P:(c + 1) * P], idn)
                    last.then_inc(s_v_tr.up(), 1)

                def da_scores(n):
                    h, qt = n // NC, n % NC
                    nk = (qt + 1) * P
                    if n >= 2:
                        pe.wait_ge(s_da_p.sem, s_da_p.at(l, 2 * (n - 1)))
                    for c in range(2):
                        r = slice(64 * c, 64 * c + 64)
                        b = bk[4 + 2 * (n % 2) + c]
                        mm(b[:, 0:nk], projT[r, h, qt * P:nk], projT[r, 4 + h, 0:nk], True, False)
                        last = mm(b[:, nk - P:nk], idb[:], negq[:], False, True)
                    last.then_inc(s_da_s.up(), 1)

                def da_turn(n):
                    pe.wait_ge(s_da_w.sem, s_da_w.at(l, n + 1))
                    if n >= 2:
                        pe.wait_ge(s_da_wt.sem, s_da_wt.at(l, n - 1))
                    for k in range(n % NC + 1):
                        last = pe.transpose(bk[2 + n % 2][:, k * P:(k + 1) * P], wgt[:, n % 2, k * P:(k + 1) * P], idn)
                    last.then_inc(s_da_t.up(), 1)

                def da_values(n):
                    h, qt = n // NC, n % NC
                    pe.wait_ge(s_da_wt.sem, s_da_wt.at(l, n + 1))
                    if qt == 0 and h >= 2:
                        pe.wait_ge(s_da_o.sem, s_da_o.at(l, h - 1))
                    for k in range(qt + 1):
                        last = mm(bk[h % 2][:, qt * P:(qt + 1) * P], vtok[:, k, h, :], wgtT[:, n % 2, k * P:(k + 1) * P],
                                  k == 0, k == qt)
                    last.then_inc(s_da_pv.up(), 1)

                pe.wait_ge(s_qk_n.sem, s_qk_n.at(l, 8))
                pe.wait_ge(s_v_ev.sem, s_v_ev.at(l, NC))
                ND = DA_H * NC
                for n in range(ND):
                    da_scores(n)
                    if n >= 1:
                        da_turn(n - 1)
                    if n >= 2:
                        da_values(n - 2)
                da_turn(ND - 1)
                da_values(ND - 2)
                da_values(ND - 1)
                for h in range(DA_H):
                    pe.wait_ge(s_on_sq.sem, s_on_sq.at(l, h + 1))
                    if h >= 2:
                        pe.wait_ge(s_on_rs.sem, s_on_rs.at(l, h - 1))
                    mm(bk[2 + h % 2], ones, sq[:, h % 2, :]).then_inc(s_on_ss.up(), 1)

                pe.wait_ge(s_on_rs.sem, s_on_rs.at(l, DA_H))
                pe.wait_ge(s_g_a.sem, s_g_a.at(l, 1))
                gaf = ga[:].rearrange("p c h -> p (c h)")
                mm(bk[3][:, 64:96], tri, gaf)
                mm(bk[3][:, 96:128], ones, gaf).then_inc(s_g_cum.up(), 1)

                def decays(b, c, h0):
                    for h in range(4):
                        o = b[:, h * P:(h + 1) * P]
                        mm(o, ga[:, c, h0 + h:h0 + h + 1].to_broadcast([P, P]), tri, True, False)
                        last = mm(o, idb[:], negd[:], False, True)
                    return last

                pe.wait_ge(s_g_dk.sem, s_g_dk.at(l, 1))
                for c in range(NC):
                    if c == 0:
                        pe.wait_ge(s_convs.sem, s_convs.at(l, 4))
                    if c >= 2:
                        pe.wait_ge(s_s_ev.sem, s_s_ev.at(l, c - 1))
                        pe.wait_ge(s_s_x.sem, s_s_x.at(l, 2 * (c - 1)))
                    for t in range(4):
                        last = pe.transpose(bk[2 + 2 * (t // 2) + c % 2][:, (t % 2) * P:(t % 2 + 1) * P],
                                            convT[:, t, c * P:(c + 1) * P], idn)
                    last.then_inc(s_s_tr.up(), 1)
                pe.wait_ge(s_s_ev.sem, s_s_ev.at(l, NC))
                pe.wait_ge(s_s_x.sem, s_s_x.at(l, 2 * NC))
                for i in range(2):
                    for c in range(2):
                        for t in range(2):
                            cc = 2 * i + c
                            last = pe.transpose(bk[2 + i][:, (2 * c + t) * P:(2 * c + t + 1) * P],
                                                projT[:, 12 + t, cc * P:(cc + 1) * P], idn)
                    last.then_inc(s_z_tr.up(), 1)
                pe.wait_ge(s_convs.sem, s_convs.at(l, 6))
                for c in range(NC):
                    cs = slice(c * P, (c + 1) * P)
                    if c >= 2:
                        pe.wait_ge(s_s_dec.sem, s_s_dec.at(l, 4 * (c - 1)))
                    decays(bk[4 + c % 2], c, 0).then_inc(s_s_d.up(), 1)
                    if c >= 1:
                        pe.wait_ge(s_s_st.sem, s_s_st.at(l, c))
                    for g in range(2):
                        last = mm(bk[6][:, g * P:(g + 1) * P], convT[:, 2 + g, cs], convT[:, 4 + g, cs])
                    last.then_inc(s_s_cb.up(), 1)
                    if c < NC - 1:
                        if c >= 2:
                            pe.wait_ge(s_s_hst.sem, s_s_hst.at(l, c - 1))
                        for g in range(2):
                            last = mm(bk[c % 2][:, g * P:(g + 1) * P], btok[:, c, g, :],
                                      xdd[:, c, 2 * g:2 * g + 2, :].rearrange("p h d -> p (h d)"))
                        last.then_inc(s_s_h.up(), 1)
                    pe.wait_ge(s_s_st.sem, s_s_st.at(l, c + 1))
                    if c >= 1:
                        pe.wait_ge(s_s_ya.sem, s_s_ya.at(l, c))
                        pe.wait_ge(s_s_hst.sem, s_s_hst.at(l, c))
                    for h in range(S_H):
                        last = mm(bk[7][:, h * S_D:(h + 1) * S_D], scoT[:, c % 2, h, :], xd[:, c, h, :])
                    if c:
                        for g in range(2):
                            last = mm(bk[7][:, 256 + g * P:256 + (g + 1) * P], convT[:, 4 + g, cs],
                                      hst[:, c % 2, 2 * g:2 * g + 2, :].rearrange("p h d -> p (h d)"))
                    last.then_inc(s_s_y.up(), 1)
                pe.wait_ge(s_s_yn.sem, s_s_yn.at(l, 1))
                for f in range(2):
                    for c in range(NC):
                        last = pe.transpose(bk[2 + f][:, c * P:(c + 1) * P],
                                            ysd[:, c, 2 * f:2 * f + 2, :].rearrange("p h d -> p (h d)"), idn)
                    last.then_inc(s_so_tr.up(), 1)

                pe.wait_ge(s_convs.sem, s_convs.at(l, 12))
                pe.wait_ge(s_h_f32.sem, s_h_f32.at(l, H_MIX + 6))
                for c in range(NC):
                    if c >= 2:
                        pe.wait_ge(s_gt_ev.sem, s_gt_ev.at(l, 2 * (c - 1)))
                    for t in range(6):
                        o = bk[2 + c % 2][:, t * P:(t + 1) * P] if t < 4 else bk[4 + c % 2][:, (t - 4) * P:(t - 3) * P]
                        last = pe.transpose(o, convG[:, t, c * P:(c + 1) * P], idn)
                    last.then_inc(s_gt_tr.up(), 1)
                pe.wait_ge(s_gt_ev.sem, s_gt_ev.at(l, 8))
                for i in range(6):
                    which, pr = i // 2, i % 2
                    if i == 0:
                        pe.wait_ge(s_gn_n.sem, s_gn_n.at(l, 2))
                    if i >= 2:
                        pe.wait_ge(s_g3_ev.sem, s_g3_ev.at(l, i - 1))
                    for c in range(NC):
                        src = (qktok[:, c, 1], qktok[:, c, 0], qE[:, c])[which]
                        last = pe.transpose(bk[2 + pr][:, c * P:(c + 1) * P],
                                            src[:, 2 * pr:2 * pr + 2, :].rearrange("p h d -> p (h d)"), idn)
                    last.then_inc(s_g3_tr.up(), 1)
                pe.wait_ge(s_g3_ev.sem, s_g3_ev.at(l, 6))
                for c in range(NC):
                    cs = slice(c * P, (c + 1) * P)
                    if c >= 2:
                        pe.wait_ge(s_gd_dec.sem, s_gd_dec.at(l, 4 * (c - 1)))
                    decays(bk[4 + c % 2], c, 4).then_inc(s_gd_d.up(), 1)
                    if c >= 1:
                        pe.wait_ge(s_gd_at.sem, s_gd_at.at(l, c))
                        pe.wait_ge(s_gd_att.sem, s_gd_att.at(l, c))
                    for h in range(G_H):
                        r = slice(64 * (h % 2), 64 * (h % 2) + 64)
                        kk = tr3[r, 0, h // 2, cs]
                        o = bk[6 + h % 2]
                        mm(o[:, (h // 2) * P:(h // 2 + 1) * P], kk, kk)
                        last = mm(o[:, (2 + h // 2) * P:(3 + h // 2) * P], kk, tr3[r, 1, h // 2, cs])
                    last.then_inc(s_gd_kq.up(), 1)
                for c in range(NC):
                    pe.wait_ge(s_ti_0.sem, s_ti_0.at(l, c + 1))
                    if c >= 2:
                        pe.wait_ge(s_ti_ev.sem, s_ti_ev.at(l, c - 1))
                    for h in range(G_H):
                        last = pe.transpose(bk[2 + c % 2][:, h * P:(h + 1) * P], tri_t[:, c, h, :], idn)
                    last.then_inc(s_ti_tr.up(), 1)
                for v in range(NLEV - 1):
                    for c in range(NC + 1):
                        if c < NC:
                            n = v * NC + c
                            pe.wait_ge(s_lvl.sem, s_lvl.at(l, n + 1))
                            if n < 2:
                                pe.wait_ge(s_ti_ev.sem, s_ti_ev.at(l, c + 3))
                            else:
                                pe.wait_ge(s_m1_ev.sem, s_m1_ev.at(l, n - 1))
                            if v >= 1:
                                pe.wait_ge(s_t_upd.sem, s_t_upd.at(l, n - NC + 1))
                            elif c < NC:
                                pe.wait_ge(s_ti_ev.sem, s_ti_ev.at(l, NC))
                            for h in range(G_H):
                                last = mm(bk[2 + c % 2][:, h * P:(h + 1) * P], lvlA[:, c % 2, h, :], tri_i[:, c, h, :])
                            last.then_inc(s_m1_mm.up(), 1)
                        if c >= 1:
                            d = c - 1
                            n = v * NC + d
                            pe.wait_ge(s_m1_ev.sem, s_m1_ev.at(l, n + 1))
                            if n >= 2:
                                pe.wait_ge(s_tt_upd.sem, s_tt_upd.at(l, n - 1))
                            if v >= 1:
                                pe.wait_ge(s_tt_upd.sem, s_tt_upd.at(l, n - NC + 1))
                            for h in range(G_H):
                                if v < NLEV - 2:
                                    mm(bk[4 + d % 2][:, h * P:(h + 1) * P], tri_t[:, d, h, :], m1[:, d, h, :])
                                last = mm(bk[6 + d % 2][:, h * P:(h + 1) * P], m1[:, d, h, :], tri_t[:, d, h, :])
                            last.then_inc(s_tx_mm.up(), 1)
                pe.wait_ge(s_tt_upd.sem, s_tt_upd.at(l, (NLEV - 1) * NC))
                pe.wait_ge(s_m1_ev.sem, s_m1_ev.at(l, (NLEV - 1) * NC))
                for pr in range(2):
                    for c in range(NC):
                        for hh in range(2):
                            h = 2 * pr + hh
                            last = mm(bk[2 + pr][64 * hh:64 * hh + 64, c * P:(c + 1) * P], kE[:, c, h, :],
                                      tri_t[:, c, h, :])
                    last.then_inc(s_w_mm.up(), 1)
                pe.wait_ge(s_w_ev.sem, s_w_ev.at(l, 2))
                for c in range(NC):
                    cs = slice(c * P, (c + 1) * P)
                    if c >= 1:
                        pe.wait_ge(s_vn.sem, s_vn.at(l, c))
                        pe.wait_ge(s_st.sem, s_st.at(l, c))
                    for h in range(G_H):
                        r = slice(64 * (h % 2), 64 * (h % 2) + 64)
                        o = bk[4 + h % 2][:, (h // 2) * G_D:(h // 2 + 1) * G_D]
                        last = mm(o, tri_t[:, c, h, :], gvtok[:, c, h, :], True, c == 0)
                        if c:
                            last = mm(o, wTn[r, h // 2, cs], stS[r, c % 2, h // 2, :], False, True)
                    last.then_inc(s_vn_mm.up(), 1)
                    pe.wait_ge(s_vn.sem, s_vn.at(l, c + 1))
                    if c < NC - 1:
                        for h in range(G_H):
                            r = slice(64 * (h % 2), 64 * (h % 2) + 64)
                            last = mm(bk[c % 2][r, (h // 2) * G_D:(h // 2 + 1) * G_D], kgt[:, c, h, :], vnew[:, c % 2, h, :])
                        last.then_inc(s_st_mm.up(), 1)
                    if c >= 1:
                        pe.wait_ge(s_o_ev.sem, s_o_ev.at(l, c))
                    for h in range(G_H):
                        r = slice(64 * (h % 2), 64 * (h % 2) + 64)
                        o = bk[6 + h % 2][:, (h // 2) * G_D:(h // 2 + 1) * G_D]
                        if c:
                            mm(o, tr3[r, 2, h // 2, cs], stS[r, c % 2, h // 2, :], True, False)
                        last = mm(o, attT[:, c, h, :], vnew[:, c % 2, h, :], c == 0, True)
                    last.then_inc(s_o_mm.up(), 1)
                for i in range(2):
                    for c in range(2):
                        for t in range(2):
                            cc = 2 * i + c
                            last = pe.transpose(bk[2 + i][:, (2 * c + t) * P:(2 * c + t + 1) * P],
                                                projT[:, 14 + t, cc * P:(cc + 1) * P], idn)
                    last.then_inc(s_zg_tr.up(), 1)
                pe.wait_ge(s_zg_ev.sem, s_zg_ev.at(l, 2))
                pe.wait_ge(s_go_n.sem, s_go_n.at(l, 1))
                for f in range(2):
                    for c in range(NC):
                        last = pe.transpose(bk[2 + f][:, c * P:(c + 1) * P],
                                            otok[:, c, 2 * f:2 * f + 2, :].rearrange("p h d -> p (h d)"), idn)
                    last.then_inc(s_go_tr.up(), 1)

                dense(B_OUT, N_OUT, KT, h_hi, h_lo, SEQ, s_evac_d, ED_OUT, (s_h_lo, H_MIX + KT))
                dense(B_KV, N_KV, KT, h_hi, h_lo, MEM, s_evac_a, EA_KV, (s_h_lo, H_MEM + KT), (s_evac_d, ED_OUT + N_OUT))
                norm(1)
                dense(B_CQ, N_CQ, KT, h_hi, h_lo, SEQ, s_evac_a, EA_CQ, (s_h_lo, H_X + KT))
                for n in range(16):
                    w = SEQ if n < 8 else MEM
                    pe.wait_ge(s_c_sq.sem, s_c_sq.at(l, n + 1))
                    if n % 2 == 0 and n >= 4:
                        pe.wait_ge(s_c_rs.sem, s_c_rs.at(l, n // 2 - 1))
                    mm(bk[2 + (n // 2) % 2][:, 0:w], ones, sq[:, n % 2, 0:w], n % 2 == 0, n % 2 == 1).then_inc(s_c_ssm.up(), 1)
                pe.wait_ge(s_c_rs.sem, s_c_rs.at(l, 8))
                for i in range(4):
                    if i >= 2:
                        pe.wait_ge(s_cv_ev.sem, s_cv_ev.at(l, i - 1))
                    for t in range(4):
                        last = pe.transpose(bk[2 + i % 2][:, t * P:(t + 1) * P],
                                            kvT[:, 8 + 4 * (i % 2) + t, (i // 2) * P:(i // 2 + 1) * P], idn)
                    last.then_inc(s_cv_tr.up(), 1)

                def c_scores(n):
                    h, qp = n // 2, n % 2
                    if n >= 2:
                        pe.wait_ge(s_c_p.sem, s_c_p.at(l, 2 * (n - 1)))
                    for i in range(2):
                        q0 = (2 * qp + i) * P
                        for f in range(2):
                            last = mm(bk[4 + n % 2][:, i * MEM:(i + 1) * MEM], qcT[:, 2 * h + f, q0:q0 + P],
                                      kvT[:, 2 * h + f, :], f == 0, f == 1)
                    last.then_inc(s_c_s.up(), 1)

                def c_turn(n):
                    pe.wait_ge(s_c_w.sem, s_c_w.at(l, n + 1))
                    if n >= 2:
                        pe.wait_ge(s_c_pt.sem, s_c_pt.at(l, n - 1))
                    for i in range(2):
                        for m in range(2):
                            last = pe.transpose(bk[6 + n % 2][:, m * 256 + i * P:m * 256 + (i + 1) * P],
                                                pc[:, n % 2, i, m * P:(m + 1) * P], idn)
                    last.then_inc(s_c_t.up(), 1)

                def c_values(h):
                    pe.wait_ge(s_c_pt.sem, s_c_pt.at(l, 2 * h + 2))
                    for e in range(2):
                        if h >= 1:
                            pe.wait_ge(s_h_lo.sem, s_h_lo.at(l, H_CA + 2 * (h - 1) + e + 1))
                        for m in range(2):
                            last = mm(bk[e], vmt[:, m, h * X_D + e * P:h * X_D + (e + 1) * P], pT[:, h % 2, m, :],
                                      m == 0, m == 1)
                        last.then_inc(s_c_pv.up(), 1)

                pe.wait_ge(s_c_n.sem, s_c_n.at(l, 16))
                pe.wait_ge(s_cv_ev.sem, s_cv_ev.at(l, 4))
                for n in range(8):
                    c_scores(n)
                    if n >= 1:
                        c_turn(n - 1)
                    if n >= 2 and n % 2 == 0:
                        c_values(n // 2 - 1)
                c_turn(7)
                c_values(3)
                dense(B_CO, N_CO, KT, h_hi, h_lo, SEQ, s_evac_d, ED_CO, (s_h_lo, H_CA + KT))
                norm(2)
                b = B_FF
                for half in range(2):
                    f0, e0 = half * FH, ED_DN + half * N_DN
                    trips[0] = FH
                    with pe.Fori(0, FH) as i:
                        pe.wait_ge(s_h_lo.sem, s_h_lo.at(l, H_FF + KT))
                        pe.wait_ge(s_evac_d.sem, s_evac_d.at(l, e0))
                        for j, free in enumerate((s_f_sg, s_f_h2)):
                            pe.wait_ge(s_w_lo.sem, s_w_lo.at(l, 2 * i + (b + j + 1)))
                            pe.wait_ge(free.sem, free.at(l, i + f0))
                            product(j, KT, h_hi, h_lo, SEQ)
                    trips[0] = 1
                    b += N_GU
                    dense(b, N_DN, FH, f_hi, f_lo, SEQ, s_evac_d, e0, (s_f_sg, f0 + FH), (s_f_lo, f0 + FH))
                    b += N_DN
            for n in range(8):
                c, i = n // 2, n % 2
                if n == 0:
                    pe.wait_ge(s_evac_d.sem, s_evac_d.at(DEPTH, 0))
                if n >= 2:
                    pe.wait_ge(s_y_ready.sem, n - 1)
                for k in range(4):
                    last = pe.transpose(bk[2 + n % 2][:, k * P:(k + 1) * P], xT[:, 4 * i + k, c * P:(c + 1) * P], idn)
                last.then_inc(s_y_tr.sem, 1)

        got = {k: v for k, v in ((k, s.n) for k, s in signals.items()) if v}
        if got != PER_LAYER:
            if strict:
                raise AssertionError(f"PER_LAYER = {got}")
        return got


def layout(inp):
    f = lambda n: np.ascontiguousarray(np.asarray(inp[n]))
    L = DEPTH
    w_in = f("w_in")
    o = np.cumsum([0, 512, 512, 512, 256, 768, 4, 768, 256, 4, 4])
    part = {n: w_in[:, :, o[i]:o[i + 1]] for i, n in enumerate(("qa", "ka", "va", "zs", "xbc", "dt", "qkv", "zg", "b", "a"))}
    big = np.concatenate([part[n] for n in ("qa", "ka", "va", "zs", "zg", "xbc", "qkv")], axis=2)
    small = np.concatenate([part[n] for n in ("dt", "a", "b")], axis=2)

    def blocks(w, k):
        Lw, K, N = w.shape
        return w.reshape(Lw, k, P, N // P, P).transpose(0, 3, 2, 1, 4).reshape(Lw, N // P, P, k * P)

    gu = blocks(f("w_gate_up"), KT)
    gu = np.stack([gu[:, :FT], gu[:, FT:]], axis=2).reshape(L, 2 * FT, P, WA)
    wa = np.concatenate([blocks(big, KT), blocks(f("w_out"), KT), blocks(f("w_ckv"), KT), blocks(f("w_cq"), KT),
                         blocks(f("w_co"), KT), gu], axis=1)
    wa = wa.reshape(L, PAIRS_A, 2, P, WA).transpose(0, 1, 3, 2, 4).reshape(L * PAIRS_A, P, 2 * WA)
    dn = f("w_down").reshape(L, 2, FH * P, D_MODEL)
    wd = np.stack([blocks(dn[:, h], FH) for h in range(2)], axis=1)
    wd = wd.reshape(L, PAIRS_D, 2, P, WD).transpose(0, 1, 3, 2, 4).reshape(L * PAIRS_D, P, 2 * WD)
    wsm = small.reshape(L, KT, P, 12).transpose(0, 2, 1, 3).reshape(L, P, KT * 12)

    rows = lambda a: np.broadcast_to(a[:, None, :], (L, P, a.shape[-1]))
    tiles = lambda a: a.reshape(L, -1, P).transpose(0, 2, 1)
    twice = lambda a: np.concatenate([a, a], axis=-1)[:, :, None]
    cw = np.concatenate([f("ssd_conv_w"), f("gdn_conv_w")], axis=2)
    cw = cw.reshape(L, 4, 12, P).transpose(0, 3, 2, 1).reshape(L, P, 48)
    cb = tiles(np.concatenate([f("ssd_conv_b"), np.zeros((L, 768), np.float32)], axis=1))
    li = np.array([0.8 - 0.6 * math.exp(-0.3 * l) for l in range(L)], np.float32)
    lamv = np.concatenate([f("da_lambda_q1"), f("da_lambda_k1"), f("da_lambda_q2"), f("da_lambda_k2")], axis=1)
    gng = twice(f("gdn_norm_g"))
    prm = np.concatenate([
        tiles(f("norm_mix_g")), tiles(f("norm_x_g")), tiles(f("norm_mem_g")), tiles(f("norm_ffn_g")),
        twice(f("da_q_norm_g")), twice(f("da_k_norm_g")), f("da_sub_norm_g")[:, :, None], cw, cb,
        rows(np.concatenate([f("ssd_dt_bias"), f("gdn_dt_bias")], axis=1)),
        rows(np.concatenate([f("ssd_A_log"), f("gdn_A_log")], axis=1)),
        rows(f("ssd_D")), tiles(f("ssd_norm_g")), gng, gng, tiles(f("xq_norm_g")), tiles(f("xk_norm_g")),
        rows(li[:, None]), rows(np.array([1.0 - (0.8 - 0.6 * math.exp(-0.3 * l)) for l in range(L)], np.float32)[:, None]),
        rows(lamv)], axis=2)
    i = np.arange(P)
    con = np.zeros((P, NCON), np.float32)
    put = lambda n, a: con.__setitem__((slice(None), slice(*CC[n])), a)
    put("idn", np.eye(P))
    put("ones", 1.0)
    put("blk", i[:, None] // 64 == i[None, :] // 64)
    put("tri", i[:, None] <= i[None, :])
    put("negq", np.where(i[None, :] > i[:, None], -1e30, 0.0))
    put("negd", np.where(i[None, :] < i[:, None], -1e30, 0.0))
    levels = []
    for v in range(NLEV):
        b = 1 << v
        same = (i[:, None] // (2 * b)) == (i[None, :] // (2 * b))
        levels.append(same & (i[:, None] % (2 * b) < b) & (i[None, :] % (2 * b) >= b))
    put("lev", np.concatenate(levels, axis=1))
    c = np.ascontiguousarray
    return {"x": c(f("x")[0]), "mem": c(f("mem")[0]), "wa": c(wa), "wd": c(wd), "wsm": c(wsm), "prm": c(prm), "con": con}


def kernel(**inputs):
    import concourse.bacc as _bacc
    from concourse.bass_utils import run_bass_kernel_spmd as _run

    nc = _bacc.Bacc("TRN2", target_bir_lowering=False, num_devices=1)
    arrays = layout(inputs)
    args = [nc.dram_tensor(f"in_{n}", a.shape, mybir.dt.from_np(a.dtype), kind="ExternalInput").ap()
            for n, a in arrays.items()]
    out = nc.dram_tensor("out_x", (SEQ, D_MODEL), F32, kind="ExternalOutput").ap()
    trunk(nc, *args, out)
    r = _run(nc, [{f"in_{n}": a for n, a in arrays.items()}], core_ids=[0])
    return r.results[0]["out_x"].reshape(1, SEQ, D_MODEL)
```

```python
import math
from contextlib import ExitStack

import numpy as np
import concourse.bass as bass
from concourse import mybir

P = 128
D_MODEL, SEQ, DEPTH, MEM = 1024, 512, 2, 256
EPS = 1e-6
KT = D_MODEL // P
CH = 128
NC = SEQ // CH
DA_H, DA_D, DA_V = 4, 64, 128
S_H, S_D = 4, 64
G_H, G_D = 4, 64
X_H, X_D = 4, 256
ND = DA_H * NC
D_FF = 2816
FT = D_FF // P
FH = FT // 2
NLEV = 7
NJ = (NLEV - 1) * NC

F32, F32R, BF16 = mybir.dt.float32, mybir.dt.float32r, mybir.dt.bfloat16
ACT = mybir.ActivationFunctionType
ALU = mybir.AluOpType
AX = mybir.AxisListType

LN_EXP = "natural_log_exp_and_others"

B_IN, N_IN = 0, 28
N_QK, N_V, N_CONV = 8, 4, 12
B_OUT, N_OUT = 28, 8
B_KV, N_KV = 36, 16
B_CQ, N_CQ = 52, 8
B_CO, N_CO = 60, 8
B_FF = 68
N_GU, N_DN = 2 * FH, 8
NB = B_FF + 2 * (N_GU + N_DN)
PAIRS_A = (B_FF + 2 * N_GU) // 2
PAIRS_D = N_DN
WA, WD = KT * P, FH * P

H_MIX, H_IN, H_MEM, H_X, H_CA, H_FF = 8, 0, 16, 24, 32, 40

EA_IN, EA_KV, EA_CQ = 0, 28, 44
ED_OUT, ED_CO, ED_DN = 0, 8, 16

PC = {}
_at = 0
for _n, _w in (("g_mix", 8), ("g_x", 8), ("g_mem", 8), ("g_ffn", 8), ("qkg", 8), ("subg", 1),
               ("cw", 48), ("cb", 12), ("dtb", 8), ("alog", 8), ("dsk", 4), ("sng", 2), ("gng", 2),
               ("xqg", 2), ("xkg", 2), ("laminit", 1), ("onemin", 1), ("lamv", 256)):
    PC[_n] = (_at, _at + _w)
    _at += _w
NPRM = _at
CC = {n: (i * P, (i + 1) * P) for i, n in enumerate(("idn", "ones", "blk", "tri", "negq", "negd"))}
CC["lev"] = (6 * P, (6 + NLEV) * P)
NCON = (6 + NLEV) * P

PER_LAYER = {
    "act_step": 28, "blk_done": 128, "c_n": 16, "c_nm": 8, "c_p": 16, "c_pt": 8, "c_pv": 8, "c_rs": 8, "c_s": 8,
    "c_sq": 16, "c_ssm": 16, "c_t": 8, "c_w": 8, "conv": 12, "convs": 12, "cv_ev": 4, "cv_tr": 4, "da_nm": 16,
    "da_o": 4, "da_p": 32, "da_pv": 16, "da_s": 16, "da_t": 16, "da_w": 16, "da_wt": 16, "dve_step": 157,
    "evac_a": 52, "evac_d": 32, "f_h2": 22, "f_hi": 22, "f_lo": 22, "f_sg": 22, "g3_ev": 6, "g3_tr": 6, "g_a":
    1, "g_cum": 1, "g_dk": 1, "g_edk": 1, "g_ex": 1, "g_ln": 2, "g_ps": 1, "g_v": 2, "gd_at": 4, "gd_att": 4,
    "gd_d": 4, "gd_dec": 16, "gd_kq": 4, "gn_n": 4, "gn_rs": 1, "gn_ss": 1, "go_n": 1, "go_rs": 1, "go_ss": 1,
    "go_tr": 2, "gt_ev": 8, "gt_tr": 4, "h_f32": 40, "h_hi": 48, "h_lo": 48, "lam_exp": 2, "lam_sum": 1, "lvl":
    24, "m1_ev": 24, "m1_mm": 24, "nrm_mm": 24, "nrm_rs": 3, "nrm_sq": 24, "o_ev": 4, "o_mm": 4, "on_rs": 4,
    "on_sq": 4, "on_ss": 4, "prm_in": 32, "qk_n": 8, "qk_rs": 8, "qk_sq": 8, "qk_ss": 8, "raw_in0": 512,
    "raw_in1": 512, "s_cb": 4, "s_d": 4, "s_dec": 16, "s_ev": 4, "s_h": 3, "s_hst": 3, "s_rs": 1, "s_ss": 1,
    "s_st": 4, "s_tr": 4, "s_x": 8, "s_y": 4, "s_ya": 4, "s_yn": 1, "so_tr": 2, "st": 3, "st_mm": 3, "t_upd":
    20, "ti_0": 4, "ti_ev": 4, "ti_tr": 4, "tt_upd": 24, "tx_mm": 24, "v_ev": 4, "v_tr": 4, "vn": 4, "vn_mm": 4,
    "w_ev": 2, "w_hi": 128, "w_lo": 128, "w_mm": 2, "wsm_hi": 1, "wsm_lo": 1, "z_ev": 2, "z_tr": 2, "zg_ev": 2,
    "zg_tr": 2
}


START = {"qk_ss": 1, "qk_n": 1, "w_lo": 3, "blk_done": 2, "evac_a": 2, "evac_d": 2, "f_sg": 1, "f_h2": 1, "f_hi": 1, "f_lo": 1, "h_lo": 1}


class Signal:

    def __init__(self, nc, ctx, name, trips):
        self.sem = ctx.enter_context(nc.semaphore(name))
        self.name, self.n, self.trips = name, 0, trips
        self.per_layer, self.start = PER_LAYER.get(name, 0), START.get(name, 0)

    def up(self, by=1):
        self.n += by * self.trips[0]
        return self.sem

    def at(self, l, v):
        return l * self.per_layer + (v + self.start)


def trunk(nc, x_d, mem_d, wa_d, wd_d, wsm_d, prm_d, con_d, out_d, strict=True):
    ctx = ExitStack()
    nc.disable_value_cache = True
    with ctx:
        trips = [1]
        signals = {}

        def signal(name):
            signals[name] = Signal(nc, ctx, name, trips)
            return signals[name]

        s_act_step = signal("act_step")
        s_blk_done = signal("blk_done")
        s_c_bf = signal("c_bf")
        s_c_n = signal("c_n")
        s_c_nm = signal("c_nm")
        s_c_p = signal("c_p")
        s_c_pt = signal("c_pt")
        s_c_pv = signal("c_pv")
        s_c_rs = signal("c_rs")
        s_c_s = signal("c_s")
        s_c_sq = signal("c_sq")
        s_c_ssm = signal("c_ssm")
        s_c_t = signal("c_t")
        s_c_w = signal("c_w")
        s_const_in = signal("const_in")
        s_conv = signal("conv")
        s_convs = signal("convs")
        s_cv_ev = signal("cv_ev")
        s_cv_tr = signal("cv_tr")
        s_da_nm = signal("da_nm")
        s_da_o = signal("da_o")
        s_da_p = signal("da_p")
        s_da_pv = signal("da_pv")
        s_da_s = signal("da_s")
        s_da_t = signal("da_t")
        s_da_w = signal("da_w")
        s_da_wt = signal("da_wt")
        s_dve_step = signal("dve_step")
        s_evac_a = signal("evac_a")
        s_evac_d = signal("evac_d")
        s_f_h2 = signal("f_h2")
        s_f_hi = signal("f_hi")
        s_f_lo = signal("f_lo")
        s_f_sg = signal("f_sg")
        s_g3_ev = signal("g3_ev")
        s_g3_tr = signal("g3_tr")
        s_g_a = signal("g_a")
        s_g_cum = signal("g_cum")
        s_g_dk = signal("g_dk")
        s_g_edk = signal("g_edk")
        s_g_ex = signal("g_ex")
        s_g_ln = signal("g_ln")
        s_g_ps = signal("g_ps")
        s_g_v = signal("g_v")
        s_gd_at = signal("gd_at")
        s_gd_att = signal("gd_att")
        s_gd_d = signal("gd_d")
        s_gd_dec = signal("gd_dec")
        s_gd_kq = signal("gd_kq")
        s_gn_n = signal("gn_n")
        s_gn_rs = signal("gn_rs")
        s_gn_ss = signal("gn_ss")
        s_go_n = signal("go_n")
        s_go_rs = signal("go_rs")
        s_go_ss = signal("go_ss")
        s_go_tr = signal("go_tr")
        s_gt_ev = signal("gt_ev")
        s_gt_tr = signal("gt_tr")
        s_h_f32 = signal("h_f32")
        s_h_hi = signal("h_hi")
        s_h_lo = signal("h_lo")
        s_lam_exp = signal("lam_exp")
        s_lam_sum = signal("lam_sum")
        s_lvl = signal("lvl")
        s_m1_ev = signal("m1_ev")
        s_m1_mm = signal("m1_mm")
        s_m_ev = signal("m_ev")
        s_m_tr = signal("m_tr")
        s_mem_in = signal("mem_in")
        s_mem_n = signal("mem_n")
        s_mem_rs = signal("mem_rs")
        s_mem_sq = signal("mem_sq")
        s_nrm_mm = signal("nrm_mm")
        s_nrm_rs = signal("nrm_rs")
        s_nrm_sq = signal("nrm_sq")
        s_o_ev = signal("o_ev")
        s_o_mm = signal("o_mm")
        s_on_rs = signal("on_rs")
        s_on_sq = signal("on_sq")
        s_on_ss = signal("on_ss")
        s_prm_in = signal("prm_in")
        s_qk_n = signal("qk_n")
        s_qk_rs = signal("qk_rs")
        s_qk_sq = signal("qk_sq")
        s_qk_ss = signal("qk_ss")
        s_s_cb = signal("s_cb")
        s_s_d = signal("s_d")
        s_s_dec = signal("s_dec")
        s_s_ev = signal("s_ev")
        s_s_h = signal("s_h")
        s_s_hst = signal("s_hst")
        s_s_rs = signal("s_rs")
        s_s_ss = signal("s_ss")
        s_s_st = signal("s_st")
        s_s_tr = signal("s_tr")
        s_s_x = signal("s_x")
        s_s_y = signal("s_y")
        s_s_ya = signal("s_ya")
        s_s_yn = signal("s_yn")
        s_setup = signal("setup")
        s_so_tr = signal("so_tr")
        s_st = signal("st")
        s_st_mm = signal("st_mm")
        s_t_upd = signal("t_upd")
        s_ti_0 = signal("ti_0")
        s_ti_ev = signal("ti_ev")
        s_ti_tr = signal("ti_tr")
        s_tt_upd = signal("tt_upd")
        s_tx_mm = signal("tx_mm")
        s_v_ev = signal("v_ev")
        s_v_setup = signal("v_setup")
        s_v_tr = signal("v_tr")
        s_vn = signal("vn")
        s_vn_mm = signal("vn_mm")
        s_w_ev = signal("w_ev")
        s_w_hi = signal("w_hi")
        s_w_lo = signal("w_lo")
        s_w_mm = signal("w_mm")
        s_wsm_hi = signal("wsm_hi")
        s_wsm_lo = signal("wsm_lo")
        s_x_in = signal("x_in")
        s_x_tr = signal("x_tr")
        s_x_turned = signal("x_turned")
        s_y_out = signal("y_out")
        s_y_ready = signal("y_ready")
        s_y_tr = signal("y_tr")
        s_z_ev = signal("z_ev")
        s_z_tr = signal("z_tr")
        s_zg_ev = signal("zg_ev")
        s_zg_tr = signal("zg_tr")
        s_raw_in = [signal("raw_in0"), signal("raw_in1")]
        base = (nc.sbuf_base + 31) // 32 * 32
        total = (nc.sbuf_usable_end - base) // 4
        cur = [0]

        def at(name, off, shape, dt=F32):
            return nc.alloc_sbuf_tensor_at(name, [P] + list(shape), dt, offset=base + 4 * off)

        def new(name, shape, dt=F32):
            n = int(np.prod(shape))
            words = n if dt != BF16 else (n + 1) // 2
            words = (words + 7) // 8 * 8
            t = at(name, cur[0], shape, dt)
            cur[0] += words
            return t

        xT = new("xT", [KT, SEQ])
        h_hi = new("h_hi", [KT, SEQ], F32R)
        h_lo = new("h_lo", [KT, SEQ], F32R)
        memn = new("memn", [KT, MEM])
        raw = new("raw", [2, 2 * WD])
        w_hi = [new(f"w_hi{i}", [FH, P], F32R) for i in range(2)]
        w_lo = [new(f"w_lo{i}", [FH, P], F32R) for i in range(2)]
        con = new("con", [NCON])
        idb, negq, negd = (new(n, [P], BF16) for n in ("idb", "negq", "negd"))
        prm = new("prm", [NPRM])
        wsm = new("wsm", [KT, 12])
        wsm_hi = new("wsm_hi", [KT, 12], F32R)
        wsm_lo = new("wsm_lo", [KT, 12], F32R)
        eps, seed = new("eps", [2]), new("seed", [sum(START.values())])
        htmp = new("htmp", [2, SEQ])
        sq = new("sq", [2, SEQ])
        rs = new("rs", [2, SEQ])
        lp, lsum, lexp, nlam = new("lp", [2, 64]), new("lsum", [2]), new("lexp", [2]), new("nlam", [2])
        ag, sg1 = new("ag", [8]), new("sg1", [1])
        mx, sm, rr = new("mx", [16, 2]), new("sm", [16, 2]), new("rr", [16, 2])
        gv, gb, g1, sp, ga = (new(n, [NC, w]) for n, w in (("gv", 8), ("gb", 4), ("g1", 8), ("sp", 8), ("ga", 8)))
        beta = new("beta", [NC, 4])
        cums, ex = new("cums", [2, NC, 8]), new("ex", [2, NC, 8])
        ncum, edk = new("ncum", [NC, 8]), new("edk", [NC, 8])
        ss8, ss16, ss32 = new("ss8", [8]), new("ss16", [16]), new("ss32", [NC, 8])
        A0 = cur[0]
        assert A0 + 21248 <= total, (A0, total)
        projT = at("projT", A0, [8, SEQ])
        vT = at("vT", A0 + 4096, [4, SEQ])
        zT = at("zT", A0 + 4096, [4, SEQ])
        convT = at("convT", A0 + 6144, [6, SEQ])
        convG = at("convG", A0 + 9216, [6, SEQ])
        cin = at("cin", A0 + 12288, [2, SEQ])
        vtok = at("vtok", A0 + 13312, [NC, DA_H, DA_V])
        prob = at("prob", A0 + 15360, [2, 2, SEQ])
        wgt = at("wgt", A0 + 17408, [2, SEQ])
        wgtT = at("wgtT", A0 + 18432, [2, SEQ])
        btok = at("btok", A0 + 2048, [NC, 2, P])
        ysq = at("ysq", A0 + 3072, [NC, 256])
        xd = at("xd", A0 + 12288, [NC, S_H, S_D])
        xdd = at("xdd", A0 + 13312, [NC, S_H, S_D])
        xskip = at("xskip", A0 + 14336, [NC, S_H, S_D])
        dec = at("dec", A0 + 15360, [2, 4, P])
        scoT = at("scoT", A0 + 16384, [2, 4, P])
        hst = at("hst", A0 + 17408, [2, S_H, S_D])
        ysd = at("ysd", A0 + 17920, [NC, S_H, S_D])
        ytmp = at("ytmp", A0 + 18944, [S_H, S_D])
        zst = at("zst", A0 + 19200, [NC, 256])
        tr3 = at("tr3", A0, [3, 2, SEQ])
        m1 = at("m1", A0, [NC, G_H, P])
        decG = at("decG", A0 + 3072, [2, 4, P])
        lvlA = at("lvlA", A0 + 3072, [2, 4, P])
        zgt = at("zgt", A0 + 4096, [NC, 256])
        attT = at("attT", A0 + 6144, [NC, G_H, P])
        tri_i = at("tri_i", A0 + 8192, [NC, G_H, P])
        tri_t = at("tri_t", A0 + 10240, [NC, G_H, P])
        qktok = at("qktok", A0 + 12288, [NC, 2, G_H, G_D])
        wTn = at("wTn", A0 + 12288, [2, SEQ])
        otok = at("otok", A0 + 13312, [NC, G_H, G_D])
        gvtok = at("gvtok", A0 + 14336, [NC, G_H, G_D])
        kE = at("kE", A0 + 15360, [NC, G_H, G_D])
        osq = at("osq", A0 + 15360, [NC, 256])
        kgt = at("kgt", A0 + 16384, [NC, G_H, G_D])
        qE = at("qE", A0 + 17408, [NC, G_H, G_D])
        gsq = at("gsq", A0 + 18432, [NC, 2, G_H, G_D])
        aT = at("aT", A0 + 18432, [NC, G_H, P])
        stS = at("stS", A0 + 20480, [2, 2, G_D])
        vnew = at("vnew", A0 + 20736, [2, G_H, G_D])
        qcT = at("qcT", A0, [KT, SEQ])
        kvT = at("kvT", A0 + 4096, [16, MEM])
        vmt = at("vmt", A0 + 8192, [2, D_MODEL])
        pT = at("pT", A0 + 10240, [2, 2, SEQ])
        pc = at("pc", A0 + 12288, [2, 2, MEM])
        f_hi = at("f_hi", A0, [FH, SEQ], F32R)
        f_lo = at("f_lo", A0 + 5632, [FH, SEQ], F32R)
        sgate = at("sgate", A0 + 11264, [SEQ])
        h2 = at("h2", A0 + 11776, [SEQ])
        xtok = at("xtok", A0, [NC, D_MODEL])
        mtok = at("mtok", A0 + 4096, [2, D_MODEL])
        mjunk = at("mjunk", A0 + 6144, [2, D_MODEL])

        bank = [ctx.enter_context(nc.psum_tensor(f"bank{i}", [P, 512], F32)) for i in range(4)]
        hi_banks = ctx.enter_context(nc.psum_tensor("hi_banks", [P, 4, 512], F32))
        bk = [b[:] for b in bank] + [hi_banks[:, i, :] for i in range(4)]

        def col(name, i=0, n=1):
            a = PC[name][0] + i
            return prm[:, a:a + n]

        def cst(name):
            return con[:, CC[name][0]:CC[name][1]]

        def lev(i):
            a = CC["lev"][0] + i * P
            return con[:, a:a + P]

        def bcl(ap, n):
            return ap.unsqueeze(len(ap.shape)).to_broadcast(list(ap.shape) + [n])

        def bcm(ap, n):
            return ap.unsqueeze(1).to_broadcast([ap.shape[0], n] + list(ap.shape[1:]))

        def halves(tile, v, side):
            s = 2 ** (v + 1)
            return tile.rearrange("p h (k a s) -> p h k a s", a=2, s=s)[:, :, :, side, :]

        def joined(c, v, side):
            s = 2 ** (v + 1)
            return bk[4 + c][:, side * 256:(side + 1) * 256].rearrange("p (h k s) -> p h k s", h=G_H, s=s)

        block = ctx.enter_context(nc.Block())

        @block.sync
        def _(sp_):
            sp_.dma_start(con[:], con_d).then_inc(s_const_in.sem, 16)
            sp_.dma_start(xtok[:], x_d.rearrange("(c p) d -> p c d", p=P)).then_inc(s_x_in.sem, 16)
            sp_.dma_start(mtok[:], mem_d.rearrange("(c p) d -> p c d", p=P)).then_inc(s_mem_in.sem, 16)

            with sp_.Fori(0, DEPTH) as l:

                def load(p, slot, src, width):
                    sp_.wait_ge(s_w_lo.sem, s_w_lo.at(l, 2 * p - 2))
                    sp_.dma_start(raw[:, slot, 0:2 * width], src.rearrange("a p n -> p (a n)")).then_inc(s_raw_in[slot].up(16), 16)

                def run(p0, n, src_d, per, q0, width):
                    trips[0] = n // 2
                    with sp_.Fori(0, n // 2) as i:
                        for j in range(2):
                            load(p0 + 2 * i + j, (p0 + j) % 2,
                                 src_d[bass.ds(l * per + 2 * i + (q0 + j), 1), :, :], width)
                    trips[0] = 1
                    if n % 2:
                        load(p0 + n - 1, (p0 + n - 1) % 2, src_d[bass.ds(l * per + (q0 + n - 1), 1), :, :], width)

                p = qa = B_FF // 2
                run(0, p, wa_d, PAIRS_A, 0, WA)
                for half in range(2):
                    run(p, N_GU // 2, wa_d, PAIRS_A, qa, WA)
                    p, qa = p + N_GU // 2, qa + N_GU // 2
                    run(p, N_DN // 2, wd_d, PAIRS_D, half * N_DN // 2, WD)
                    p += N_DN // 2
            for c in range(NC):
                sp_.wait_ge(s_y_ready.sem, 2 * c + 2)
                sp_.dma_start(out_d.rearrange("(c p) d -> c p d", p=P)[c], xtok[:, c, :]).then_inc(s_y_out.sem, 16)
            sp_.wait_ge(s_y_out.sem, 16 * NC)

        @block.gpsimd
        def _(pool):
            with pool.Fori(0, DEPTH) as l:
                pool.wait_ge(s_evac_d.sem, s_evac_d.at(l, 0))
                pool.dma_start(prm[:], prm_d[bass.ds(l, 1), :, :].rearrange("a p n -> p (a n)")).then_inc(s_prm_in.up(16), 16)
                pool.dma_start(wsm[:].rearrange("p k n -> p (k n)"),
                                     wsm_d[bass.ds(l, 1), :, :].rearrange("a p n -> p (a n)")).then_inc(s_prm_in.up(16), 16)
                pool.wait_ge(s_gd_at.sem, s_gd_at.at(l, NC))
                for n in range(NJ):
                    v, c = n // NC, n % NC
                    if n >= 2:
                        pool.wait_ge(s_m1_mm.sem, s_m1_mm.at(l, n - 1))
                    pool.tensor_tensor(lvlA[:, c % 2], aT[:, c], bcm(lev(v + 1), G_H), ALU.mult).then_inc(s_lvl.up(), 1)

        def pair_loop(eng, p0, n, body):
            body(0, p0 % 2, p0 // 2 + 1, True)
            rounds = (n - 1) // 2
            if rounds:
                trips[0] = rounds
                with eng.Fori(0, rounds) as i:
                    for j in (1, 2):
                        body(2 * i + j, (p0 + j) % 2, (p0 + j) // 2 + 1 + i, False)
                trips[0] = 1
            if (n - 1) % 2:
                body(n - 1, (p0 + n - 1) % 2, (p0 + n - 1) // 2 + 1, False)

        @block.scalar
        def _(act):
            def link(l, ins):
                ins.then_inc(s_act_step.up(), 1)
                act.wait_ge(s_act_step.sem, s_act_step.at(l, s_act_step.n))

            act.preload_act_table_set(LN_EXP)
            act.wait_ge(s_mem_in.sem, 16)
            act.wait_ge(s_setup.sem, 1)
            for c in range(2):
                act.activation(mjunk[:, c, :], mtok[:, c, :], ACT.Square,
                               accum_out=ss8[:, c:c + 1]).then_inc(s_mem_sq.sem, 1)
            act.wait_ge(s_mem_sq.sem, 2)
            act.activation(ss8[:, 2:4], ss8[:, 0:2], ACT.Ln, bias=eps[:, 0:1], scale=1.0 / D_MODEL
                           ).then_inc(s_mem_sq.sem, 1)
            act.wait_ge(s_mem_sq.sem, 3)
            act.activation(ss8[:, 4:6], ss8[:, 2:4], ACT.Exp, scale=-0.5).then_inc(s_mem_rs.sem, 1)

            act.wait_ge(s_x_turned.sem, 8)

            with act.Fori(0, DEPTH) as l:

                def rsqrt(out, in_, scale, e, done):
                    link(l, act.activation(out, in_, ACT.Ln, bias=eps[0:in_.shape[0], e:e + 1], scale=scale))
                    act.activation(out, out, ACT.Exp, scale=-0.5).then_inc(done.up(), 1)

                def split_hi(n, w=SEQ, src=None, free=None):
                    if free is not None:
                        act.wait_ge(s_blk_done.sem, s_blk_done.at(l, free))
                    if src is None:
                        act.wait_ge(s_h_f32.sem, s_h_f32.at(l, n + 1 - (KT if n >= H_FF else 0)))
                        src = htmp[:, n % 2, 0:w]
                    act.activation(h_hi[:, n % KT, 0:w], src, ACT.Copy).then_inc(s_h_hi.up(), 1)

                def weights_hi(b, slot, loads):
                    act.wait_ge(s_blk_done.sem, s_blk_done.at(l, b - 1))
                    if b % 2 == 0:
                        act.wait_ge(s_raw_in[slot].sem, s_raw_in[slot].at(l, 16 * loads))
                    act.activation(w_hi[b % 2][:, 0:KT, :].rearrange("p k n -> p (k n)"),
                                   raw[:, slot, (b % 2) * WA:(b % 2 + 1) * WA], ACT.Copy).then_inc(s_w_hi.up(), 1)

                def dense(b0, n, K, evac):
                    width = K * P

                    def body(q, slot, loads, first):
                        for j in range(2):
                            act.wait_ge(s_blk_done.sem, s_blk_done.at(l, 2 * q + (b0 + j - 1)))
                            if j == 0:
                                act.wait_ge(s_raw_in[slot].sem, s_raw_in[slot].at(l, 16 * loads))
                            act.activation(w_hi[j][:, 0:K, :].rearrange("p k n -> p (k n)"), raw[:, slot, j * width:(j + 1) * width], ACT.Copy).then_inc(s_w_hi.up(), 1)
                            if not first and evac is not None:
                                evac(2 * q + (j - 2))
                    pair_loop(act, b0 // 2, n // 2, body)
                    if evac is not None:
                        for o in (n - 2, n - 1):
                            evac(o)

                def copy_out(b0, dst, w):
                    def evac(o):
                        act.wait_ge(s_blk_done.sem, s_blk_done.at(l, o + (b0 + 1)))
                        act.activation(dst[:, bass.ds(o, 1), 0:w].rearrange("p a n -> p (a n)"), bk[o_parity(o)][:, 0:w], ACT.Copy).then_inc(s_evac_a.up(), 1)
                    return evac

                par = [0]

                def o_parity(o):
                    par[0] ^= 1
                    return par[0] ^ 1

                def norm(idx, ready):
                    for k in range(KT):
                        n = idx * KT + k
                        ready(k)
                        if n >= 2:
                            act.wait_ge(s_nrm_mm.sem, s_nrm_mm.at(l, n - 1))
                        act.activation(sq[:, k % 2, :], xT[:, k, :], ACT.Square).then_inc(s_nrm_sq.up(), 1)
                    act.wait_ge(s_nrm_mm.sem, s_nrm_mm.at(l, (idx + 1) * KT))
                    rsqrt(rs[:, 0, :], bk[2], 1.0 / D_MODEL, 0, s_nrm_rs)

                act.preload_act_table_set(LN_EXP)
                act.wait_ge(s_prm_in.sem, s_prm_in.at(l, 32))
                act.wait_ge(s_lam_sum.sem, s_lam_sum.at(l, 1))
                act.activation(lexp[:], lsum[:], ACT.Exp).then_inc(s_lam_exp.up(), 1)
                act.activation(ag[:], col("alog", 0, 8), ACT.Exp).then_inc(s_lam_exp.up(), 1)
                act.activation(wsm_hi[:].rearrange("p k n -> p (k n)"), wsm[:].rearrange("p k n -> p (k n)"), ACT.Copy).then_inc(s_wsm_hi.up(), 1)

                norm(0, lambda k: None if k else act.wait_ge(s_evac_d.sem, s_evac_d.at(l, 0)))
                for k in range(KT):
                    split_hi(H_IN + k, free=None if k else 0)
                def qk_out(o):
                    act.wait_ge(s_blk_done.sem, s_blk_done.at(l, o + 1))
                    j = o_parity(o)
                    act.activation(projT[:, bass.ds(o, 1), :].rearrange("p a n -> p (a n)"), bk[j],
                                   ACT.Copy).then_inc(s_evac_a.up(), 1)
                    act.wait_ge(s_qk_ss.sem, s_qk_ss.at(l, o - 1))
                    act.activation(sq[:, j, :], bk[j], ACT.Square).then_inc(s_qk_sq.up(), 1)
                    act.wait_ge(s_qk_ss.sem, s_qk_ss.at(l, o + 1))
                    act.wait_ge(s_qk_n.sem, s_qk_n.at(l, o - 1))
                    rsqrt(rs[:, j, :], bk[2 + j], 1.0 / DA_D, 0, s_qk_rs)

                dense(B_IN, N_QK, KT, qk_out)

                def in_out(b):
                    act.wait_ge(s_blk_done.sem, s_blk_done.at(l, b + 1))
                    t = b - N_QK
                    if t < N_V:
                        dst = vT[:, t, :]
                    elif t < N_V + N_CONV:
                        dst = cin[:, t % 2, :]
                        if t - N_V >= 2:
                            act.wait_ge(s_conv.sem, s_conv.at(l, t - N_V - 1))
                    else:
                        if t == N_V + N_CONV:
                            act.wait_ge(s_v_tr.sem, s_v_tr.at(l, NC))
                        dst = zT[:, t - N_V - N_CONV, :]
                    act.activation(dst, bk[b % 2], ACT.Copy).then_inc(s_evac_a.up(), 1)

                def v_out(c):
                    act.wait_ge(s_v_tr.sem, s_v_tr.at(l, c + 1))
                    act.activation(vtok[:, c].rearrange("p h e -> p (h e)"), bk[2], ACT.Copy).then_inc(s_v_ev.up(), 1)

                def da_exp(n):
                    nk = (n % NC + 1) * P
                    act.wait_ge(s_da_nm.sem, s_da_nm.at(l, n + 1))
                    if n >= 2:
                        act.wait_ge(s_da_w.sem, s_da_w.at(l, n - 1))
                    for c in range(2):
                        act.activation(prob[:, n % 2, c, 0:nk], bk[4 + 2 * (n % 2) + c][:, 0:nk], ACT.Exp,
                                       bias=mx[:, n, c:c + 1], scale=DA_D ** -0.5,
                                       accum_out=sm[:, n, c:c + 1]).then_inc(s_da_p.up(), 1)

                def da_turned(n):
                    nk = (n % NC + 1) * P
                    act.wait_ge(s_da_t.sem, s_da_t.at(l, n + 1))
                    if n >= 2:
                        act.wait_ge(s_da_pv.sem, s_da_pv.at(l, n - 1))
                    act.activation(wgtT[:, n % 2, 0:nk], bk[2][:, 0:nk], ACT.Copy).then_inc(s_da_wt.up(), 1)

                def da_out(h):
                    act.wait_ge(s_da_pv.sem, s_da_pv.at(l, NC * (h + 1)))
                    act.activation(projT[:, h, :], bk[3], ACT.Copy).then_inc(s_da_o.up(), 1)

                for b in range(N_QK, N_QK + N_V):
                    weights_hi(b, (b // 2) % 2, b // 4 + 1)
                    if b - 2 >= N_QK:
                        in_out(b - 2)
                for s in range(ND + 3):
                    b = N_QK + N_V + s
                    if b < N_IN:
                        weights_hi(b, (b // 2) % 2, b // 4 + 1)
                    if b - 2 < N_IN:
                        in_out(b - 2)
                    if 0 < s <= NC:
                        v_out(s - 1)
                    if 0 < s <= ND:
                        da_exp(s - 1)
                    if 0 <= s - 2 < ND:
                        da_turned(s - 2)
                    if s >= 3 and (s - 3) % NC == NC - 1:
                        da_out((s - 3) // NC)
                act.wait_ge(s_da_pv.sem, s_da_pv.at(l, ND))
                act.wait_ge(s_da_o.sem, s_da_o.at(l, DA_H))
                for h in range(2):
                    act.activation(sq[:, h % 2, :], projT[:, h, :], ACT.Square).then_inc(s_on_sq.up(), 1)
                for h in range(DA_H):
                    act.wait_ge(s_on_ss.sem, s_on_ss.at(l, h + 1))
                    if h >= 2:
                        act.wait_ge(s_h_f32.sem, s_h_f32.at(l, H_MIX + h - 1))
                    rsqrt(rs[:, h % 2, :], bk[2 + h % 2], 1.0 / DA_V, 0, s_on_rs)
                    if h + 2 < DA_H:
                        act.activation(sq[:, h % 2, :], projT[:, h + 2, :], ACT.Square).then_inc(s_on_sq.up(), 1)
                    split_hi(H_MIX + h)

                act.wait_ge(s_g_v.sem, s_g_v.at(l, 2))
                link(l, act.activation(g1[:], gv[:], ACT.Abs))
                link(l, act.activation(g1[:], g1[:], ACT.Exp, scale=-1.0))
                act.activation(g1[:], g1[:], ACT.Ln, bias=1.0).then_inc(s_g_ln.up(), 1)
                act.activation(gb[:], gb[:], ACT.Exp, scale=-1.0).then_inc(s_g_ln.up(), 1)
                act.wait_ge(s_g_dk.sem, s_g_dk.at(l, 1))
                act.activation(ex[:].rearrange("p a c h -> p (a c h)"), cums[:].rearrange("p a c h -> p (a c h)"), ACT.Exp).then_inc(s_g_ex.up(), 1)
                act.activation(edk[:], edk[:], ACT.Exp).then_inc(s_g_edk.up(), 1)

                for t in range(6):
                    act.wait_ge(s_conv.sem, s_conv.at(l, t + 1))
                    act.activation(convT[:, t, :], convT[:, t, :], ACT.Silu).then_inc(s_convs.up(), 1)
                for c in range(NC):
                    act.wait_ge(s_s_tr.sem, s_s_tr.at(l, c + 1))
                    act.activation(btok[:, c].rearrange("p g n -> p (g n)"), bk[4 + c % 2][:, 0:256], ACT.Copy).then_inc(s_s_ev.up(), 1)
                for i in range(2):
                    act.wait_ge(s_z_tr.sem, s_z_tr.at(l, i + 1))
                    act.activation(zst[:, 2 * i:2 * i + 2].rearrange("p c n -> p (c n)"), bk[2 + i], ACT.Silu).then_inc(s_z_ev.up(), 1)
                act.preload_act_table_set(LN_EXP)
                for c in range(NC):
                    act.wait_ge(s_s_d.sem, s_s_d.at(l, c + 1))
                    if c >= 2:
                        act.wait_ge(s_s_st.sem, s_s_st.at(l, c - 1))
                    for h in range(S_H):
                        act.activation(dec[:, c % 2, h, :], bk[4 + c % 2][:, h * P:(h + 1) * P], ACT.Exp, bias=ncum[:, c, h:h + 1]).then_inc(s_s_dec.up(), 1)
                act.wait_ge(s_s_ss.sem, s_s_ss.at(l, 1))
                rsqrt(ss8[:], ss8[:], 1.0 / P, 0, s_s_rs)
                for f in range(2):
                    split_hi(H_MIX + 4 + f)

                for t in range(6):
                    act.wait_ge(s_conv.sem, s_conv.at(l, 7 + t))
                    act.activation(convG[:, t, :], convG[:, t, :], ACT.Silu).then_inc(s_convs.up(), 1)
                for c in range(NC):
                    act.wait_ge(s_gt_tr.sem, s_gt_tr.at(l, c + 1))
                    act.activation(qktok[:, c].rearrange("p a h d -> p (a h d)"), bk[2 + c % 2], ACT.Copy).then_inc(s_gt_ev.up(), 1)
                    act.activation(gvtok[:, c].rearrange("p h d -> p (h d)"), bk[4 + c % 2][:, 0:256], ACT.Copy).then_inc(s_gt_ev.up(), 1)
                act.preload_act_table_set(LN_EXP)
                act.wait_ge(s_gn_ss.sem, s_gn_ss.at(l, 1))
                rsqrt(ss32[:], ss32[:], 1.0, 0, s_gn_rs)
                for i in range(6):
                    act.wait_ge(s_g3_tr.sem, s_g3_tr.at(l, i + 1))
                    act.activation(tr3[:, i // 2, i % 2, :], bk[2 + i % 2], ACT.Copy).then_inc(s_g3_ev.up(), 1)
                for c in range(NC):
                    act.wait_ge(s_gd_d.sem, s_gd_d.at(l, c + 1))
                    if c >= 2:
                        act.wait_ge(s_gd_at.sem, s_gd_at.at(l, c - 1))
                    for h in range(G_H):
                        act.activation(decG[:, c % 2, h, :], bk[4 + c % 2][:, h * P:(h + 1) * P], ACT.Exp, bias=ncum[:, c, 4 + h:5 + h]).then_inc(s_gd_dec.up(), 1)
                for c in range(NC):
                    act.wait_ge(s_ti_tr.sem, s_ti_tr.at(l, c + 1))
                    act.activation(tri_i[:, c].rearrange("p h n -> p (h n)"), bk[2 + c % 2], ACT.Copy).then_inc(s_ti_ev.up(), 1)
                for n in range(NJ):
                    act.wait_ge(s_m1_mm.sem, s_m1_mm.at(l, n + 1))
                    if n >= NC:
                        act.wait_ge(s_tx_mm.sem, s_tx_mm.at(l, n - NC + 1))
                    act.activation(m1[:, n % NC].rearrange("p h n -> p (h n)"), bk[2 + n % 2], ACT.Copy).then_inc(s_m1_ev.up(), 1)
                for p_ in range(2):
                    act.wait_ge(s_w_mm.sem, s_w_mm.at(l, p_ + 1))
                    act.activation(wTn[:, p_, :], bk[2 + p_], ACT.Copy, scale=-1.0).then_inc(s_w_ev.up(), 1)
                for c in range(NC):
                    act.wait_ge(s_o_mm.sem, s_o_mm.at(l, c + 1))
                    act.activation(otok[:, c].rearrange("p (a r) d -> p r a d", r=2), hi_banks[:, 2:4, 0:P].rearrange("p r (a d) -> p r a d", a=2), ACT.Copy).then_inc(s_o_ev.up(), 1)
                for i in range(2):
                    act.wait_ge(s_zg_tr.sem, s_zg_tr.at(l, i + 1))
                    act.activation(zgt[:, 2 * i:2 * i + 2].rearrange("p c n -> p (c n)"), bk[2 + i], ACT.Silu).then_inc(s_zg_ev.up(), 1)
                act.preload_act_table_set(LN_EXP)
                act.wait_ge(s_go_ss.sem, s_go_ss.at(l, 1))
                rsqrt(ss16[:], ss16[:], 1.0 / G_D, 0, s_go_rs)
                for f in range(2):
                    split_hi(H_MIX + 6 + f)

                dense(B_OUT, N_OUT, KT, None)
                for k in range(KT):
                    split_hi(H_MEM + k, MEM, free=B_OUT + N_OUT)
                dense(B_KV, N_KV, KT, copy_out(B_KV, kvT, MEM))
                norm(1, lambda k: act.wait_ge(s_evac_d.sem, s_evac_d.at(l, ED_OUT + k + 1)))
                for k in range(KT):
                    split_hi(H_X + k, free=B_KV + N_KV)
                dense(B_CQ, N_CQ, KT, copy_out(B_CQ, qcT, SEQ))
                act.wait_ge(s_evac_a.sem, s_evac_a.at(l, EA_CQ + N_CQ))
                for n in range(16):
                    if n >= 2:
                        act.wait_ge(s_c_ssm.sem, s_c_ssm.at(l, n - 1))
                    w = SEQ if n < 8 else MEM
                    act.activation(sq[:, n % 2, 0:w], qcT[:, n, :] if n < 8 else kvT[:, n - 8, :], ACT.Square).then_inc(s_c_sq.up(), 1)
                    if n % 2 == 1:
                        m = n // 2
                        act.wait_ge(s_c_ssm.sem, s_c_ssm.at(l, n + 1))
                        if m >= 2:
                            act.wait_ge(s_c_n.sem, s_c_n.at(l, 2 * m - 2))
                        rsqrt(rs[:, m % 2, 0:w], bk[2 + m % 2][:, 0:w], 1.0 / X_D, 0, s_c_rs)
                for i in range(4):
                    act.wait_ge(s_cv_tr.sem, s_cv_tr.at(l, i + 1))
                    act.activation(vmt[:, i // 2, (i % 2) * 512:(i % 2 + 1) * 512], bk[2 + i % 2], ACT.Copy).then_inc(s_cv_ev.up(), 1)

                def c_exp(n):
                    act.wait_ge(s_c_nm.sem, s_c_nm.at(l, n + 1))
                    if n >= 2:
                        act.wait_ge(s_c_t.sem, s_c_t.at(l, n - 1))
                    for i in range(2):
                        act.activation(pc[:, n % 2, i, :], bk[4 + n % 2][:, i * MEM:(i + 1) * MEM], ACT.Exp, bias=mx[:, n, i:i + 1], scale=X_D ** -0.5, accum_out=sm[:, n, i:i + 1]).then_inc(s_c_p.up(), 1)

                def c_turned(n):
                    h, qp = n // 2, n % 2
                    act.wait_ge(s_c_t.sem, s_c_t.at(l, n + 1))
                    if h >= 2 and qp == 0:
                        act.wait_ge(s_c_pv.sem, s_c_pv.at(l, 2 * (h - 1)))
                    act.activation(pT[:, h % 2, :, qp * 256:(qp + 1) * 256], bk[6 + n % 2].rearrange("p (m q) -> p m q", m=2), ACT.Copy).then_inc(s_c_pt.up(), 1)
                    if qp == 0 and h > 0:
                        c_out(h - 1)

                def c_out(h):
                    for e in range(2):
                        act.wait_ge(s_c_pv.sem, s_c_pv.at(l, 2 * h + e + 1))
                        split_hi(H_CA + 2 * h + e, src=bk[e], free=B_CQ + N_CQ)

                for n in range(8):
                    c_exp(n)
                    if n >= 1:
                        c_turned(n - 1)
                c_turned(7)
                c_out(3)
                dense(B_CO, N_CO, KT, None)
                norm(2, lambda k: act.wait_ge(s_evac_d.sem, s_evac_d.at(l, ED_CO + k + 1)))
                for k in range(KT):
                    split_hi(H_FF + k, free=B_CO + N_CO)
                act.preload_act_table(ACT.Silu)
                b = B_FF
                for half in range(2):

                    f0 = half * FH

                    def body(q, slot, loads, first, b=b, f0=f0):
                        for j in range(2):
                            act.wait_ge(s_blk_done.sem, s_blk_done.at(l, 2 * q + (b + j - 1)))
                            if j == 0:
                                act.wait_ge(s_raw_in[slot].sem, s_raw_in[slot].at(l, 16 * loads))
                            act.activation(w_hi[j][:, 0:KT, :].rearrange("p k n -> p (k n)"), raw[:, slot, j * WA:(j + 1) * WA], ACT.Copy).then_inc(s_w_hi.up(), 1)
                            if not first:
                                ffn_out(q - 1, j, b, f0)

                    def ffn_out(i, j, b, f0):
                        if j == 0:
                            act.wait_ge(s_blk_done.sem, s_blk_done.at(l, 2 * i + (b + 1)))
                            act.wait_ge(s_f_h2.sem, s_f_h2.at(l, i + f0))
                            act.activation(sgate[:], bk[0], ACT.Silu).then_inc(s_f_sg.up(), 1)
                        else:
                            act.wait_ge(s_f_h2.sem, s_f_h2.at(l, i + (f0 + 1)))
                            act.activation(f_hi[:, bass.ds(i, 1), :].rearrange("p a n -> p (a n)"), h2[:], ACT.Copy).then_inc(s_f_hi.up(), 1)
                    pair_loop(act, b // 2, FH, body)
                    for j in range(2):
                        ffn_out(FH - 1, j, b, f0)
                    b += N_GU
                    dense(b, N_DN, FH, None)
                    b += N_DN

            for c in range(NC):
                for i in range(2):
                    n = 2 * c + i
                    act.wait_ge(s_y_tr.sem, n + 1)
                    act.activation(xtok[:, c, i * 512:(i + 1) * 512], bk[2 + n % 2], ACT.Copy
                                   ).then_inc(s_y_ready.sem, 1)

        @block.vector
        def _(dve):
            def tt(out, a, b, op):
                return dve.tensor_tensor(out, a, b, op)

            def stt(out, a, s, b, op0, op1):
                return dve.scalar_tensor_tensor(out=out, in0=a, scalar=s, in1=b, op0=op0, op1=op1)

            MUL, ADD, SUB = ALU.mult, ALU.add, ALU.subtract

            def first(ins):
                ins.then_inc(s_v_setup.sem, 1)
                setup_n[0] += 1
                dve.wait_ge(s_v_setup.sem, setup_n[0])
            setup_n = [0]
            first(dve.memset(eps[:, 0:1], EPS))
            dve.memset(eps[:, 1:2], 0.0).then_inc(s_setup.sem, 1)
            for i, name in enumerate([n for n in START for _ in range(START[n])]):
                dve.memset(seed[:, i:i + 1], 0.0).then_inc(signals[name].sem, 1)
            dve.wait_ge(s_const_in.sem, 16)
            first(dve.tensor_copy(idb[:], cst("idn")))
            first(dve.tensor_copy(negq[:], cst("negq")))
            dve.tensor_copy(negd[:], cst("negd")).then_inc(s_c_bf.sem, 1)
            for n in range(8):
                dve.wait_ge(s_x_tr.sem, n + 1)
                c, i = n // 2, n % 2
                dve.tensor_copy(xT[:, 4 * i:4 * i + 4, c * P:(c + 1) * P],
                                bk[2 + n % 2].rearrange("p (k n) -> p k n", k=4)).then_inc(s_x_turned.sem, 1)
            dve.wait_ge(s_mem_rs.sem, 1)
            for c in range(2):
                dve.tensor_scalar(mjunk[:, c, :], mtok[:, c, :], ss8[:, 4 + c:5 + c], None, MUL
                                  ).then_inc(s_mem_n.sem, 1)
            for n in range(4):
                dve.wait_ge(s_m_tr.sem, n + 1)
                c, i = n // 2, n % 2
                dve.tensor_copy(memn[:, 4 * i:4 * i + 4, c * P:(c + 1) * P],
                                bk[4 + n % 2].rearrange("p (k n) -> p k n", k=4)).then_inc(s_m_ev.sem, 1)
            dve.wait_ge(s_m_ev.sem, 4)
            dve.wait_ge(s_x_turned.sem, 8)

            with dve.Fori(0, DEPTH) as l:
                def own(ins, s):
                    ins.then_inc(s.up(), 1)
                    dve.wait_ge(s.sem, s.at(l, s.n))

                def link(ins):
                    own(ins, s_dve_step)

                def split_lo(n, w=SEQ, src=None):
                    dve.wait_ge(s_h_hi.sem, s_h_hi.at(l, n + 1))
                    tt(h_lo[:, n % KT, 0:w], htmp[:, n % 2, 0:w] if src is None else src,
                             h_hi[:, n % KT, 0:w].bitcast(F32), SUB).then_inc(s_h_lo.up(), 1)

                def free_htmp(n):
                    if n >= 2:
                        dve.wait_ge(s_h_lo.sem, s_h_lo.at(l, n - 1))
                    else:
                        dve.wait_ge(s_h_lo.sem, s_h_lo.at(l, 0))

                def scaled(first_n, count, make):
                    for k in range(count):
                        free_htmp(first_n + k)
                        make(k, htmp[:, (first_n + k) % 2, :]).then_inc(s_h_f32.up(), 1)
                        if k >= 1:
                            split_lo(first_n + k - 1)
                    split_lo(first_n + count - 1)

                def norm_out(idx, first_n, g):
                    dve.wait_ge(s_nrm_rs.sem, s_nrm_rs.at(l, idx + 1))
                    scaled(first_n, KT, lambda k, o: stt(o, xT[:, k, :], col(g, k), rs[:, 0, :], MUL, MUL))

                def weights_lo(b, slot):
                    dve.wait_ge(s_w_hi.sem, s_w_hi.at(l, b + 1))
                    tt(w_lo[b % 2][:, 0:KT, :].rearrange("p k n -> p (k n)"), raw[:, slot, (b % 2) * WA:(b % 2 + 1) * WA],
                       w_hi[b % 2][:, 0:KT, :].rearrange("p k n -> p (k n)").bitcast(F32), SUB).then_inc(s_w_lo.up(), 1)

                def dense(b0, n, K, evac):
                    width = K * P

                    def body(q, slot, loads, first_):
                        for j in range(2):
                            dve.wait_ge(s_w_hi.sem, s_w_hi.at(l, 2 * q + (b0 + j + 1)))
                            tt(w_lo[j][:, 0:K, :].rearrange("p k n -> p (k n)"),
                                     raw[:, slot, j * width:(j + 1) * width],
                                     w_hi[j][:, 0:K, :].rearrange("p k n -> p (k n)").bitcast(F32), SUB).then_inc(s_w_lo.up(), 1)
                            if not first_ and evac is not None:
                                evac(2 * q + (j - 2), j)
                    pair_loop(dve, b0 // 2, n // 2, body)
                    if evac is not None:
                        for j in range(2):
                            evac(n - 2 + j, j)

                def add_out(b0):
                    def evac(o, j):
                        dve.wait_ge(s_blk_done.sem, s_blk_done.at(l, o + (b0 + 1)))
                        dst = xT[:, bass.ds(o, 1), :].rearrange("p a n -> p (a n)")
                        tt(dst, bk[j], dst, ADD).then_inc(s_evac_d.up(), 1)
                    return evac

                dve.wait_ge(s_prm_in.sem, s_prm_in.at(l, 32))
                lv = col("lamv", 0, 256).rearrange("p (a b n) -> p a b n", a=2, b=2)
                link(tt(lp[:], lv[:, :, 0, :], lv[:, :, 1, :], MUL))
                dve.reduce_sum(lsum[:], lp[:], AX.X).then_inc(s_lam_sum.up(), 1)
                link(tt(sg1[:], col("subg"), col("onemin"), MUL))
                dve.wait_ge(s_lam_exp.sem, s_lam_exp.at(l, 1))
                link(tt(nlam[:, 0:1], lexp[:, 1:2], lexp[:, 0:1], SUB))
                link(tt(nlam[:, 1:2], nlam[:, 0:1], col("laminit"), SUB))
                dve.wait_ge(s_wsm_hi.sem, s_wsm_hi.at(l, 1))
                tt(wsm_lo[:].rearrange("p k n -> p (k n)"), wsm[:].rearrange("p k n -> p (k n)"),
                         wsm_hi[:].rearrange("p k n -> p (k n)").bitcast(F32), SUB).then_inc(s_wsm_lo.up(), 1)

                norm_out(0, H_IN, "g_mix")
                def qk_scale(o, j):
                    dve.wait_ge(s_qk_rs.sem, s_qk_rs.at(l, o + 1))
                    t = projT[:, bass.ds(o, 1), :].rearrange("p a n -> p (a n)")
                    stt(t, t, prm[:, bass.ds(o + PC["qkg"][0], 1)], rs[:, j, :], MUL, MUL).then_inc(s_qk_n.up(), 1)

                dense(B_IN, N_QK, KT, qk_scale)

                dve.wait_ge(s_g_ps.sem, s_g_ps.at(l, 1))
                gp = bk[7][:, 0:48].rearrange("p (c n) -> p c n", c=NC)
                tt(gv[:], gp[:, :, 0:8], bcm(col("dtb", 0, 8), NC), ADD).then_inc(s_g_v.up(), 1)
                dve.tensor_copy(gb[:], gp[:, :, 8:12]).then_inc(s_g_v.up(), 1)

                def da_max(n):
                    nk = (n % NC + 1) * P
                    i = n % 2
                    dve.wait_ge(s_da_s.sem, s_da_s.at(l, n + 1))
                    link(dve.reduce_max(rr[:, n, :], hi_banks[:, 2 * i:2 * i + 2, 0:nk], AX.X))
                    dve.tensor_scalar(mx[:, n, :], rr[:, n, :], -(DA_D ** -0.5), None, MUL).then_inc(s_da_nm.up(), 1)

                def da_weigh(n):
                    nk = (n % NC + 1) * P
                    dve.wait_ge(s_da_p.sem, s_da_p.at(l, 2 * n + 2))
                    link(dve.reciprocal(rr[:, n, :], sm[:, n, :]))
                    link(tt(rr[:, n, 1:2], rr[:, n, 1:2], nlam[:, 1:2], MUL))
                    if n >= 2:
                        dve.wait_ge(s_da_t.sem, s_da_t.at(l, n - 1))
                    w = wgt[:, n % 2, 0:nk]
                    link(dve.tensor_scalar(w, prob[:, n % 2, 0, 0:nk], rr[:, n, 0:1], None, MUL))
                    stt(w, prob[:, n % 2, 1, 0:nk], rr[:, n, 1:2], w, MUL, ADD).then_inc(s_da_w.up(), 1)

                def conv(t):
                    src = cin[:, t % 2, :]
                    dst = convT[:, t, :] if t < 6 else convG[:, t - 6, :]
                    dve.wait_ge(s_evac_a.sem, s_evac_a.at(l, N_QK + N_V + t + 1))
                    w = lambda j: col("cw", 4 * t + j)
                    link(dve.tensor_scalar(dst, src, w(3), col("cb", t), MUL, ADD))
                    for j in (1, 2):
                        link(stt(dst[:, j:SEQ], src[:, 0:SEQ - j], w(3 - j), dst[:, j:SEQ], MUL, ADD))
                    stt(dst[:, 3:SEQ], src[:, 0:SEQ - 3], w(0), dst[:, 3:SEQ], MUL, ADD).then_inc(s_conv.up(), 1)

                for b in range(N_QK, N_QK + N_V):
                    weights_lo(b, (b // 2) % 2)
                for s in range(ND + 1):
                    b = N_QK + N_V + s
                    if s:
                        da_max(s - 1)
                    if b < N_IN:
                        weights_lo(b, (b // 2) % 2)
                    if s:
                        da_weigh(s - 1)
                    if 0 <= s - 2 < N_CONV:
                        conv(s - 2)
                for h in range(DA_H):
                    n = H_MIX + h
                    dve.wait_ge(s_on_rs.sem, s_on_rs.at(l, h + 1))
                    free_htmp(n)
                    stt(htmp[:, n % 2, :], projT[:, h, :], sg1[:, 0:1], rs[:, h % 2, :], MUL, MUL).then_inc(s_h_f32.up(), 1)
                    if h >= 1:
                        split_lo(n - 1)
                split_lo(H_MIX + DA_H - 1)

                dve.wait_ge(s_g_ln.sem, s_g_ln.at(l, 2))
                link(stt(sp[:], gv[:], 0.0, g1[:], ALU.max, ADD))
                stt(ga[:], sp[:], -1.0, bcm(ag[:], NC), MUL, MUL).then_inc(s_g_a.up(), 1)
                link(dve.tensor_scalar(gb[:], gb[:], 1.0, None, ADD))
                link(dve.reciprocal(beta[:], gb[:]))
                dve.wait_ge(s_g_cum.sem, s_g_cum.at(l, 1))
                link(dve.tensor_copy(cums[:].rearrange("p a c h -> p (a c h)"), bk[3][:, 64:128]))
                link(dve.tensor_scalar(ncum[:], cums[:, 0], -1.0, None, MUL))
                tt(edk[:], cums[:, 1], cums[:, 0], SUB).then_inc(s_g_dk.up(), 1)

                dve.wait_ge(s_g_edk.sem, s_g_edk.at(l, 1))
                for c in range(NC):
                    dve.wait_ge(s_s_tr.sem, s_s_tr.at(l, c + 1))
                    xp = bk[2 + c % 2][:, 0:256].rearrange("p (h d) -> p h d", h=S_H)
                    link(tt(xd[:, c], xp, bcl(sp[:, c, 0:4], S_D), MUL))
                    tt(xskip[:, c], xp, bcl(col("dsk", 0, 4), S_D), MUL).then_inc(s_s_x.up(), 1)
                    tt(xdd[:, c], xd[:, c], bcl(edk[:, c, 0:4], S_D), MUL).then_inc(s_s_x.up(), 1)

                def s_scores(c):
                    dve.wait_ge(s_s_dec.sem, s_s_dec.at(l, 4 * c + 4))
                    dve.wait_ge(s_s_cb.sem, s_s_cb.at(l, c + 1))
                    if c >= 2:
                        dve.wait_ge(s_s_y.sem, s_s_y.at(l, c - 1))
                    tt(scoT[:, c % 2].rearrange("p (g h) n -> p g h n", g=2),
                             dec[:, c % 2].rearrange("p (g h) n -> p g h n", g=2),
                             bk[6][:, 0:256].rearrange("p (g n) -> p g n", g=2).unsqueeze(2).to_broadcast([P, 2, 2, P]),
                             MUL).then_inc(s_s_st.up(), 1)

                def s_state(c):
                    dve.wait_ge(s_s_h.sem, s_s_h.at(l, c + 1))
                    ph = bk[c % 2][:, 0:256].rearrange("p (h d) -> p h d", h=S_H)
                    if c >= 1:
                        link(tt(hst[:, (c + 1) % 2], hst[:, c % 2], bcl(ex[:, 1, c, 0:4], S_D), MUL))
                        own(tt(hst[:, (c + 1) % 2], hst[:, (c + 1) % 2], ph, ADD), s_s_hst)
                    else:
                        own(dve.tensor_copy(hst[:, 1], ph), s_s_hst)

                def s_out(c):
                    dve.wait_ge(s_s_y.sem, s_s_y.at(l, c + 1))
                    yp = bk[7][:, 0:256].rearrange("p (h d) -> p h d", h=S_H)
                    yo = bk[7][:, 256:512].rearrange("p (h d) -> p h d", h=S_H)
                    if c:
                        link(tt(ytmp[:], yo, bcl(ex[:, 0, c, 0:4], S_D), MUL))
                        link(tt(ytmp[:], ytmp[:], xskip[:, c], ADD))
                        own(tt(ysd[:, c], ytmp[:], yp, ADD), s_s_ya)
                    else:
                        own(tt(ysd[:, c], xskip[:, c], yp, ADD), s_s_ya)

                dve.wait_ge(s_s_x.sem, s_s_x.at(l, 8))
                dve.wait_ge(s_g_ex.sem, s_g_ex.at(l, 1))
                for c in range(NC):
                    s_scores(c)
                    if c < NC - 1:
                        s_state(c)
                    s_out(c)
                dve.wait_ge(s_z_ev.sem, s_z_ev.at(l, 2))
                yf = ysd[:].rearrange("p c h d -> p (c h d)")
                link(tt(yf, yf, zst[:].rearrange("p c n -> p (c n)"), MUL))
                link(tt(ysq[:].rearrange("p c n -> p (c n)"), yf, yf, MUL))
                dve.reduce_sum(ss8[:], ysq[:].rearrange("p c (g n) -> p (c g) n", g=2), AX.X).then_inc(s_s_ss.up(), 1)
                dve.wait_ge(s_s_rs.sem, s_s_rs.at(l, 1))
                y8 = ysd[:].rearrange("p c (g h) d -> p (c g) (h d)", g=2)
                tt(y8, y8, bcl(ss8[:], P), MUL).then_inc(s_s_yn.up(), 1)
                for f in range(2):
                    n = H_MIX + 4 + f
                    dve.wait_ge(s_so_tr.sem, s_so_tr.at(l, f + 1))
                    free_htmp(n)
                    dve.tensor_scalar(htmp[:, n % 2, :], bk[2 + f], col("sng", f), None, MUL).then_inc(s_h_f32.up(), 1)
                for f in range(2):
                    split_lo(H_MIX + 4 + f)

                dve.wait_ge(s_gt_ev.sem, s_gt_ev.at(l, 8))
                flat = lambda a: a.rearrange("p c a h d -> p (c a h d)")
                link(tt(flat(gsq[:]), flat(qktok[:]), flat(qktok[:]), MUL))
                dve.reduce_sum(ss32[:].rearrange("p c n -> p (c n)"),
                                     gsq[:].rearrange("p c a h d -> p (c a h) d"), AX.X).then_inc(s_gn_ss.up(), 1)
                dve.wait_ge(s_gn_rs.sem, s_gn_rs.at(l, 1))
                link(dve.tensor_scalar(ss32[:, :, 0:4], ss32[:, :, 0:4], G_D ** -0.5, None, MUL))
                qk3 = qktok[:].rearrange("p c a h d -> p (c a h) d")
                own(tt(qk3, qk3, bcl(ss32[:].rearrange("p c n -> p (c n)"), G_D), MUL), s_gn_n)
                tt(qE[:], qktok[:, :, 0], bcl(ex[:, 0, :, 4:8], G_D), MUL).then_inc(s_gn_n.up(), 1)
                tt(kE[:], qktok[:, :, 1], bcl(ex[:, 0, :, 4:8], G_D), MUL).then_inc(s_gn_n.up(), 1)
                tt(kgt[:], qktok[:, :, 1], bcl(edk[:, :, 4:8], G_D), MUL).then_inc(s_gn_n.up(), 1)
                for c in range(NC):
                    dve.wait_ge(s_gd_dec.sem, s_gd_dec.at(l, 4 * c + 4))
                    dve.wait_ge(s_gd_kq.sem, s_gd_kq.at(l, c + 1))
                    D4 = decG[:, c % 2]
                    by_row = lambda a: a.rearrange("p (a r) n -> p r a n", r=2)
                    kkqk = hi_banks[:, 2:4, :].rearrange("p r (k a n) -> p k r a n", k=2, a=2)
                    own(tt(by_row(attT[:, c]), by_row(D4), kkqk[:, 1], MUL), s_gd_att)
                    link(tt(D4, D4, bcl(beta[:, c, :], P), MUL))
                    own(tt(by_row(aT[:, c]), by_row(D4), kkqk[:, 0], MUL), s_gd_at)
                for c in range(NC):
                    link(tt(tri_t[:, c], aT[:, c], bcm(lev(0), G_H), MUL))
                    own(tt(tri_t[:, c], bcm(cst("idn"), G_H), tri_t[:, c], SUB), s_ti_0)
                for n in range(NJ):
                    v, c = n // NC, n % NC
                    dve.wait_ge(s_tx_mm.sem, s_tx_mm.at(l, n + 1))
                    if v < NLEV - 2:
                        t = halves(tri_i[:, c], v, 0)
                        tt(t, t, joined(c, v, 0), SUB).then_inc(s_t_upd.up(), 1)
                    t = halves(tri_t[:, c], v, 1)
                    tt(t, t, joined(c, v, 1), SUB).then_inc(s_tt_upd.up(), 1)
                for c in range(NC):
                    dve.wait_ge(s_vn_mm.sem, s_vn_mm.at(l, c + 1))
                    if c >= 2:
                        dve.wait_ge(s_o_mm.sem, s_o_mm.at(l, c - 1))
                        dve.wait_ge(s_st_mm.sem, s_st_mm.at(l, c - 1))
                    tt(vnew[:, c % 2].rearrange("p (a r) d -> p r a d", r=2),
                             hi_banks[:, 0:2, 0:P].rearrange("p r (a d) -> p r a d", a=2),
                             bcl(beta[:, c, :].rearrange("p (a r) -> p r a", r=2), G_D), MUL).then_inc(s_vn.up(), 1)
                    if c < NC - 1:
                        dve.wait_ge(s_st_mm.sem, s_st_mm.at(l, c + 1))
                        new_, old = (c + 1) % 2, c % 2
                        if c == 0:
                            dve.tensor_copy(stS[:, new_].rearrange("p a d -> p (a d)"), bk[0][:, 0:P]).then_inc(s_st.up(), 1)
                        else:
                            for p_ in range(2):
                                for hh in range(2):
                                    r = slice(64 * hh, 64 * hh + 64)
                                    last = stt(stS[r, new_, p_, :], stS[r, old, p_, :],
                                               ex[r, 1, c, 4 + 2 * p_ + hh:5 + 2 * p_ + hh],
                                               bk[c % 2][r, p_ * 64:p_ * 64 + 64], MUL, ADD)
                                    if p_ + hh < 2:
                                        last.then_inc(s_dve_step.up(), 1)
                            last.then_inc(s_st.up(), 1)
                        dve.wait_ge(s_st.sem, s_st.at(l, c + 1))
                        dve.wait_ge(s_dve_step.sem, s_dve_step.at(l, s_dve_step.n))
                dve.wait_ge(s_o_ev.sem, s_o_ev.at(l, NC))
                dve.wait_ge(s_zg_ev.sem, s_zg_ev.at(l, 2))
                of = otok[:].rearrange("p c h d -> p (c h d)")
                link(tt(osq[:].rearrange("p c n -> p (c n)"), of, of, MUL))
                dve.reduce_sum(ss16[:], osq[:].rearrange("p c (h d) -> p (c h) d", h=G_H), AX.X).then_inc(s_go_ss.up(), 1)
                dve.wait_ge(s_go_rs.sem, s_go_rs.at(l, 1))
                link(tt(of, of, zgt[:].rearrange("p c n -> p (c n)"), MUL))
                o16 = otok[:].rearrange("p c h d -> p (c h) d")
                tt(o16, o16, bcl(ss16[:], G_D), MUL).then_inc(s_go_n.up(), 1)
                for f in range(2):
                    n = H_MIX + 6 + f
                    dve.wait_ge(s_go_tr.sem, s_go_tr.at(l, f + 1))
                    free_htmp(n)
                    dve.tensor_scalar(htmp[:, n % 2, :], bk[2 + f], col("gng", f), None, MUL).then_inc(s_h_f32.up(), 1)
                for f in range(2):
                    split_lo(H_MIX + 6 + f)

                dense(B_OUT, N_OUT, KT, add_out(B_OUT))
                for k in range(KT):
                    n = H_MEM + k
                    free_htmp(n)
                    dve.tensor_scalar(htmp[:, n % 2, 0:MEM], memn[:, k, :], col("g_mem", k), None, MUL).then_inc(s_h_f32.up(), 1)
                    if k >= 1:
                        split_lo(n - 1, MEM)
                split_lo(H_MEM + KT - 1, MEM)
                dense(B_KV, N_KV, KT, None)
                norm_out(1, H_X, "g_x")
                dense(B_CQ, N_CQ, KT, None)
                for m in range(8):
                    dve.wait_ge(s_c_rs.sem, s_c_rs.at(l, m + 1))
                    for f in range(2):
                        n = 2 * m + f
                        w = SEQ if n < 8 else MEM
                        t = qcT[:, n, :] if n < 8 else kvT[:, n - 8, :]
                        stt(t, t, col("xqg" if n < 8 else "xkg", f), rs[:, m % 2, 0:w], MUL, MUL).then_inc(s_c_n.up(), 1)

                def c_max(n):
                    dve.wait_ge(s_c_s.sem, s_c_s.at(l, n + 1))
                    link(dve.reduce_max(rr[:, n, :], bk[4 + n % 2].rearrange("p (i m) -> p i m", i=2), AX.X))
                    dve.tensor_scalar(mx[:, n, :], rr[:, n, :], -(X_D ** -0.5), None, MUL).then_inc(s_c_nm.up(), 1)

                def c_scale(n):
                    dve.wait_ge(s_c_p.sem, s_c_p.at(l, 2 * n + 2))
                    link(dve.reciprocal(rr[:, n, :], sm[:, n, :]))
                    tt(pc[:, n % 2], pc[:, n % 2], bcl(rr[:, n, :], MEM), MUL).then_inc(s_c_w.up(), 1)

                for n in range(8):
                    c_max(n)
                    if n >= 1:
                        c_scale(n - 1)
                    if n >= 3 and n % 2 == 1:
                        h = (n - 3) // 2
                        for e in range(2):
                            split_lo(H_CA + 2 * h + e, src=bk[e])
                c_scale(7)
                for e in range(2):
                    split_lo(H_CA + 6 + e, src=bk[e])
                dense(B_CO, N_CO, KT, add_out(B_CO))
                norm_out(2, H_FF, "g_ffn")
                b = B_FF
                for half in range(2):
                    f0 = half * FH

                    def ffn_out(i, j, b, f0):
                        if j == 0:
                            return
                        dve.wait_ge(s_f_sg.sem, s_f_sg.at(l, i + (f0 + 1)))
                        dve.wait_ge(s_blk_done.sem, s_blk_done.at(l, 2 * i + (b + 2)))
                        dve.wait_ge(s_f_hi.sem, s_f_hi.at(l, i + f0))
                        dve.wait_ge(s_f_lo.sem, s_f_lo.at(l, i + f0))
                        tt(h2[:], sgate[:], bk[1], MUL).then_inc(s_f_h2.up(), 1)
                        dve.wait_ge(s_f_hi.sem, s_f_hi.at(l, i + (f0 + 1)))
                        tt(f_lo[:, bass.ds(i, 1), :].rearrange("p a n -> p (a n)"), h2[:],
                                 f_hi[:, bass.ds(i, 1), :].rearrange("p a n -> p (a n)").bitcast(F32), SUB).then_inc(s_f_lo.up(), 1)

                    def body(q, slot, loads, first_, b=b, f0=f0):
                        for j in range(2):
                            dve.wait_ge(s_w_hi.sem, s_w_hi.at(l, 2 * q + (b + j + 1)))
                            tt(w_lo[j][:, 0:KT, :].rearrange("p k n -> p (k n)"),
                                     raw[:, slot, j * WA:(j + 1) * WA],
                                     w_hi[j][:, 0:KT, :].rearrange("p k n -> p (k n)").bitcast(F32), SUB).then_inc(s_w_lo.up(), 1)
                            if not first_:
                                ffn_out(q - 1, j, b, f0)
                    pair_loop(dve, b // 2, FH, body)
                    ffn_out(FH - 1, 1, b, f0)
                    b += N_GU
                    dense(b, N_DN, FH, add_out(b))
                    b += N_DN

        @block.tensor
        def _(pe):
            def mm(out, lhsT, rhs, start=True, stop=True):
                return pe.matmul(out, lhsT, rhs, start=start, stop=stop)

            idn, ones, blk, tri = cst("idn"), cst("ones"), cst("blk"), cst("tri")

            pe.wait_ge(s_const_in.sem, 16)
            pe.wait_ge(s_x_in.sem, 16)
            for n in range(8):
                c, i = n // 2, n % 2
                if n >= 2:
                    pe.wait_ge(s_x_turned.sem, n - 1)
                for k in range(4):
                    last = pe.transpose(bk[2 + n % 2][:, k * P:(k + 1) * P], xtok[:, c, (4 * i + k) * P:(4 * i + k + 1) * P], idn)
                last.then_inc(s_x_tr.sem, 1)
            pe.wait_ge(s_mem_n.sem, 2)
            for n in range(4):
                c, i = n // 2, n % 2
                if n >= 2:
                    pe.wait_ge(s_m_ev.sem, n - 1)
                for k in range(4):
                    last = pe.transpose(bk[4 + n % 2][:, k * P:(k + 1) * P], mjunk[:, c, (4 * i + k) * P:(4 * i + k + 1) * P], idn)
                last.then_inc(s_m_tr.sem, 1)
            pe.wait_ge(s_c_bf.sem, 1)

            with pe.Fori(0, DEPTH) as l:
                def product(j, K, hi, lo, w):
                    for k in range(K):
                        mm(bk[j][:, 0:w], w_hi[j][:, k, :], hi[:, k, 0:w], k == 0, False)
                        mm(bk[j][:, 0:w], w_hi[j][:, k, :], lo[:, k, 0:w], False, False)
                        last = mm(bk[j][:, 0:w], w_lo[j][:, k, :], hi[:, k, 0:w], False, k == K - 1)
                    last.then_inc(s_blk_done.up(), 1)

                def dense(b0, n, K, hi, lo, w, free, e0, *needs):
                    trips[0] = n // 2
                    with pe.Fori(0, n // 2) as i:
                        for j in range(2):
                            if j == 0:
                                for s, v in needs:
                                    pe.wait_ge(s.sem, s.at(l, v))
                            pe.wait_ge(s_w_lo.sem, s_w_lo.at(l, 2 * i + (b0 + j + 1)))
                            pe.wait_ge(free.sem, free.at(l, 2 * i + (e0 + j - 1)))
                            product(j, K, hi, lo, w)
                    trips[0] = 1

                def norm(idx):
                    for k in range(KT):
                        pe.wait_ge(s_nrm_sq.sem, s_nrm_sq.at(l, idx * KT + k + 1))
                        mm(bk[2], ones, sq[:, k % 2, :], k == 0, k == KT - 1).then_inc(s_nrm_mm.up(), 1)

                norm(0)
                pe.wait_ge(s_wsm_lo.sem, s_wsm_lo.at(l, 1))
                pe.wait_ge(s_h_lo.sem, s_h_lo.at(l, H_IN + KT))
                for c in range(NC):
                    o = bk[7][:, 12 * c:12 * c + 12]
                    for k in range(KT):
                        hh, hl = h_hi[:, k, c * P:(c + 1) * P], h_lo[:, k, c * P:(c + 1) * P]
                        mm(o, hh, wsm_hi[:, k, :], k == 0, False)
                        mm(o, hh, wsm_lo[:, k, :], False, False)
                        last = mm(o, hl, wsm_hi[:, k, :], False, k == KT - 1)
                last.then_inc(s_g_ps.up(), 1)

                def product_in(b):
                    pe.wait_ge(s_w_lo.sem, s_w_lo.at(l, b + 1))
                    pe.wait_ge(s_evac_a.sem, s_evac_a.at(l, b - 1))

                def qk_sum(o, j):
                    pe.wait_ge(s_qk_sq.sem, s_qk_sq.at(l, o + 1))
                    mm(bk[2 + j], blk, sq[:, j, :]).then_inc(s_qk_ss.up(), 1)

                product_in(0)
                product(0, KT, h_hi, h_lo, SEQ)
                trips[0] = 3
                with pe.Fori(0, 3) as i:
                    for j in range(2):
                        product_in(2 * i + (j + 1))
                        product((j + 1) % 2, KT, h_hi, h_lo, SEQ)
                        qk_sum(2 * i + j, j)
                trips[0] = 1
                for b in range(7, N_QK + N_V):
                    product_in(b)
                    product(b % 2, KT, h_hi, h_lo, SEQ)
                    if b == 7:
                        qk_sum(6, 0)
                        qk_sum(7, 1)

                def v_turn(c):
                    if c == 0:
                        pe.wait_ge(s_evac_a.sem, s_evac_a.at(l, N_QK + N_V))
                        pe.wait_ge(s_qk_n.sem, s_qk_n.at(l, N_QK))
                        pe.wait_ge(s_g_v.sem, s_g_v.at(l, 2))
                    if c == 1:
                        pe.wait_ge(s_v_ev.sem, s_v_ev.at(l, 1))
                    if c >= 2:
                        pe.wait_ge(s_da_wt.sem, s_da_wt.at(l, c - 1))
                    for h in range(DA_H):
                        last = pe.transpose(bk[2][:, h * P:(h + 1) * P], vT[:, h, c * P:(c + 1) * P], idn)
                    last.then_inc(s_v_tr.up(), 1)

                def da_scores(n):
                    h, qt = n // NC, n % NC
                    nk = (qt + 1) * P
                    if n >= 2:
                        pe.wait_ge(s_da_p.sem, s_da_p.at(l, 2 * (n - 1)))
                    for c in range(2):
                        r = slice(64 * c, 64 * c + 64)
                        b = bk[4 + 2 * (n % 2) + c]
                        mm(b[:, 0:nk], projT[r, h, qt * P:nk], projT[r, 4 + h, 0:nk], True, False)
                        last = mm(b[:, nk - P:nk], idb[:], negq[:], False, True)
                    last.then_inc(s_da_s.up(), 1)

                def da_turn(n):
                    pe.wait_ge(s_da_w.sem, s_da_w.at(l, n + 1))
                    if n >= 1:
                        pe.wait_ge(s_da_wt.sem, s_da_wt.at(l, n))
                    if n < NC:
                        pe.wait_ge(s_v_ev.sem, s_v_ev.at(l, min(n + 2, NC)))
                    for k in range(n % NC + 1):
                        last = pe.transpose(bk[2][:, k * P:(k + 1) * P], wgt[:, n % 2, k * P:(k + 1) * P], idn)
                    last.then_inc(s_da_t.up(), 1)

                def da_values(n):
                    h, qt = n // NC, n % NC
                    pe.wait_ge(s_da_wt.sem, s_da_wt.at(l, n + 1))
                    if qt == 0 and h >= 1:
                        pe.wait_ge(s_da_o.sem, s_da_o.at(l, h))
                    for k in range(qt + 1):
                        last = mm(bk[3][:, qt * P:(qt + 1) * P], vtok[:, k, h, :], wgtT[:, n % 2, k * P:(k + 1) * P],
                                  k == 0, k == qt)
                    last.then_inc(s_da_pv.up(), 1)

                for s in range(ND + 2):
                    b = N_QK + N_V + s
                    if b < N_IN:
                        product_in(b)
                        product(b % 2, KT, h_hi, h_lo, SEQ)
                    if s < NC:
                        v_turn(s)
                    if s < ND:
                        da_scores(s)
                    if 0 <= s - 1 < ND:
                        da_turn(s - 1)
                    if 0 <= s - 2:
                        da_values(s - 2)
                for h in range(DA_H):
                    pe.wait_ge(s_on_sq.sem, s_on_sq.at(l, h + 1))
                    if h >= 2:
                        pe.wait_ge(s_on_rs.sem, s_on_rs.at(l, h - 1))
                    mm(bk[2 + h % 2], ones, sq[:, h % 2, :]).then_inc(s_on_ss.up(), 1)

                pe.wait_ge(s_on_rs.sem, s_on_rs.at(l, DA_H))
                pe.wait_ge(s_g_a.sem, s_g_a.at(l, 1))
                gaf = ga[:].rearrange("p c h -> p (c h)")
                mm(bk[3][:, 64:96], tri, gaf)
                mm(bk[3][:, 96:128], ones, gaf).then_inc(s_g_cum.up(), 1)

                def decays(b, c, h0):
                    for h in range(4):
                        o = b[:, h * P:(h + 1) * P]
                        mm(o, ga[:, c, h0 + h:h0 + h + 1].to_broadcast([P, P]), tri, True, False)
                        last = mm(o, idb[:], negd[:], False, True)
                    return last

                pe.wait_ge(s_g_dk.sem, s_g_dk.at(l, 1))
                for c in range(NC):
                    if c == 0:
                        pe.wait_ge(s_convs.sem, s_convs.at(l, 4))
                    if c >= 2:
                        pe.wait_ge(s_s_ev.sem, s_s_ev.at(l, c - 1))
                        pe.wait_ge(s_s_x.sem, s_s_x.at(l, 2 * (c - 1)))
                    for t in range(4):
                        last = pe.transpose(bk[2 + 2 * (t // 2) + c % 2][:, (t % 2) * P:(t % 2 + 1) * P],
                                            convT[:, t, c * P:(c + 1) * P], idn)
                    last.then_inc(s_s_tr.up(), 1)
                pe.wait_ge(s_s_ev.sem, s_s_ev.at(l, NC))
                pe.wait_ge(s_s_x.sem, s_s_x.at(l, 2 * NC))
                for i in range(2):
                    for c in range(2):
                        for t in range(2):
                            cc = 2 * i + c
                            last = pe.transpose(bk[2 + i][:, (2 * c + t) * P:(2 * c + t + 1) * P],
                                                zT[:, t, cc * P:(cc + 1) * P], idn)
                    last.then_inc(s_z_tr.up(), 1)
                pe.wait_ge(s_convs.sem, s_convs.at(l, 6))
                for c in range(NC):
                    cs = slice(c * P, (c + 1) * P)
                    if c >= 2:
                        pe.wait_ge(s_s_dec.sem, s_s_dec.at(l, 4 * (c - 1)))
                    decays(bk[4 + c % 2], c, 0).then_inc(s_s_d.up(), 1)
                    if c >= 1:
                        pe.wait_ge(s_s_st.sem, s_s_st.at(l, c))
                    for g in range(2):
                        last = mm(bk[6][:, g * P:(g + 1) * P], convT[:, 2 + g, cs], convT[:, 4 + g, cs])
                    last.then_inc(s_s_cb.up(), 1)
                    if c < NC - 1:
                        if c >= 2:
                            pe.wait_ge(s_s_hst.sem, s_s_hst.at(l, c - 1))
                        for g in range(2):
                            last = mm(bk[c % 2][:, g * P:(g + 1) * P], btok[:, c, g, :],
                                      xdd[:, c, 2 * g:2 * g + 2, :].rearrange("p h d -> p (h d)"))
                        last.then_inc(s_s_h.up(), 1)
                    pe.wait_ge(s_s_st.sem, s_s_st.at(l, c + 1))
                    if c >= 1:
                        pe.wait_ge(s_s_ya.sem, s_s_ya.at(l, c))
                        pe.wait_ge(s_s_hst.sem, s_s_hst.at(l, c))
                    for h in range(S_H):
                        last = mm(bk[7][:, h * S_D:(h + 1) * S_D], scoT[:, c % 2, h, :], xd[:, c, h, :])
                    if c:
                        for g in range(2):
                            last = mm(bk[7][:, 256 + g * P:256 + (g + 1) * P], convT[:, 4 + g, cs],
                                      hst[:, c % 2, 2 * g:2 * g + 2, :].rearrange("p h d -> p (h d)"))
                    last.then_inc(s_s_y.up(), 1)
                pe.wait_ge(s_s_yn.sem, s_s_yn.at(l, 1))
                for f in range(2):
                    for c in range(NC):
                        last = pe.transpose(bk[2 + f][:, c * P:(c + 1) * P],
                                            ysd[:, c, 2 * f:2 * f + 2, :].rearrange("p h d -> p (h d)"), idn)
                    last.then_inc(s_so_tr.up(), 1)

                pe.wait_ge(s_convs.sem, s_convs.at(l, 12))
                pe.wait_ge(s_h_f32.sem, s_h_f32.at(l, H_MIX + 6))
                for c in range(NC):
                    if c >= 2:
                        pe.wait_ge(s_gt_ev.sem, s_gt_ev.at(l, 2 * (c - 1)))
                    for t in range(6):
                        o = bk[2 + c % 2][:, t * P:(t + 1) * P] if t < 4 else bk[4 + c % 2][:, (t - 4) * P:(t - 3) * P]
                        last = pe.transpose(o, convG[:, t, c * P:(c + 1) * P], idn)
                    last.then_inc(s_gt_tr.up(), 1)
                pe.wait_ge(s_gt_ev.sem, s_gt_ev.at(l, 8))
                for i in range(6):
                    which, pr = i // 2, i % 2
                    if i == 0:
                        pe.wait_ge(s_gn_n.sem, s_gn_n.at(l, 2))
                    if i >= 2:
                        pe.wait_ge(s_g3_ev.sem, s_g3_ev.at(l, i - 1))
                    for c in range(NC):
                        src = (qktok[:, c, 1], qktok[:, c, 0], qE[:, c])[which]
                        last = pe.transpose(bk[2 + pr][:, c * P:(c + 1) * P],
                                            src[:, 2 * pr:2 * pr + 2, :].rearrange("p h d -> p (h d)"), idn)
                    last.then_inc(s_g3_tr.up(), 1)
                pe.wait_ge(s_g3_ev.sem, s_g3_ev.at(l, 6))
                for c in range(NC):
                    cs = slice(c * P, (c + 1) * P)
                    if c >= 2:
                        pe.wait_ge(s_gd_dec.sem, s_gd_dec.at(l, 4 * (c - 1)))
                    decays(bk[4 + c % 2], c, 4).then_inc(s_gd_d.up(), 1)
                    if c >= 1:
                        pe.wait_ge(s_gd_at.sem, s_gd_at.at(l, c))
                        pe.wait_ge(s_gd_att.sem, s_gd_att.at(l, c))
                    for h in range(G_H):
                        r = slice(64 * (h % 2), 64 * (h % 2) + 64)
                        kk = tr3[r, 0, h // 2, cs]
                        o = bk[6 + h % 2]
                        mm(o[:, (h // 2) * P:(h // 2 + 1) * P], kk, kk)
                        last = mm(o[:, (2 + h // 2) * P:(3 + h // 2) * P], kk, tr3[r, 1, h // 2, cs])
                    last.then_inc(s_gd_kq.up(), 1)
                for c in range(NC):
                    pe.wait_ge(s_ti_0.sem, s_ti_0.at(l, c + 1))
                    if c >= 2:
                        pe.wait_ge(s_ti_ev.sem, s_ti_ev.at(l, c - 1))
                    for h in range(G_H):
                        last = pe.transpose(bk[2 + c % 2][:, h * P:(h + 1) * P], tri_t[:, c, h, :], idn)
                    last.then_inc(s_ti_tr.up(), 1)
                def join_1(n):
                    c = n % NC
                    pe.wait_ge(s_lvl.sem, s_lvl.at(l, n + 1))
                    if n < 2:
                        pe.wait_ge(s_ti_ev.sem, s_ti_ev.at(l, n + 3))
                    else:
                        pe.wait_ge(s_m1_ev.sem, s_m1_ev.at(l, n - 1))
                    if n >= NC:
                        pe.wait_ge(s_t_upd.sem, s_t_upd.at(l, n - NC + 1))
                    for h in range(G_H):
                        last = mm(bk[2 + n % 2][:, h * P:(h + 1) * P], lvlA[:, n % 2, h, :], tri_i[:, c, h, :])
                    last.then_inc(s_m1_mm.up(), 1)

                def join_2(n):
                    v, c = n // NC, n % NC
                    pe.wait_ge(s_m1_ev.sem, s_m1_ev.at(l, n + 1))
                    if n >= NC:
                        pe.wait_ge(s_tt_upd.sem, s_tt_upd.at(l, n - NC + 1))
                    for h in range(G_H):
                        if v < NLEV - 2:
                            mm(joined(c, v, 0)[:, h], tri_t[:, c, h, :], halves(m1[:, c], v, 0)[:, h])
                        last = mm(joined(c, v, 1)[:, h], m1[:, c, h, :], halves(tri_t[:, c], v, 1)[:, h])
                    last.then_inc(s_tx_mm.up(), 1)

                join_1(0)
                for n in range(1, NJ):
                    join_1(n)
                    join_2(n - 1)
                join_2(NJ - 1)
                pe.wait_ge(s_tt_upd.sem, s_tt_upd.at(l, (NLEV - 1) * NC))
                pe.wait_ge(s_m1_ev.sem, s_m1_ev.at(l, (NLEV - 1) * NC))
                for pr in range(2):
                    for c in range(NC):
                        for hh in range(2):
                            h = 2 * pr + hh
                            last = mm(bk[2 + pr][64 * hh:64 * hh + 64, c * P:(c + 1) * P], kE[:, c, h, :],
                                      tri_t[:, c, h, :])
                    last.then_inc(s_w_mm.up(), 1)
                pe.wait_ge(s_w_ev.sem, s_w_ev.at(l, 2))
                for c in range(NC):
                    cs = slice(c * P, (c + 1) * P)
                    if c >= 1:
                        pe.wait_ge(s_vn.sem, s_vn.at(l, c))
                        pe.wait_ge(s_st.sem, s_st.at(l, c))
                    for h in range(G_H):
                        r = slice(64 * (h % 2), 64 * (h % 2) + 64)
                        o = bk[4 + h % 2][:, (h // 2) * G_D:(h // 2 + 1) * G_D]
                        last = mm(o, tri_t[:, c, h, :], gvtok[:, c, h, :], True, c == 0)
                        if c:
                            last = mm(o, wTn[r, h // 2, cs], stS[r, c % 2, h // 2, :], False, True)
                    last.then_inc(s_vn_mm.up(), 1)
                    pe.wait_ge(s_vn.sem, s_vn.at(l, c + 1))
                    if c < NC - 1:
                        for h in range(G_H):
                            r = slice(64 * (h % 2), 64 * (h % 2) + 64)
                            last = mm(bk[c % 2][r, (h // 2) * G_D:(h // 2 + 1) * G_D], kgt[:, c, h, :], vnew[:, c % 2, h, :])
                        last.then_inc(s_st_mm.up(), 1)
                    if c >= 1:
                        pe.wait_ge(s_o_ev.sem, s_o_ev.at(l, c))
                    for h in range(G_H):
                        r = slice(64 * (h % 2), 64 * (h % 2) + 64)
                        o = bk[6 + h % 2][:, (h // 2) * G_D:(h // 2 + 1) * G_D]
                        if c:
                            mm(o, tr3[r, 2, h // 2, cs], stS[r, c % 2, h // 2, :], True, False)
                        last = mm(o, attT[:, c, h, :], vnew[:, c % 2, h, :], c == 0, True)
                    last.then_inc(s_o_mm.up(), 1)
                for i in range(2):
                    for c in range(2):
                        for t in range(2):
                            cc = 2 * i + c
                            last = pe.transpose(bk[2 + i][:, (2 * c + t) * P:(2 * c + t + 1) * P],
                                                zT[:, 2 + t, cc * P:(cc + 1) * P], idn)
                    last.then_inc(s_zg_tr.up(), 1)
                pe.wait_ge(s_zg_ev.sem, s_zg_ev.at(l, 2))
                pe.wait_ge(s_go_n.sem, s_go_n.at(l, 1))
                for f in range(2):
                    for c in range(NC):
                        last = pe.transpose(bk[2 + f][:, c * P:(c + 1) * P],
                                            otok[:, c, 2 * f:2 * f + 2, :].rearrange("p h d -> p (h d)"), idn)
                    last.then_inc(s_go_tr.up(), 1)

                dense(B_OUT, N_OUT, KT, h_hi, h_lo, SEQ, s_evac_d, ED_OUT, (s_h_lo, H_MIX + KT))
                dense(B_KV, N_KV, KT, h_hi, h_lo, MEM, s_evac_a, EA_KV, (s_h_lo, H_MEM + KT), (s_evac_d, ED_OUT + N_OUT))
                norm(1)
                dense(B_CQ, N_CQ, KT, h_hi, h_lo, SEQ, s_evac_a, EA_CQ, (s_h_lo, H_X + KT))
                for n in range(16):
                    w = SEQ if n < 8 else MEM
                    pe.wait_ge(s_c_sq.sem, s_c_sq.at(l, n + 1))
                    if n % 2 == 0 and n >= 4:
                        pe.wait_ge(s_c_rs.sem, s_c_rs.at(l, n // 2 - 1))
                    mm(bk[2 + (n // 2) % 2][:, 0:w], ones, sq[:, n % 2, 0:w], n % 2 == 0, n % 2 == 1).then_inc(s_c_ssm.up(), 1)
                pe.wait_ge(s_c_rs.sem, s_c_rs.at(l, 8))
                for i in range(4):
                    if i >= 2:
                        pe.wait_ge(s_cv_ev.sem, s_cv_ev.at(l, i - 1))
                    for t in range(4):
                        last = pe.transpose(bk[2 + i % 2][:, t * P:(t + 1) * P],
                                            kvT[:, 8 + 4 * (i % 2) + t, (i // 2) * P:(i // 2 + 1) * P], idn)
                    last.then_inc(s_cv_tr.up(), 1)

                def c_scores(n):
                    h, qp = n // 2, n % 2
                    if n >= 2:
                        pe.wait_ge(s_c_p.sem, s_c_p.at(l, 2 * (n - 1)))
                    for i in range(2):
                        q0 = (2 * qp + i) * P
                        for f in range(2):
                            last = mm(bk[4 + n % 2][:, i * MEM:(i + 1) * MEM], qcT[:, 2 * h + f, q0:q0 + P],
                                      kvT[:, 2 * h + f, :], f == 0, f == 1)
                    last.then_inc(s_c_s.up(), 1)

                def c_turn(n):
                    pe.wait_ge(s_c_w.sem, s_c_w.at(l, n + 1))
                    if n >= 2:
                        pe.wait_ge(s_c_pt.sem, s_c_pt.at(l, n - 1))
                    for i in range(2):
                        for m in range(2):
                            last = pe.transpose(bk[6 + n % 2][:, m * 256 + i * P:m * 256 + (i + 1) * P],
                                                pc[:, n % 2, i, m * P:(m + 1) * P], idn)
                    last.then_inc(s_c_t.up(), 1)

                def c_values(h):
                    pe.wait_ge(s_c_pt.sem, s_c_pt.at(l, 2 * h + 2))
                    for e in range(2):
                        if h >= 1:
                            pe.wait_ge(s_h_lo.sem, s_h_lo.at(l, H_CA + 2 * (h - 1) + e + 1))
                        for m in range(2):
                            last = mm(bk[e], vmt[:, m, h * X_D + e * P:h * X_D + (e + 1) * P], pT[:, h % 2, m, :],
                                      m == 0, m == 1)
                        last.then_inc(s_c_pv.up(), 1)

                pe.wait_ge(s_c_n.sem, s_c_n.at(l, 16))
                pe.wait_ge(s_cv_ev.sem, s_cv_ev.at(l, 4))
                for n in range(8):
                    c_scores(n)
                    if n >= 1:
                        c_turn(n - 1)
                    if n >= 2 and n % 2 == 0:
                        c_values(n // 2 - 1)
                c_turn(7)
                c_values(3)
                dense(B_CO, N_CO, KT, h_hi, h_lo, SEQ, s_evac_d, ED_CO, (s_h_lo, H_CA + KT))
                norm(2)
                b = B_FF
                for half in range(2):
                    f0, e0 = half * FH, ED_DN + half * N_DN
                    trips[0] = FH
                    with pe.Fori(0, FH) as i:
                        pe.wait_ge(s_h_lo.sem, s_h_lo.at(l, H_FF + KT))
                        pe.wait_ge(s_evac_d.sem, s_evac_d.at(l, e0))
                        for j, free in enumerate((s_f_sg, s_f_h2)):
                            pe.wait_ge(s_w_lo.sem, s_w_lo.at(l, 2 * i + (b + j + 1)))
                            pe.wait_ge(free.sem, free.at(l, i + f0))
                            product(j, KT, h_hi, h_lo, SEQ)
                    trips[0] = 1
                    b += N_GU
                    dense(b, N_DN, FH, f_hi, f_lo, SEQ, s_evac_d, e0, (s_f_sg, f0 + FH), (s_f_lo, f0 + FH))
                    b += N_DN
            for n in range(8):
                c, i = n // 2, n % 2
                if n == 0:
                    pe.wait_ge(s_evac_d.sem, s_evac_d.at(DEPTH, 0))
                if n >= 2:
                    pe.wait_ge(s_y_ready.sem, n - 1)
                for k in range(4):
                    last = pe.transpose(bk[2 + n % 2][:, k * P:(k + 1) * P], xT[:, 4 * i + k, c * P:(c + 1) * P], idn)
                last.then_inc(s_y_tr.sem, 1)

        got = {k: v for k, v in ((k, s.n) for k, s in signals.items()) if v}
        if got != PER_LAYER:
            if strict:
                raise AssertionError(f"PER_LAYER = {got}")
        return got


def layout(inp):
    f = lambda n: np.ascontiguousarray(np.asarray(inp[n]))
    L = DEPTH
    w_in = f("w_in")
    o = np.cumsum([0, 512, 512, 512, 256, 768, 4, 768, 256, 4, 4])
    part = {n: w_in[:, :, o[i]:o[i + 1]] for i, n in enumerate(("qa", "ka", "va", "zs", "xbc", "dt", "qkv", "zg", "b", "a"))}
    big = np.concatenate([part[n] for n in ("qa", "ka", "va", "xbc", "qkv", "zs", "zg")], axis=2)
    small = np.concatenate([part[n] for n in ("dt", "a", "b")], axis=2)

    def blocks(w, k):
        Lw, K, N = w.shape
        return w.reshape(Lw, k, P, N // P, P).transpose(0, 3, 2, 1, 4).reshape(Lw, N // P, P, k * P)

    gu = blocks(f("w_gate_up"), KT)
    gu = np.stack([gu[:, :FT], gu[:, FT:]], axis=2).reshape(L, 2 * FT, P, WA)
    wa = np.concatenate([blocks(big, KT), blocks(f("w_out"), KT), blocks(f("w_ckv"), KT), blocks(f("w_cq"), KT),
                         blocks(f("w_co"), KT), gu], axis=1)
    wa = wa.reshape(L, PAIRS_A, 2, P, WA).transpose(0, 1, 3, 2, 4).reshape(L * PAIRS_A, P, 2 * WA)
    dn = f("w_down").reshape(L, 2, FH * P, D_MODEL)
    wd = np.stack([blocks(dn[:, h], FH) for h in range(2)], axis=1)
    wd = wd.reshape(L, PAIRS_D, 2, P, WD).transpose(0, 1, 3, 2, 4).reshape(L * PAIRS_D, P, 2 * WD)
    wsm = small.reshape(L, KT, P, 12).transpose(0, 2, 1, 3).reshape(L, P, KT * 12)

    rows = lambda a: np.broadcast_to(a[:, None, :], (L, P, a.shape[-1]))
    tiles = lambda a: a.reshape(L, -1, P).transpose(0, 2, 1)
    twice = lambda a: np.concatenate([a, a], axis=-1)[:, :, None]
    cw = np.concatenate([f("ssd_conv_w"), f("gdn_conv_w")], axis=2)
    cw = cw.reshape(L, 4, 12, P).transpose(0, 3, 2, 1).reshape(L, P, 48)
    cb = tiles(np.concatenate([f("ssd_conv_b"), np.zeros((L, 768), np.float32)], axis=1))
    li = np.array([0.8 - 0.6 * math.exp(-0.3 * l) for l in range(L)], np.float32)
    lamv = np.concatenate([f("da_lambda_q1"), f("da_lambda_k1"), f("da_lambda_q2"), f("da_lambda_k2")], axis=1)
    gng = twice(f("gdn_norm_g"))
    prm = np.concatenate([
        tiles(f("norm_mix_g")), tiles(f("norm_x_g")), tiles(f("norm_mem_g")), tiles(f("norm_ffn_g")),
        *([twice(f("da_q_norm_g"))] * 4), *([twice(f("da_k_norm_g"))] * 4), f("da_sub_norm_g")[:, :, None], cw, cb,
        rows(np.concatenate([f("ssd_dt_bias"), f("gdn_dt_bias")], axis=1)),
        rows(np.concatenate([f("ssd_A_log"), f("gdn_A_log")], axis=1)),
        rows(f("ssd_D")), tiles(f("ssd_norm_g")), gng, gng, tiles(f("xq_norm_g")), tiles(f("xk_norm_g")),
        rows(li[:, None]), rows(np.array([1.0 - (0.8 - 0.6 * math.exp(-0.3 * l)) for l in range(L)], np.float32)[:, None]),
        rows(lamv)], axis=2)
    i = np.arange(P)
    con = np.zeros((P, NCON), np.float32)
    put = lambda n, a: con.__setitem__((slice(None), slice(*CC[n])), a)
    put("idn", np.eye(P))
    put("ones", 1.0)
    put("blk", i[:, None] // 64 == i[None, :] // 64)
    put("tri", i[:, None] <= i[None, :])
    put("negq", np.where(i[None, :] > i[:, None], -1e30, 0.0))
    put("negd", np.where(i[None, :] < i[:, None], -1e30, 0.0))
    levels = []
    for v in range(NLEV):
        b = 1 << v
        same = (i[:, None] // (2 * b)) == (i[None, :] // (2 * b))
        levels.append(same & (i[:, None] % (2 * b) < b) & (i[None, :] % (2 * b) >= b))
    put("lev", np.concatenate(levels, axis=1))
    c = np.ascontiguousarray
    return {"x": c(f("x")[0]), "mem": c(f("mem")[0]), "wa": c(wa), "wd": c(wd), "wsm": c(wsm), "prm": c(prm), "con": con}


def kernel(**inputs):
    import concourse.bacc as _bacc
    from concourse.bass_utils import run_bass_kernel_spmd as _run

    nc = _bacc.Bacc("TRN2", target_bir_lowering=False, num_devices=1)
    arrays = layout(inputs)
    args = [nc.dram_tensor(f"in_{n}", a.shape, mybir.dt.from_np(a.dtype), kind="ExternalInput").ap()
            for n, a in arrays.items()]
    out = nc.dram_tensor("out_x", (SEQ, D_MODEL), F32, kind="ExternalOutput").ap()
    trunk(nc, *args, out)
    r = _run(nc, [{f"in_{n}": a for n, a in arrays.items()}], core_ids=[0])
    return r.results[0]["out_x"].reshape(1, SEQ, D_MODEL)
```

```python
import math
from contextlib import ExitStack

import numpy as np
import concourse.bass as bass
from concourse import mybir

P = 128
D_MODEL, SEQ, DEPTH, MEM = 1024, 512, 2, 256
EPS = 1e-6
KT = D_MODEL // P
CH = 128
NC = SEQ // CH
DA_H, DA_D, DA_V = 4, 64, 128
S_H, S_D = 4, 64
G_H, G_D = 4, 64
X_H, X_D = 4, 256
ND = DA_H * NC
D_FF = 2816
FT = D_FF // P
FH = FT // 2
NLEV = 7
NJ = (NLEV - 1) * NC

F32, F32R, BF16 = mybir.dt.float32, mybir.dt.float32r, mybir.dt.bfloat16
ACT = mybir.ActivationFunctionType
ALU = mybir.AluOpType
AX = mybir.AxisListType

LN_EXP = "natural_log_exp_and_others"

B_IN, N_IN = 0, 28
N_QK, N_V, N_CONV = 8, 4, 12
B_OUT, N_OUT = 28, 8
B_KV, N_KV = 36, 16
B_CQ, N_CQ = 52, 8
B_CO, N_CO = 60, 8
N_CA = 8
B_FF = 68
N_GU, N_DN = 2 * FH, 8
NB = B_FF + 2 * (N_GU + N_DN)
PAIRS_A = (B_FF + 2 * N_GU) // 2
PAIRS_D = N_DN
WA, WD = KT * P, FH * P

H_MIX, H_IN, H_MEM, H_X, H_CA, H_FF = 8, 0, 16, 24, 32, 40

EA_IN, EA_KV, EA_CQ = 0, 28, 44
ED_OUT, ED_CO, ED_DN = 0, 8, 16

PC = {}
_at = 0
for _n, _w in (("g_mix", 8), ("g_x", 8), ("g_mem", 8), ("g_ffn", 8), ("qkg", 8), ("subg", 1),
               ("cw", 48), ("cb", 12), ("dtb", 8), ("alog", 8), ("dsk", 4), ("sng", 2), ("gng", 2),
               ("xqg", 2), ("xkg", 2), ("laminit", 1), ("onemin", 1), ("lamv", 256)):
    PC[_n] = (_at, _at + _w)
    _at += _w
NPRM = _at
CC = {n: (i * P, (i + 1) * P) for i, n in enumerate(("idn", "ones", "blk", "tri", "negq", "negd"))}
CC["lev"] = (6 * P, (6 + NLEV) * P)
NCON = (6 + NLEV) * P

PER_LAYER = {
    "act_step": 28, "blk_done": 128, "c_nm": 8, "c_p": 16, "c_pt": 8, "c_pv": 8, "c_s": 8, "c_t": 8, "c_w": 8,
    "ck_n": 8, "ck_rs": 4, "ck_sq": 8, "ck_ss": 4, "conv": 12, "convs": 12, "cq_n": 8, "cq_rs": 4, "cq_sq": 8,
    "cq_ss": 8, "cv_ev": 4, "cv_tr": 4, "da_nm": 16, "da_o": 4, "da_p": 32, "da_pv": 16, "da_s": 16, "da_t": 16,
    "da_w": 16, "da_wt": 16, "dve_step": 154, "evac_a": 52, "evac_d": 32, "f_h2": 22, "f_hi": 22, "f_lo": 22,
    "f_sg": 22, "g3_ev": 6, "g3_tr": 6, "g_a": 1, "g_cum": 1, "g_dk": 1, "g_edk": 1, "g_ex": 1, "g_ln": 2,
    "g_mm": 1, "g_out": 1, "g_ps": 1, "g_v": 2, "gd_at": 4, "gd_att": 4, "gd_d": 4, "gd_dec": 16, "gd_kq": 4,
    "gn_n": 3, "gn_rs": 1, "gn_ss": 1, "go_n": 1, "go_rs": 1, "go_ss": 1, "go_tr": 2, "gsq": 4, "gt_ev": 8,
    "gt_tr": 4, "h_f32": 40, "h_hi": 48, "h_lo": 48, "kdec": 2, "lam_exp": 2, "lam_sum": 1, "lvl": 24, "m1_ev":
    24, "m1_mm": 24, "nrm_acc": 18, "nrm_mm": 9, "nrm_rs": 3, "nrm_sq": 24, "o_ev": 4, "o_mm": 4, "on_rs": 4,
    "on_sq": 4, "on_ss": 4, "prm_in": 32, "qk_n": 8, "qk_rs": 8, "qk_sq": 8, "qk_ss": 8, "raw_in0": 512,
    "raw_in1": 512, "s_cb": 4, "s_d": 4, "s_dec": 16, "s_ev": 4, "s_h": 3, "s_hst": 3, "s_rs": 1, "s_ss": 1,
    "s_st": 4, "s_tr": 4, "s_x": 8, "s_y": 4, "s_ya": 4, "s_yn": 1, "so_tr": 2, "st": 3, "st_mm": 3, "t_upd":
    20, "ti_0": 4, "ti_ev": 4, "ti_m": 4, "ti_tr": 4, "tt_upd": 24, "tx_mm": 24, "v_ev": 4, "v_tr": 4, "vn": 4,
    "vn_mm": 4, "w_ev": 2, "w_hi": 128, "w_lo": 128, "w_mm": 2, "wsm_0": 2, "wsm_hi": 1, "wsm_lo": 1, "z_ev": 2,
    "z_tr": 2, "zg_ev": 2, "zg_tr": 2, "zs": 4
}


START = {"nrm_acc": 2, "qk_ss": 1, "qk_n": 1, "w_lo": 3, "blk_done": 2, "evac_a": 2, "evac_d": 2, "f_sg": 1, "f_h2": 1, "f_hi": 1, "f_lo": 1, "h_lo": 1}


SETUP = {"nrm_sq": 8, "nrm_mm": 8}


class Signal:

    def __init__(self, nc, ctx, name, trips):
        self.sem = ctx.enter_context(nc.semaphore(name))
        self.name, self.n, self.trips = name, 0, trips
        self.per_layer, self.start = PER_LAYER.get(name, 0), START.get(name, 0) + SETUP.get(name, 0)

    def up(self, by=1):
        self.n += by * self.trips[0]
        return self.sem

    def at(self, l, v):
        return l * self.per_layer + (v + self.start)


def trunk(nc, x_d, mem_d, wa_d, wd_d, wsm_d, prm_d, con_d, out_d, strict=True):
    ctx = ExitStack()
    nc.disable_value_cache = True
    with ctx:
        trips = [1]
        signals = {}

        def signal(name):
            signals[name] = Signal(nc, ctx, name, trips)
            return signals[name]

        s_act_step = signal("act_step")
        s_blk_done = signal("blk_done")
        s_c_bf = signal("c_bf")
        s_cq_sq = signal("cq_sq")
        s_cq_ss = signal("cq_ss")
        s_cq_rs = signal("cq_rs")
        s_cq_n = signal("cq_n")
        s_ck_sq = signal("ck_sq")
        s_ck_ss = signal("ck_ss")
        s_ck_rs = signal("ck_rs")
        s_ck_n = signal("ck_n")
        s_c_nm = signal("c_nm")
        s_c_p = signal("c_p")
        s_c_pt = signal("c_pt")
        s_c_pv = signal("c_pv")
        s_c_s = signal("c_s")
        s_c_t = signal("c_t")
        s_c_w = signal("c_w")
        s_const_in = signal("const_in")
        s_conv = signal("conv")
        s_convs = signal("convs")
        s_cv_ev = signal("cv_ev")
        s_cv_tr = signal("cv_tr")
        s_da_nm = signal("da_nm")
        s_da_o = signal("da_o")
        s_da_p = signal("da_p")
        s_da_pv = signal("da_pv")
        s_da_s = signal("da_s")
        s_da_t = signal("da_t")
        s_da_w = signal("da_w")
        s_da_wt = signal("da_wt")
        s_dve_step = signal("dve_step")
        s_evac_a = signal("evac_a")
        s_evac_d = signal("evac_d")
        s_f_h2 = signal("f_h2")
        s_f_hi = signal("f_hi")
        s_f_lo = signal("f_lo")
        s_f_sg = signal("f_sg")
        s_g3_ev = signal("g3_ev")
        s_g3_tr = signal("g3_tr")
        s_g_a = signal("g_a")
        s_g_cum = signal("g_cum")
        s_g_dk = signal("g_dk")
        s_g_edk = signal("g_edk")
        s_g_ex = signal("g_ex")
        s_g_ln = signal("g_ln")
        s_g_ps = signal("g_ps")
        s_g_v = signal("g_v")
        s_gd_at = signal("gd_at")
        s_gd_att = signal("gd_att")
        s_gd_d = signal("gd_d")
        s_gd_dec = signal("gd_dec")
        s_gd_kq = signal("gd_kq")
        s_gn_n = signal("gn_n")
        s_gn_rs = signal("gn_rs")
        s_gn_ss = signal("gn_ss")
        s_go_n = signal("go_n")
        s_go_rs = signal("go_rs")
        s_go_ss = signal("go_ss")
        s_go_tr = signal("go_tr")
        s_gt_ev = signal("gt_ev")
        s_gt_tr = signal("gt_tr")
        s_h_f32 = signal("h_f32")
        s_h_hi = signal("h_hi")
        s_h_lo = signal("h_lo")
        s_lam_exp = signal("lam_exp")
        s_lam_sum = signal("lam_sum")
        s_lvl = signal("lvl")
        s_m1_ev = signal("m1_ev")
        s_m1_mm = signal("m1_mm")
        s_m_ev = signal("m_ev")
        s_m_tr = signal("m_tr")
        s_mem_in = signal("mem_in")
        s_mem_n = signal("mem_n")
        s_mem_rs = signal("mem_rs")
        s_mem_sq = signal("mem_sq")
        s_nrm_mm = signal("nrm_mm")
        s_nrm_acc = signal("nrm_acc")
        s_nrm_rs = signal("nrm_rs")
        s_nrm_sq = signal("nrm_sq")
        s_o_ev = signal("o_ev")
        s_o_mm = signal("o_mm")
        s_on_rs = signal("on_rs")
        s_on_sq = signal("on_sq")
        s_on_ss = signal("on_ss")
        s_prm_in = signal("prm_in")
        s_qk_n = signal("qk_n")
        s_qk_rs = signal("qk_rs")
        s_qk_sq = signal("qk_sq")
        s_qk_ss = signal("qk_ss")
        s_s_cb = signal("s_cb")
        s_s_d = signal("s_d")
        s_s_dec = signal("s_dec")
        s_s_ev = signal("s_ev")
        s_s_h = signal("s_h")
        s_s_hst = signal("s_hst")
        s_s_rs = signal("s_rs")
        s_s_ss = signal("s_ss")
        s_s_st = signal("s_st")
        s_s_tr = signal("s_tr")
        s_s_x = signal("s_x")
        s_s_y = signal("s_y")
        s_s_ya = signal("s_ya")
        s_s_yn = signal("s_yn")
        s_setup = signal("setup")
        s_so_tr = signal("so_tr")
        s_st = signal("st")
        s_st_mm = signal("st_mm")
        s_t_upd = signal("t_upd")
        s_ti_0 = signal("ti_0")
        s_ti_ev = signal("ti_ev")
        s_ti_tr = signal("ti_tr")
        s_tt_upd = signal("tt_upd")
        s_tx_mm = signal("tx_mm")
        s_v_ev = signal("v_ev")
        s_v_setup = signal("v_setup")
        s_v_tr = signal("v_tr")
        s_vn = signal("vn")
        s_vn_mm = signal("vn_mm")
        s_w_ev = signal("w_ev")
        s_w_hi = signal("w_hi")
        s_w_lo = signal("w_lo")
        s_w_mm = signal("w_mm")
        s_wsm_hi = signal("wsm_hi")
        s_wsm_lo = signal("wsm_lo")
        s_x_in = signal("x_in")
        s_x_tr = signal("x_tr")
        s_x_turned = signal("x_turned")
        s_y_out = signal("y_out")
        s_y_ready = signal("y_ready")
        s_y_tr = signal("y_tr")
        s_z_ev = signal("z_ev")
        s_z_tr = signal("z_tr")
        s_zs = signal("zs")
        s_kdec = signal("kdec")
        s_wsm_0 = signal("wsm_0")
        s_g_mm = signal("g_mm")
        s_g_out = signal("g_out")
        s_gsq = signal("gsq")
        s_ti_m = signal("ti_m")
        s_zg_ev = signal("zg_ev")
        s_zg_tr = signal("zg_tr")
        s_raw_in = [signal("raw_in0"), signal("raw_in1")]
        base = (nc.sbuf_base + 31) // 32 * 32
        total = (nc.sbuf_usable_end - base) // 4
        cur = [0]

        def at(name, off, shape, dt=F32):
            return nc.alloc_sbuf_tensor_at(name, [P] + list(shape), dt, offset=base + 4 * off)

        def new(name, shape, dt=F32):
            n = int(np.prod(shape))
            words = n if dt != BF16 else (n + 1) // 2
            words = (words + 7) // 8 * 8
            t = at(name, cur[0], shape, dt)
            cur[0] += words
            return t

        xT = new("xT", [KT, SEQ])
        h_hi = new("h_hi", [KT, SEQ], F32R)
        h_lo = new("h_lo", [KT, SEQ], F32R)
        memn = new("memn", [KT, MEM])
        raw = new("raw", [2, 2 * WD])
        w_hi = [new(f"w_hi{i}", [FH, P], F32R) for i in range(2)]
        w_lo = [new(f"w_lo{i}", [FH, P], F32R) for i in range(2)]
        con = new("con", [NCON])
        idb, negq, negd = (new(n, [P], BF16) for n in ("idb", "negq", "negd"))
        prm = new("prm", [NPRM])
        wsm = new("wsm", [KT, 12])
        eps, seed = new("eps", [2]), new("seed", [sum(START.values())])
        htmp = new("htmp", [2, SEQ])
        sq = new("sq", [2, SEQ])
        rs = new("rs", [2, SEQ])
        lp, lsum, lexp, nlam = new("lp", [2, 64]), new("lsum", [2]), new("lexp", [2]), new("nlam", [2])
        ag, sg1 = new("ag", [8]), new("sg1", [1])
        mx, sm, rr = new("mx", [16, 2]), new("sm", [16, 2]), new("rr", [16, 2])
        gv, gb, g1, sp, ga = (new(n, [NC, w]) for n, w in (("gv", 8), ("gb", 4), ("g1", 8), ("sp", 8), ("ga", 8)))
        beta = new("beta", [NC, 4])
        cums, ex = new("cums", [2, NC, 8]), new("ex", [2, NC, 8])
        ncum, edk = new("ncum", [NC, 8]), new("edk", [NC, 8])
        ss8, ss16, ss32 = new("ss8", [8]), new("ss16", [16]), new("ss32", [NC, 8])
        A0 = cur[0]
        assert A0 + 21248 <= total, (A0, total)
        projT = at("projT", A0, [8, SEQ])
        vT = at("vT", A0 + 4096, [4, SEQ])
        zT = at("zT", A0 + 4096, [4, SEQ])
        convT = at("convT", A0 + 6144, [6, SEQ])
        convG = at("convG", A0 + 9216, [6, SEQ])
        cin = at("cin", A0 + 12288, [2, SEQ])
        vtok = at("vtok", A0 + 13312, [NC, DA_H, DA_V])
        prob = at("prob", A0 + 15360, [2, 2, SEQ])
        wgt = at("wgt", A0 + 17408, [2, SEQ])
        wgtT = at("wgtT", A0 + 18432, [2, SEQ])
        wsm_hi = at("wsm_hi", A0 + 15360, [KT, P], F32R)
        wsm_lo = at("wsm_lo", A0 + 16384, [KT, P], F32R)
        gates = at("gates", A0 + 17408, [SEQ])
        btok = at("btok", A0 + 2048, [NC, 2, P])
        ysq = at("ysq", A0 + 3072, [NC, 256])
        xd = at("xd", A0 + 12288, [NC, S_H, S_D])
        xdd = at("xdd", A0 + 13312, [NC, S_H, S_D])
        xskip = at("xskip", A0 + 14336, [NC, S_H, S_D])
        dec = at("dec", A0 + 15360, [2, 4, P])
        scoT = at("scoT", A0 + 16384, [2, 4, P])
        hst = at("hst", A0 + 17408, [2, S_H, S_D])
        ysd = at("ysd", A0 + 17920, [NC, S_H, S_D])
        ytmp = at("ytmp", A0 + 18944, [S_H, S_D])
        zst = at("zst", A0 + 19200, [NC, 256])
        tr3 = at("tr3", A0, [3, 2, SEQ])
        m1 = at("m1", A0, [NC, G_H, P])
        decG = at("decG", A0 + 3072, [2, 4, P])
        lvlA = at("lvlA", A0 + 3072, [2, 4, P])
        zgt = at("zgt", A0 + 4096, [NC, 256])
        attT = at("attT", A0 + 6144, [NC, G_H, P])
        tri_i = at("tri_i", A0 + 8192, [NC, G_H, P])
        tri_t = at("tri_t", A0 + 10240, [NC, G_H, P])
        qktok = at("qktok", A0 + 12288, [NC, 2, G_H, G_D])
        wTn = at("wTn", A0 + 12288, [2, SEQ])
        otok = at("otok", A0 + 13312, [NC, G_H, G_D])
        gvtok = at("gvtok", A0 + 14336, [NC, G_H, G_D])
        kE = at("kE", A0 + 15360, [NC, G_H, G_D])
        osq = at("osq", A0 + 15360, [NC, 256])
        kgt = at("kgt", A0 + 16384, [NC, G_H, G_D])
        qE = at("qE", A0 + 17408, [NC, G_H, G_D])
        gsq = at("gsq", A0, [NC, 2, G_H, G_D])
        aT = at("aT", A0 + 18432, [NC, G_H, P])
        stS = at("stS", A0 + 20480, [2, 2, G_D])
        vnew = at("vnew", A0 + 20736, [2, G_H, G_D])
        memh = at("memh", A0 + 16384, [KT, MEM], F32R)
        meml = at("meml", A0 + 18432, [KT, MEM], F32R)
        qcT = at("qcT", A0, [KT, SEQ])
        kvT = at("kvT", A0 + 4096, [16, MEM])
        vmt = at("vmt", A0 + 8192, [2, D_MODEL])
        pT = at("pT", A0 + 10240, [2, 2, SEQ])
        pc = at("pc", A0 + 12288, [3, 2, MEM])
        ksq = at("ksq", A0 + 13824, [2, MEM])
        f_hi = at("f_hi", A0, [FH, SEQ], F32R)
        f_lo = at("f_lo", A0 + 5632, [FH, SEQ], F32R)
        sgate = at("sgate", A0 + 11264, [SEQ])
        h2 = at("h2", A0 + 11776, [SEQ])
        sqsum = at("sqsum", A0 + 20480, [SEQ])
        xtok = at("xtok", A0, [NC, D_MODEL])
        mtok = at("mtok", A0 + 4096, [2, D_MODEL])
        mjunk = at("mjunk", A0 + 6144, [2, D_MODEL])

        bank = [ctx.enter_context(nc.psum_tensor(f"bank{i}", [P, 512], F32)) for i in range(4)]
        hi_banks = ctx.enter_context(nc.psum_tensor("hi_banks", [P, 4, 512], F32))
        bk = [b[:] for b in bank] + [hi_banks[:, i, :] for i in range(4)]

        def col(name, i=0, n=1):
            a = PC[name][0] + i
            return prm[:, a:a + n]

        def cst(name):
            return con[:, CC[name][0]:CC[name][1]]

        def lev(i):
            a = CC["lev"][0] + i * P
            return con[:, a:a + P]

        def bcl(ap, n):
            return ap.unsqueeze(len(ap.shape)).to_broadcast(list(ap.shape) + [n])

        def bcm(ap, n):
            return ap.unsqueeze(1).to_broadcast([ap.shape[0], n] + list(ap.shape[1:]))

        def halves(tile, v, side):
            s = 2 ** (v + 1)
            return tile.rearrange("p h (k a s) -> p h k a s", a=2, s=s)[:, :, :, side, :]

        def joined(c, v, side):
            s = 2 ** (v + 1)
            return bk[4 + c][:, side * 256:(side + 1) * 256].rearrange("p (h k s) -> p h k s", h=G_H, s=s)

        block = ctx.enter_context(nc.Block())

        @block.sync
        def _(sp_):
            sp_.dma_start(con[:], con_d).then_inc(s_const_in.sem, 16)
            sp_.dma_start(xtok[:], x_d.rearrange("(c p) d -> p c d", p=P)).then_inc(s_x_in.sem, 16)
            sp_.dma_start(mtok[:], mem_d.rearrange("(c p) d -> p c d", p=P)).then_inc(s_mem_in.sem, 16)

            with sp_.Fori(0, DEPTH) as l:

                sp_.wait_ge(s_h_lo.sem, s_h_lo.at(l, 0))
                sp_.dma_start(prm[:], prm_d[bass.ds(l, 1), :, :].rearrange("a p n -> p (a n)")).then_inc(s_prm_in.up(16), 16)
                sp_.dma_start(wsm[:].rearrange("p k n -> p (k n)"),
                              wsm_d[bass.ds(l, 1), :, :].rearrange("a p n -> p (a n)")).then_inc(s_prm_in.up(16), 16)

                def load(p, slot, src, width):
                    sp_.wait_ge(s_w_lo.sem, s_w_lo.at(l, 2 * p - 2))
                    sp_.dma_start(raw[:, slot, 0:2 * width], src.rearrange("a p n -> p (a n)")).then_inc(s_raw_in[slot].up(16), 16)

                def run(p0, n, src_d, per, q0, width):
                    trips[0] = n // 2
                    with sp_.Fori(0, n // 2) as i:
                        for j in range(2):
                            load(p0 + 2 * i + j, (p0 + j) % 2,
                                 src_d[bass.ds(l * per + 2 * i + (q0 + j), 1), :, :], width)
                    trips[0] = 1
                    if n % 2:
                        load(p0 + n - 1, (p0 + n - 1) % 2, src_d[bass.ds(l * per + (q0 + n - 1), 1), :, :], width)

                p = qa = B_FF // 2
                run(0, p, wa_d, PAIRS_A, 0, WA)
                for half in range(2):
                    run(p, N_GU // 2, wa_d, PAIRS_A, qa, WA)
                    p, qa = p + N_GU // 2, qa + N_GU // 2
                    run(p, N_DN // 2, wd_d, PAIRS_D, half * N_DN // 2, WD)
                    p += N_DN // 2
            for c in range(NC):
                sp_.wait_ge(s_y_ready.sem, 2 * c + 2)
                sp_.dma_start(out_d.rearrange("(c p) d -> c p d", p=P)[c], xtok[:, c, :]).then_inc(s_y_out.sem, 16)
            sp_.wait_ge(s_y_out.sem, 16 * NC)

        @block.gpsimd
        def _(pool):
            with pool.Fori(0, DEPTH) as l:
                for c in range(NC):
                    pool.wait_ge(s_gt_ev.sem, s_gt_ev.at(l, 2 * c + 1))
                    pool.tensor_tensor(gsq[:, c], qktok[:, c], qktok[:, c], ALU.mult).then_inc(s_gsq.up(), 1)
                pool.wait_ge(s_gn_n.sem, s_gn_n.at(l, 1))
                pool.tensor_tensor(kE[:], qktok[:, :, 1], bcl(ex[:, 0, :, 4:8], G_D), ALU.mult).then_inc(s_kdec.up(), 1)
                pool.tensor_tensor(kgt[:], qktok[:, :, 1], bcl(edk[:, :, 4:8], G_D), ALU.mult).then_inc(s_kdec.up(), 1)
                for c in range(NC):
                    pool.wait_ge(s_gd_at.sem, s_gd_at.at(l, c + 1))
                    pool.tensor_tensor(tri_t[:, c], aT[:, c], bcm(lev(0), G_H), ALU.mult).then_inc(s_ti_m.up(), 1)
                for n in range(NJ):
                    v, c = n // NC, n % NC
                    if n >= 2:
                        pool.wait_ge(s_m1_mm.sem, s_m1_mm.at(l, n - 1))
                    pool.tensor_tensor(lvlA[:, c % 2], aT[:, c], bcm(lev(v + 1), G_H), ALU.mult).then_inc(s_lvl.up(), 1)
                for g in range(3):
                    for k in range(KT - 2):
                        pool.wait_ge(s_nrm_sq.sem, s_nrm_sq.at(l, g * KT + k + 1))
                        if k == 0:
                            pool.wait_ge(s_nrm_mm.sem, s_nrm_mm.at(l, 3 * g))
                            pool.tensor_tensor(sqsum[:].rearrange("p (c n) -> p c n", c=NC), sq[:, 0, :].rearrange("p (c n) -> p c n", c=NC),
                                               bcm(cst("ones"), NC), ALU.mult).then_inc(s_nrm_acc.up(), 1)
                        else:
                            pool.wait_ge(s_nrm_acc.sem, s_nrm_acc.at(l, g * (KT - 2) + k))
                            pool.tensor_tensor(sqsum[:], sqsum[:], sq[:, k % 2, :], ALU.add).then_inc(s_nrm_acc.up(), 1)

        def pair_loop(eng, p0, n, body):
            rounds = (n - 1) // 2
            if rounds:
                trips[0] = rounds
                with eng.Fori(0, rounds) as i:
                    for j in (1, 2):
                        body(2 * i + j, (p0 + j) % 2, (p0 + j) // 2 + 1 + i, 2 * i + (j - 1), (j - 1) % 2)
                trips[0] = 1
            if (n - 1) % 2:
                body(n - 1, (p0 + n - 1) % 2, (p0 + n - 1) // 2 + 1, n - 2, n % 2)

        @block.scalar
        def _(act):
            def link(l, ins):
                ins.then_inc(s_act_step.up(), 1)
                act.wait_ge(s_act_step.sem, s_act_step.at(l, s_act_step.n))

            act.preload_act_table_set(LN_EXP)
            act.wait_ge(s_mem_in.sem, 16)
            act.wait_ge(s_setup.sem, 1)
            for c in range(2):
                act.activation(mjunk[:, c, :], mtok[:, c, :], ACT.Square,
                               accum_out=ss8[:, c:c + 1]).then_inc(s_mem_sq.sem, 1)
            act.wait_ge(s_mem_sq.sem, 2)
            act.activation(ss8[:, 2:4], ss8[:, 0:2], ACT.Ln, bias=eps[:, 0:1], scale=1.0 / D_MODEL
                           ).then_inc(s_mem_sq.sem, 1)
            act.wait_ge(s_mem_sq.sem, 3)
            act.activation(ss8[:, 4:6], ss8[:, 2:4], ACT.Exp, scale=-0.5).then_inc(s_mem_rs.sem, 1)

            act.wait_ge(s_x_turned.sem, 8)
            for k in range(KT):
                if k >= 2:
                    act.wait_ge(s_nrm_mm.sem, k - 1)
                act.activation(sq[:, k % 2, :], xT[:, k, :], ACT.Square).then_inc(s_nrm_sq.sem, 1)

            with act.Fori(0, DEPTH) as l:

                def rsqrt(out, in_, scale, e, done):
                    link(l, act.activation(out, in_, ACT.Ln, bias=eps[0:in_.shape[0], e:e + 1], scale=scale))
                    act.activation(out, out, ACT.Exp, scale=-0.5).then_inc(done.up(), 1)

                def split_hi(n, w=SEQ, src=None, free=None):
                    if free is not None:
                        act.wait_ge(s_blk_done.sem, s_blk_done.at(l, free))
                    if src is None:
                        act.wait_ge(s_h_f32.sem, s_h_f32.at(l, n + 1 - (KT if n >= H_FF else 0)))
                        src = htmp[:, n % 2, 0:w]
                    act.activation(h_hi[:, n % KT, 0:w], src, ACT.Copy).then_inc(s_h_hi.up(), 1)

                def weights_hi(b, K=KT):
                    slot = (b // 2) % 2
                    act.wait_ge(s_blk_done.sem, s_blk_done.at(l, b - 1))
                    if b % 2 == 0:
                        act.wait_ge(s_raw_in[slot].sem, s_raw_in[slot].at(l, 16 * (b // 4 + 1)))
                    act.activation(w_hi[b % 2][:, 0:K, :].rearrange("p k n -> p (k n)"),
                                   raw[:, slot, (b % 2) * K * P:(b % 2 + 1) * K * P], ACT.Copy).then_inc(s_w_hi.up(), 1)

                def dense(b0, n, K, evac, then=None):
                    width = K * P

                    def body(q, slot, loads, i, par):
                        for j in range(2):
                            act.wait_ge(s_blk_done.sem, s_blk_done.at(l, 2 * q + (b0 + j - 1)))
                            if j == 0:
                                act.wait_ge(s_raw_in[slot].sem, s_raw_in[slot].at(l, 16 * loads))
                            act.activation(w_hi[j][:, 0:K, :].rearrange("p k n -> p (k n)"), raw[:, slot, j * width:(j + 1) * width], ACT.Copy).then_inc(s_w_hi.up(), 1)
                            if evac is not None:
                                evac(2 * i + j, j, i, par)
                    pair_loop(act, b0 // 2, n // 2, body)
                    for j in range(2):
                        if then is not None:
                            weights_hi(b0 + n + j, then)
                        if evac is not None:
                            evac(n - 2 + j, j, n // 2 - 1, (n // 2 - 1) % 2)

                def copy_out(b0, dst, w):
                    def evac(o, j, i, par):
                        act.wait_ge(s_blk_done.sem, s_blk_done.at(l, o + (b0 + 1)))
                        act.activation(dst[:, bass.ds(o, 1), 0:w].rearrange("p a n -> p (a n)"), bk[j][:, 0:w], ACT.Copy).then_inc(s_evac_a.up(), 1)
                    return evac

                def x_squares(g, e0):
                    def evac(o, j, i, par):
                        act.wait_ge(s_evac_d.sem, s_evac_d.at(l, o + (e0 + 1)))
                        act.wait_ge(s_nrm_acc.sem, s_nrm_acc.at(l, o + (g * (KT - 2) - 1)))
                        act.activation(sq[:, j, :], xT[:, bass.ds(o, 1), :].rearrange("p a n -> p (a n)"), ACT.Square).then_inc(s_nrm_sq.up(), 1)
                    return evac

                def norm_rs(g):
                    act.wait_ge(s_nrm_mm.sem, s_nrm_mm.at(l, (g + 1) * 3))
                    rsqrt(rs[:, 0, :], bk[2], 1.0 / D_MODEL, 0, s_nrm_rs)

                for b in range(2):
                    weights_hi(b)
                norm_rs(-1)
                act.wait_ge(s_prm_in.sem, s_prm_in.at(l, 32))
                act.wait_ge(s_wsm_0.sem, s_wsm_0.at(l, 2))
                act.activation(wsm_hi[:, :, 0:12], wsm[:], ACT.Copy).then_inc(s_wsm_hi.up(), 1)
                for k in range(KT):
                    split_hi(H_IN + k, free=None if k else 0)
                act.wait_ge(s_lam_sum.sem, s_lam_sum.at(l, 1))
                act.activation(lexp[:], lsum[:], ACT.Exp).then_inc(s_lam_exp.up(), 1)
                act.activation(ag[:], col("alog", 0, 8), ACT.Exp).then_inc(s_lam_exp.up(), 1)

                def qk_out(o):
                    j = o % 2
                    act.wait_ge(s_blk_done.sem, s_blk_done.at(l, o + 1))
                    if o >= 2:
                        act.wait_ge(s_qk_ss.sem, s_qk_ss.at(l, o - 1))
                    act.activation(sq[:, j, :], bk[j], ACT.Square).then_inc(s_qk_sq.up(), 1)
                    act.activation(projT[:, o, :], bk[j], ACT.Copy).then_inc(s_evac_a.up(), 1)

                def qk_rs(o):
                    j = o % 2
                    act.wait_ge(s_qk_ss.sem, s_qk_ss.at(l, o + 1))
                    if o >= 2:
                        act.wait_ge(s_qk_n.sem, s_qk_n.at(l, o - 1))
                    rsqrt(rs[:, j, :], bk[2 + j], 1.0 / DA_D, 0, s_qk_rs)

                def in_out(b):
                    act.wait_ge(s_blk_done.sem, s_blk_done.at(l, b + 1))
                    t = b - N_QK
                    if t < N_V:
                        dst = vT[:, t, :]
                    elif t < N_V + N_CONV:
                        dst = cin[:, t % 2, :]
                        if t - N_V >= 2:
                            act.wait_ge(s_conv.sem, s_conv.at(l, t - N_V - 1))
                    else:
                        if t == N_V + N_CONV:
                            act.wait_ge(s_v_tr.sem, s_v_tr.at(l, NC))
                        dst = zT[:, t - N_V - N_CONV, :]
                    act.activation(dst, bk[b % 2], ACT.Copy).then_inc(s_evac_a.up(), 1)

                def v_out(c):
                    act.wait_ge(s_v_tr.sem, s_v_tr.at(l, c + 1))
                    act.activation(vtok[:, c].rearrange("p h e -> p (h e)"), bk[2], ACT.Copy).then_inc(s_v_ev.up(), 1)

                def da_exp(n):
                    nk = (n % NC + 1) * P
                    act.wait_ge(s_da_nm.sem, s_da_nm.at(l, n + 1))
                    if n >= 2:
                        act.wait_ge(s_da_w.sem, s_da_w.at(l, n - 1))
                    for c in range(2):
                        act.activation(prob[:, n % 2, c, 0:nk], bk[4 + 2 * (n % 2) + c][:, 0:nk], ACT.Exp,
                                       bias=mx[:, n, c:c + 1], scale=DA_D ** -0.5,
                                       accum_out=sm[:, n, c:c + 1]).then_inc(s_da_p.up(), 1)

                def da_turned(n):
                    nk = (n % NC + 1) * P
                    act.wait_ge(s_da_t.sem, s_da_t.at(l, n + 1))
                    if n >= 2:
                        act.wait_ge(s_da_pv.sem, s_da_pv.at(l, n - 1))
                    act.activation(wgtT[:, n % 2, 0:nk], bk[2][:, 0:nk], ACT.Copy).then_inc(s_da_wt.up(), 1)

                def da_out(h):
                    act.wait_ge(s_da_pv.sem, s_da_pv.at(l, NC * (h + 1)))
                    act.activation(projT[:, h, :], bk[3], ACT.Copy).then_inc(s_da_o.up(), 1)

                for b in range(2, N_QK + N_V + 1):
                    weights_hi(b)
                    if b - 2 < N_QK:
                        qk_out(b - 2)
                    else:
                        in_out(b - 2)
                    if 0 <= b - 3 < N_QK:
                        qk_rs(b - 3)
                    if b == 8:
                        act.wait_ge(s_g_v.sem, s_g_v.at(l, 2))
                        link(l, act.activation(g1[:], gv[:], ACT.Abs))
                        link(l, act.activation(g1[:], g1[:], ACT.Exp, scale=-1.0))
                        act.activation(g1[:], g1[:], ACT.Ln, bias=1.0).then_inc(s_g_ln.up(), 1)
                        act.activation(gb[:], gb[:], ACT.Exp, scale=-1.0).then_inc(s_g_ln.up(), 1)
                act.wait_ge(s_g_dk.sem, s_g_dk.at(l, 1))
                act.activation(ex[:].rearrange("p a c h -> p (a c h)"), cums[:].rearrange("p a c h -> p (a c h)"), ACT.Exp).then_inc(s_g_ex.up(), 1)
                act.activation(edk[:], edk[:], ACT.Exp).then_inc(s_g_edk.up(), 1)

                def conv_silu(t):
                    act.wait_ge(s_conv.sem, s_conv.at(l, t + 1))
                    c = convT[:, t, :] if t < 6 else convG[:, t - 6, :]
                    act.activation(c, c, ACT.Silu).then_inc(s_convs.up(), 1)

                for s in range(ND + 3):
                    b = N_QK + N_V + s
                    if b - 1 < N_IN:
                        in_out(b - 1)
                    if b + 1 < N_IN:
                        weights_hi(b + 1)
                    if 0 < s <= NC:
                        v_out(s - 1)
                    if 0 < s <= ND:
                        da_exp(s - 1)
                    if 0 <= s - 2 < ND:
                        da_turned(s - 2)
                    if s >= 3 and (s - 3) % NC == NC - 1:
                        da_out((s - 3) // NC)
                    if s == ND:
                        act.preload_act_table(ACT.Silu)
                        for t in range(3):
                            conv_silu(t)
                    if s == ND + 1:
                        for t in range(3, 6):
                            conv_silu(t)
                for c in range(NC):
                    act.wait_ge(s_s_tr.sem, s_s_tr.at(l, c + 1))
                    act.activation(btok[:, c].rearrange("p g n -> p (g n)"), bk[4 + c % 2][:, 0:256], ACT.Copy).then_inc(s_s_ev.up(), 1)
                    if c == 1:
                        for t in range(6, 9):
                            conv_silu(t)
                act.wait_ge(s_da_o.sem, s_da_o.at(l, DA_H))
                for h in range(2):
                    act.activation(sq[:, h % 2, :], projT[:, h, :], ACT.Square).then_inc(s_on_sq.up(), 1)
                for t in range(9, N_CONV):
                    conv_silu(t)
                act.wait_ge(s_evac_a.sem, s_evac_a.at(l, N_IN))
                for t in range(4):
                    act.activation(zT[:, t, :], zT[:, t, :], ACT.Silu).then_inc(s_zs.up(), 1)
                act.preload_act_table_set(LN_EXP)

                def s_dec_exp(c):
                    act.wait_ge(s_s_d.sem, s_s_d.at(l, c + 1))
                    if c >= 2:
                        act.wait_ge(s_s_st.sem, s_s_st.at(l, c - 1))
                    for h in range(S_H):
                        act.activation(dec[:, c % 2, h, :], bk[4 + c % 2][:, h * P:(h + 1) * P], ACT.Exp, bias=ncum[:, c, h:h + 1]).then_inc(s_s_dec.up(), 1)

                for h in range(DA_H):
                    act.wait_ge(s_on_ss.sem, s_on_ss.at(l, h + 1))
                    if h >= 2:
                        act.wait_ge(s_h_f32.sem, s_h_f32.at(l, H_MIX + h - 1))
                    rsqrt(rs[:, h % 2, :], bk[6 + h % 2], 1.0 / DA_V, 0, s_on_rs)
                    if h + 2 < DA_H:
                        act.activation(sq[:, h % 2, :], projT[:, h + 2, :], ACT.Square).then_inc(s_on_sq.up(), 1)
                        s_dec_exp(h)
                    else:
                        i = h - 2
                        act.wait_ge(s_z_tr.sem, s_z_tr.at(l, i + 1))
                        act.activation(zst[:, 2 * i:2 * i + 2].rearrange("p c n -> p (c n)"), bk[i], ACT.Copy).then_inc(s_z_ev.up(), 1)
                    split_hi(H_MIX + h)
                for c in range(2, NC):
                    s_dec_exp(c)
                for c in range(NC):
                    act.wait_ge(s_gt_tr.sem, s_gt_tr.at(l, c + 1))
                    act.activation(qktok[:, c].rearrange("p a h d -> p (a h d)"), bk[2 + c % 2], ACT.Copy).then_inc(s_gt_ev.up(), 1)
                    act.activation(gvtok[:, c].rearrange("p h d -> p (h d)"), bk[4 + c % 2][:, 0:256], ACT.Copy).then_inc(s_gt_ev.up(), 1)
                act.wait_ge(s_s_ss.sem, s_s_ss.at(l, 1))
                rsqrt(ss8[:], ss8[:], 1.0 / P, 0, s_s_rs)
                act.wait_ge(s_gn_ss.sem, s_gn_ss.at(l, 1))
                rsqrt(ss32[:], ss32[:], 1.0, 0, s_gn_rs)
                for f in range(2):
                    split_hi(H_MIX + 4 + f)

                for i in range(6):
                    act.wait_ge(s_g3_tr.sem, s_g3_tr.at(l, i + 1))
                    act.activation(tr3[:, i // 2, i % 2, :], bk[2 + i % 2], ACT.Copy).then_inc(s_g3_ev.up(), 1)
                for c in range(NC):
                    act.wait_ge(s_gd_d.sem, s_gd_d.at(l, c + 1))
                    if c >= 2:
                        act.wait_ge(s_gd_at.sem, s_gd_at.at(l, c - 1))
                    for h in range(G_H):
                        act.activation(decG[:, c % 2, h, :], bk[c % 2][:, h * P:(h + 1) * P], ACT.Exp, bias=ncum[:, c, 4 + h:5 + h]).then_inc(s_gd_dec.up(), 1)
                for c in range(NC):
                    act.wait_ge(s_ti_tr.sem, s_ti_tr.at(l, c + 1))
                    act.activation(tri_i[:, c].rearrange("p h n -> p (h n)"), bk[2 + c % 2], ACT.Copy).then_inc(s_ti_ev.up(), 1)
                for b in range(B_OUT, B_OUT + 2):
                    weights_hi(b)
                for n in range(NJ):
                    act.wait_ge(s_m1_mm.sem, s_m1_mm.at(l, n + 1))
                    if n >= NC:
                        act.wait_ge(s_tx_mm.sem, s_tx_mm.at(l, n - NC + 1))
                    act.activation(m1[:, n % NC].rearrange("p h n -> p (h n)"), bk[2 + n % 2], ACT.Copy).then_inc(s_m1_ev.up(), 1)
                for p_ in range(2):
                    act.wait_ge(s_w_mm.sem, s_w_mm.at(l, p_ + 1))
                    act.activation(wTn[:, p_, :], bk[2 + p_], ACT.Copy, scale=-1.0).then_inc(s_w_ev.up(), 1)
                for c in range(NC):
                    if c < 2:
                        act.wait_ge(s_zg_tr.sem, s_zg_tr.at(l, c + 1))
                        act.activation(zgt[:, 2 * c:2 * c + 2].rearrange("p c n -> p (c n)"), bk[2 + c], ACT.Copy).then_inc(s_zg_ev.up(), 1)
                    act.wait_ge(s_o_mm.sem, s_o_mm.at(l, c + 1))
                    act.activation(otok[:, c].rearrange("p (a r) d -> p r a d", r=2), hi_banks[:, 2:4, 0:P].rearrange("p r (a d) -> p r a d", a=2), ACT.Copy).then_inc(s_o_ev.up(), 1)
                act.wait_ge(s_go_ss.sem, s_go_ss.at(l, 1))
                rsqrt(ss16[:], ss16[:], 1.0 / G_D, 0, s_go_rs)
                for f in range(2):
                    split_hi(H_MIX + 6 + f)

                def mem_hi(o, j, i, par):
                    x_sq(o, j, i, par)
                    act.wait_ge(s_h_f32.sem, s_h_f32.at(l, o + (H_MEM + 1)))
                    act.activation(memh[:, bass.ds(o, 1), :].rearrange("p a n -> p (a n)"), htmp[:, j, 0:MEM], ACT.Copy).then_inc(s_h_hi.up(), 1)

                x_sq = x_squares(0, ED_OUT)
                dense(B_OUT, N_OUT, KT, mem_hi, then=KT)
                norm_rs(0)

                def kv_out(o, j, i, par):
                    kv_copy(o, j, i, par)
                    if j == 1:
                        act.wait_ge(s_h_f32.sem, s_h_f32.at(l, i + (H_X + 1)))
                        act.activation(h_hi[:, bass.ds(i, 1), :].rearrange("p a n -> p (a n)"), htmp[:, par, :], ACT.Copy).then_inc(s_h_hi.up(), 1)

                kv_copy = copy_out(B_KV, kvT, MEM)
                dense(B_KV, N_KV, KT, kv_out, then=KT)
                def cq_out(t):
                    act.wait_ge(s_blk_done.sem, s_blk_done.at(l, B_CQ + t + 1))
                    if t >= 2:
                        act.wait_ge(s_cq_ss.sem, s_cq_ss.at(l, t - 1))
                    act.activation(sq[:, t % 2, :], bk[t % 2], ACT.Square).then_inc(s_cq_sq.up(), 1)
                    act.activation(qcT[:, t, :], bk[t % 2], ACT.Copy).then_inc(s_evac_a.up(), 1)

                def ck_squares(m):
                    if m == 0:
                        act.wait_ge(s_evac_a.sem, s_evac_a.at(l, EA_CQ))
                    else:
                        act.wait_ge(s_ck_ss.sem, s_ck_ss.at(l, m))
                    for f in range(2):
                        act.activation(ksq[:, f, :], kvT[:, 2 * m + f, :], ACT.Square).then_inc(s_ck_sq.up(), 1)

                def ck_rs(m):
                    act.wait_ge(s_ck_ss.sem, s_ck_ss.at(l, m + 1))
                    if m:
                        act.wait_ge(s_ck_n.sem, s_ck_n.at(l, 2 * m))
                    rsqrt(rs[:, 0, 0:MEM], bk[3][:, 0:MEM], 1.0 / X_D, 0, s_ck_rs)

                def cq_rs(m):
                    act.wait_ge(s_cq_ss.sem, s_cq_ss.at(l, 2 * m + 2))
                    if m:
                        act.wait_ge(s_cq_n.sem, s_cq_n.at(l, 2 * m))
                    rsqrt(rs[:, 1, :], bk[2], 1.0 / X_D, 0, s_cq_rs)

                def cv_out(g):
                    act.wait_ge(s_cv_tr.sem, s_cv_tr.at(l, g + 1))
                    act.activation(vmt[:, g // 2, (g % 2) * 512:(g % 2 + 1) * 512], bk[4 + g], ACT.Copy).then_inc(s_cv_ev.up(), 1)

                for t in range(N_CQ + 3):
                    if t < N_CQ:
                        if t % 2 == 0:
                            ck_squares(t // 2)
                    if 0 <= t - 3 < N_CQ and (t - 3) % 2 == 1:
                        cq_rs((t - 3) // 2)
                    if t >= 1 and t - 1 < N_CQ:
                        weights_hi(B_CQ + t + 1)
                        cq_out(t - 1)
                    if t < N_CQ and t % 2 == 1:
                        ck_rs(t // 2)
                    if t >= 2 and t % 2 == 0 and t // 2 <= 4:
                        cv_out(t // 2 - 1)

                def c_exp(n):
                    act.wait_ge(s_c_nm.sem, s_c_nm.at(l, n + 1))
                    if n >= 3:
                        act.wait_ge(s_c_t.sem, s_c_t.at(l, n - 2))
                    for i in range(2):
                        act.activation(pc[:, n % 3, i, :], bk[4 + n % 2][:, i * MEM:(i + 1) * MEM], ACT.Exp, bias=mx[:, n, i:i + 1], scale=X_D ** -0.5, accum_out=sm[:, n, i:i + 1]).then_inc(s_c_p.up(), 1)

                def c_turned(n):
                    h, qp = n // 2, n % 2
                    act.wait_ge(s_c_t.sem, s_c_t.at(l, n + 1))
                    if h >= 2 and qp == 0:
                        act.wait_ge(s_c_pv.sem, s_c_pv.at(l, 2 * (h - 1)))
                    act.activation(pT[:, h % 2, :, qp * 256:(qp + 1) * 256], bk[6 + n % 2].rearrange("p (m q) -> p m q", m=2), ACT.Copy).then_inc(s_c_pt.up(), 1)

                def c_out(h):
                    for e in range(2):
                        act.wait_ge(s_c_pv.sem, s_c_pv.at(l, 2 * h + e + 1))
                        split_hi(H_CA + 2 * h + e, src=bk[e], free=B_CQ + N_CQ)

                for n in range(N_CA + 3):
                    if n < N_CA:
                        c_exp(n)
                    if 0 <= n - 2 < N_CA:
                        c_turned(n - 2)
                    if n >= 4 and n % 2 == 0:
                        c_out(n // 2 - 2)
                dense(B_CO, N_CO, KT, x_squares(1, ED_CO), then=KT)
                norm_rs(1)
                for k in range(KT):
                    split_hi(H_FF + k, free=B_CO + N_CO)
                act.preload_act_table(ACT.Silu)
                b = B_FF
                for half in range(2):

                    f0 = half * FH

                    def body(q, slot, loads, i, par, b=b, f0=f0):
                        for j in range(2):
                            act.wait_ge(s_blk_done.sem, s_blk_done.at(l, 2 * q + (b + j - 1)))
                            if j == 0:
                                act.wait_ge(s_raw_in[slot].sem, s_raw_in[slot].at(l, 16 * loads))
                            act.activation(w_hi[j][:, 0:KT, :].rearrange("p k n -> p (k n)"), raw[:, slot, j * WA:(j + 1) * WA], ACT.Copy).then_inc(s_w_hi.up(), 1)
                            ffn_out(i, j, b, f0)

                    def ffn_out(i, j, b, f0):
                        if j == 0:
                            act.wait_ge(s_blk_done.sem, s_blk_done.at(l, 2 * i + (b + 1)))
                            act.wait_ge(s_f_h2.sem, s_f_h2.at(l, i + f0))
                            act.activation(sgate[:], bk[0], ACT.Silu).then_inc(s_f_sg.up(), 1)
                        else:
                            act.wait_ge(s_f_h2.sem, s_f_h2.at(l, i + (f0 + 1)))
                            act.activation(f_hi[:, bass.ds(i, 1), :].rearrange("p a n -> p (a n)"), h2[:], ACT.Copy).then_inc(s_f_hi.up(), 1)
                    pair_loop(act, b // 2, FH, body)
                    for j in range(2):
                        weights_hi(b + N_GU + j, FH)
                        ffn_out(FH - 1, j, b, f0)
                    b += N_GU
                    if half == 0:
                        dense(b, N_DN, FH, None, then=KT)
                    else:
                        act.preload_act_table_set(LN_EXP)
                        dense(b, N_DN, FH, x_squares(2, ED_DN + N_DN))
                    b += N_DN

            for c in range(NC):
                for i in range(2):
                    n = 2 * c + i
                    act.wait_ge(s_y_tr.sem, n + 1)
                    act.activation(xtok[:, c, i * 512:(i + 1) * 512], bk[2 + n % 2], ACT.Copy
                                   ).then_inc(s_y_ready.sem, 1)

        @block.vector
        def _(dve):
            def tt(out, a, b, op):
                return dve.tensor_tensor(out, a, b, op)

            def stt(out, a, s, b, op0, op1):
                return dve.scalar_tensor_tensor(out=out, in0=a, scalar=s, in1=b, op0=op0, op1=op1)

            MUL, ADD, SUB = ALU.mult, ALU.add, ALU.subtract

            def first(ins):
                ins.then_inc(s_v_setup.sem, 1)
                setup_n[0] += 1
                dve.wait_ge(s_v_setup.sem, setup_n[0])
            setup_n = [0]
            first(dve.memset(eps[:, 0:1], EPS))
            dve.memset(eps[:, 1:2], 0.0).then_inc(s_setup.sem, 1)
            for i, name in enumerate([n for n in START for _ in range(START[n])]):
                dve.memset(seed[:, i:i + 1], 0.0).then_inc(signals[name].sem, 1)
            dve.wait_ge(s_const_in.sem, 16)
            first(dve.tensor_copy(idb[:], cst("idn")))
            first(dve.tensor_copy(negq[:], cst("negq")))
            dve.tensor_copy(negd[:], cst("negd")).then_inc(s_c_bf.sem, 1)
            for n in range(8):
                dve.wait_ge(s_x_tr.sem, n + 1)
                c, i = n // 2, n % 2
                dve.tensor_copy(xT[:, 4 * i:4 * i + 4, c * P:(c + 1) * P],
                                bk[2 + n % 2].rearrange("p (k n) -> p k n", k=4)).then_inc(s_x_turned.sem, 1)
            dve.wait_ge(s_mem_rs.sem, 1)
            for c in range(2):
                dve.tensor_scalar(mjunk[:, c, :], mtok[:, c, :], ss8[:, 4 + c:5 + c], None, MUL
                                  ).then_inc(s_mem_n.sem, 1)
            for n in range(4):
                dve.wait_ge(s_m_tr.sem, n + 1)
                c, i = n // 2, n % 2
                dve.tensor_copy(memn[:, 4 * i:4 * i + 4, c * P:(c + 1) * P],
                                bk[4 + n % 2].rearrange("p (k n) -> p k n", k=4)).then_inc(s_m_ev.sem, 1)
            dve.wait_ge(s_m_ev.sem, 4)
            dve.wait_ge(s_x_turned.sem, 8)

            with dve.Fori(0, DEPTH) as l:
                def own(ins, s):
                    ins.then_inc(s.up(), 1)
                    dve.wait_ge(s.sem, s.at(l, s.n))

                def link(ins):
                    own(ins, s_dve_step)

                def split_lo(n, w=SEQ, src=None):
                    dve.wait_ge(s_h_hi.sem, s_h_hi.at(l, n + 1))
                    tt(h_lo[:, n % KT, 0:w], htmp[:, n % 2, 0:w] if src is None else src,
                             h_hi[:, n % KT, 0:w].bitcast(F32), SUB).then_inc(s_h_lo.up(), 1)

                def free_htmp(n):
                    if n >= 2:
                        dve.wait_ge(s_h_lo.sem, s_h_lo.at(l, n - 1))
                    else:
                        dve.wait_ge(s_h_lo.sem, s_h_lo.at(l, 0))

                def scaled(first_n, count, make):
                    for k in range(count):
                        free_htmp(first_n + k)
                        make(k, htmp[:, (first_n + k) % 2, :]).then_inc(s_h_f32.up(), 1)
                        if k >= 1:
                            split_lo(first_n + k - 1)
                    split_lo(first_n + count - 1)

                def norm_out(idx, first_n, g):
                    dve.wait_ge(s_nrm_rs.sem, s_nrm_rs.at(l, idx + 1))
                    scaled(first_n, KT, lambda k, o: stt(o, xT[:, k, :], col(g, k), rs[:, 0, :], MUL, MUL))

                def weights_lo(b, K=KT):
                    dve.wait_ge(s_w_hi.sem, s_w_hi.at(l, b + 1))
                    tt(w_lo[b % 2][:, 0:K, :].rearrange("p k n -> p (k n)"),
                       raw[:, (b // 2) % 2, (b % 2) * K * P:(b % 2 + 1) * K * P],
                       w_hi[b % 2][:, 0:K, :].rearrange("p k n -> p (k n)").bitcast(F32), SUB).then_inc(s_w_lo.up(), 1)

                def dense(b0, n, K, evac, then=None):
                    width = K * P

                    def body(q, slot, loads, i, par):
                        for j in range(2):
                            dve.wait_ge(s_w_hi.sem, s_w_hi.at(l, 2 * q + (b0 + j + 1)))
                            tt(w_lo[j][:, 0:K, :].rearrange("p k n -> p (k n)"),
                                     raw[:, slot, j * width:(j + 1) * width],
                                     w_hi[j][:, 0:K, :].rearrange("p k n -> p (k n)").bitcast(F32), SUB).then_inc(s_w_lo.up(), 1)
                            if evac is not None:
                                evac(2 * i + j, j, i, par)
                    pair_loop(dve, b0 // 2, n // 2, body)
                    for j in range(2):
                        if evac is not None:
                            evac(n - 2 + j, j, n // 2 - 1, (n // 2 - 1) % 2)
                        if then is not None:
                            weights_lo(b0 + n + j, then)

                def add_out(b0):
                    def evac(o, j, i, par):
                        dve.wait_ge(s_blk_done.sem, s_blk_done.at(l, o + (b0 + 1)))
                        dst = xT[:, bass.ds(o, 1), :].rearrange("p a n -> p (a n)")
                        tt(dst, bk[j], dst, ADD).then_inc(s_evac_d.up(), 1)
                    return evac

                for half in (wsm_hi, wsm_lo):
                    dve.tensor_scalar(half[:, 0:4, :].rearrange("p k n -> p (k n)"), con[:, 0:512], 0.0, None, MUL).then_inc(s_dve_step.up(), 1)
                    dve.tensor_scalar(half[:, 4:8, :].rearrange("p k n -> p (k n)"), con[:, 0:512], 0.0, None, MUL).then_inc(s_wsm_0.up(), 1)
                dve.wait_ge(s_dve_step.sem, s_dve_step.at(l, s_dve_step.n))
                dve.wait_ge(s_wsm_0.sem, s_wsm_0.at(l, 2))
                for b in range(2):
                    weights_lo(b)
                dve.wait_ge(s_wsm_hi.sem, s_wsm_hi.at(l, 1))
                tt(wsm_lo[:, :, 0:12], wsm[:], wsm_hi[:, :, 0:12].bitcast(F32), SUB).then_inc(s_wsm_lo.up(), 1)
                dve.wait_ge(s_prm_in.sem, s_prm_in.at(l, 32))
                norm_out(0, H_IN, "g_mix")
                lv = col("lamv", 0, 256).rearrange("p (a b n) -> p a b n", a=2, b=2)
                link(tt(lp[:], lv[:, :, 0, :], lv[:, :, 1, :], MUL))
                dve.reduce_sum(lsum[:], lp[:], AX.X).then_inc(s_lam_sum.up(), 1)
                link(tt(sg1[:], col("subg"), col("onemin"), MUL))
                dve.wait_ge(s_lam_exp.sem, s_lam_exp.at(l, 1))
                link(tt(nlam[:, 0:1], lexp[:, 1:2], lexp[:, 0:1], SUB))
                link(tt(nlam[:, 1:2], nlam[:, 0:1], col("laminit"), SUB))

                def qk_scale(o):
                    dve.wait_ge(s_qk_rs.sem, s_qk_rs.at(l, o + 1))
                    t = projT[:, o, :]
                    stt(t, t, col("qkg", o), rs[:, o % 2, :], MUL, MUL).then_inc(s_qk_n.up(), 1)

                for b in range(2, N_QK + N_V + 1):
                    weights_lo(b)
                    if b == 2:
                        dve.wait_ge(s_g_mm.sem, s_g_mm.at(l, 1))
                        dve.tensor_copy(gates[:], bk[7]).then_inc(s_g_out.up(), 1)
                    if 0 <= b - 3 < N_QK:
                        qk_scale(b - 3)
                    if b == 7:
                        dve.wait_ge(s_g_ps.sem, s_g_ps.at(l, 1))
                        gp = bk[7].rearrange("p (c n) -> p c n", c=NC)
                        tt(gv[:], gp[:, :, 0:8], bcm(col("dtb", 0, 8), NC), ADD).then_inc(s_g_v.up(), 1)
                        dve.tensor_copy(gb[:], gp[:, :, 8:12]).then_inc(s_g_v.up(), 1)
                    if b == 9:
                        dve.wait_ge(s_g_ln.sem, s_g_ln.at(l, 2))
                        link(stt(sp[:], gv[:], 0.0, g1[:], ALU.max, ADD))
                        stt(ga[:], sp[:], -1.0, bcm(ag[:], NC), MUL, MUL).then_inc(s_g_a.up(), 1)
                        link(dve.tensor_scalar(gb[:], gb[:], 1.0, None, ADD))
                        link(dve.reciprocal(beta[:], gb[:]))
                dve.wait_ge(s_g_cum.sem, s_g_cum.at(l, 1))
                link(dve.tensor_copy(cums[:].rearrange("p a c h -> p (a c h)"), bk[7][:, 64:128]))
                link(dve.tensor_scalar(ncum[:], cums[:, 0], -1.0, None, MUL))
                tt(edk[:], cums[:, 1], cums[:, 0], SUB).then_inc(s_g_dk.up(), 1)

                def da_max(n):
                    nk = (n % NC + 1) * P
                    i = n % 2
                    dve.wait_ge(s_da_s.sem, s_da_s.at(l, n + 1))
                    link(dve.reduce_max(rr[:, n, :], hi_banks[:, 2 * i:2 * i + 2, 0:nk], AX.X))
                    dve.tensor_scalar(mx[:, n, :], rr[:, n, :], -(DA_D ** -0.5), None, MUL).then_inc(s_da_nm.up(), 1)

                def da_weigh(n):
                    nk = (n % NC + 1) * P
                    dve.wait_ge(s_da_p.sem, s_da_p.at(l, 2 * n + 2))
                    link(dve.reciprocal(rr[:, n, :], sm[:, n, :]))
                    link(tt(rr[:, n, 1:2], rr[:, n, 1:2], nlam[:, 1:2], MUL))
                    if n >= 2:
                        dve.wait_ge(s_da_t.sem, s_da_t.at(l, n - 1))
                    w = wgt[:, n % 2, 0:nk]
                    link(dve.tensor_scalar(w, prob[:, n % 2, 0, 0:nk], rr[:, n, 0:1], None, MUL))
                    stt(w, prob[:, n % 2, 1, 0:nk], rr[:, n, 1:2], w, MUL, ADD).then_inc(s_da_w.up(), 1)

                def conv(t):
                    src = cin[:, t % 2, :]
                    dst = convT[:, t, :] if t < 6 else convG[:, t - 6, :]
                    dve.wait_ge(s_evac_a.sem, s_evac_a.at(l, N_QK + N_V + t + 1))
                    w = lambda j: col("cw", 4 * t + j)
                    link(dve.tensor_scalar(dst, src, w(3), col("cb", t), MUL, ADD))
                    for j in (1, 2):
                        link(stt(dst[:, j:SEQ], src[:, 0:SEQ - j], w(3 - j), dst[:, j:SEQ], MUL, ADD))
                    stt(dst[:, 3:SEQ], src[:, 0:SEQ - 3], w(0), dst[:, 3:SEQ], MUL, ADD).then_inc(s_conv.up(), 1)

                for s in range(ND + 1):
                    b = N_QK + N_V + s
                    if s:
                        da_max(s - 1)
                    if b + 1 < N_IN:
                        weights_lo(b + 1)
                    if s:
                        da_weigh(s - 1)
                    if 0 <= s - 2 < N_CONV:
                        conv(s - 2)
                dve.wait_ge(s_g_edk.sem, s_g_edk.at(l, 1))
                for c in range(NC):
                    dve.wait_ge(s_s_tr.sem, s_s_tr.at(l, c + 1))
                    xp = bk[2 + c % 2][:, 0:256].rearrange("p (h d) -> p h d", h=S_H)
                    link(tt(xd[:, c], xp, bcl(sp[:, c, 0:4], S_D), MUL))
                    tt(xskip[:, c], xp, bcl(col("dsk", 0, 4), S_D), MUL).then_inc(s_s_x.up(), 1)
                    tt(xdd[:, c], xd[:, c], bcl(edk[:, c, 0:4], S_D), MUL).then_inc(s_s_x.up(), 1)
                def s_scores(c):
                    dve.wait_ge(s_s_dec.sem, s_s_dec.at(l, 4 * c + 4))
                    dve.wait_ge(s_s_cb.sem, s_s_cb.at(l, c + 1))
                    if c >= 2:
                        dve.wait_ge(s_s_y.sem, s_s_y.at(l, c - 1))
                    tt(scoT[:, c % 2].rearrange("p (g h) n -> p g h n", g=2),
                             dec[:, c % 2].rearrange("p (g h) n -> p g h n", g=2),
                             bk[2 + c % 2][:, 0:256].rearrange("p (g n) -> p g n", g=2).unsqueeze(2).to_broadcast([P, 2, 2, P]),
                             MUL).then_inc(s_s_st.up(), 1)

                def s_state(c):
                    dve.wait_ge(s_s_h.sem, s_s_h.at(l, c + 1))
                    ph = bk[c % 2][:, 0:256].rearrange("p (h d) -> p h d", h=S_H)
                    if c >= 1:
                        link(tt(hst[:, (c + 1) % 2], hst[:, c % 2], bcl(ex[:, 1, c, 0:4], S_D), MUL))
                        own(tt(hst[:, (c + 1) % 2], hst[:, (c + 1) % 2], ph, ADD), s_s_hst)
                    else:
                        own(dve.tensor_copy(hst[:, 1], ph), s_s_hst)

                def s_out(c):
                    dve.wait_ge(s_s_y.sem, s_s_y.at(l, c + 1))
                    yp = bk[7][:, 0:256].rearrange("p (h d) -> p h d", h=S_H)
                    yo = bk[7][:, 256:512].rearrange("p (h d) -> p h d", h=S_H)
                    if c:
                        link(tt(ytmp[:], yo, bcl(ex[:, 0, c, 0:4], S_D), MUL))
                        link(tt(ytmp[:], ytmp[:], xskip[:, c], ADD))
                        own(tt(ysd[:, c], ytmp[:], yp, ADD), s_s_ya)
                    else:
                        own(tt(ysd[:, c], xskip[:, c], yp, ADD), s_s_ya)

                dve.wait_ge(s_s_x.sem, s_s_x.at(l, 8))
                dve.wait_ge(s_g_ex.sem, s_g_ex.at(l, 1))
                for h in range(DA_H):
                    n = H_MIX + h
                    dve.wait_ge(s_on_rs.sem, s_on_rs.at(l, h + 1))
                    free_htmp(n)
                    stt(htmp[:, n % 2, :], projT[:, h, :], sg1[:, 0:1], rs[:, h % 2, :], MUL, MUL).then_inc(s_h_f32.up(), 1)
                    if h < 2:
                        s_scores(h)
                    if h >= 1:
                        split_lo(n - 1)
                split_lo(H_MIX + DA_H - 1)
                s_state(0)
                for c in range(NC):
                    if 2 <= c + 1 < NC:
                        s_scores(c + 1)
                    if c + 1 < NC - 1:
                        s_state(c + 1)
                    s_out(c)
                dve.wait_ge(s_z_ev.sem, s_z_ev.at(l, 2))
                yf = ysd[:].rearrange("p c h d -> p (c h d)")
                link(tt(yf, yf, zst[:].rearrange("p c n -> p (c n)"), MUL))
                link(tt(ysq[:].rearrange("p c n -> p (c n)"), yf, yf, MUL))
                dve.reduce_sum(ss8[:], ysq[:].rearrange("p c (g n) -> p (c g) n", g=2), AX.X).then_inc(s_s_ss.up(), 1)
                dve.wait_ge(s_gsq.sem, s_gsq.at(l, NC))
                dve.reduce_sum(ss32[:].rearrange("p c n -> p (c n)"),
                                     gsq[:].rearrange("p c a h d -> p (c a h) d"), AX.X).then_inc(s_gn_ss.up(), 1)
                dve.wait_ge(s_s_rs.sem, s_s_rs.at(l, 1))
                y8 = ysd[:].rearrange("p c (g h) d -> p (c g) (h d)", g=2)
                tt(y8, y8, bcl(ss8[:], P), MUL).then_inc(s_s_yn.up(), 1)
                for f in range(2):
                    n = H_MIX + 4 + f
                    dve.wait_ge(s_so_tr.sem, s_so_tr.at(l, f + 1))
                    free_htmp(n)
                    dve.tensor_scalar(htmp[:, n % 2, :], bk[2 + f], col("sng", f), None, MUL).then_inc(s_h_f32.up(), 1)
                for f in range(2):
                    split_lo(H_MIX + 4 + f)

                dve.wait_ge(s_gn_rs.sem, s_gn_rs.at(l, 1))
                link(dve.tensor_scalar(ss32[:, :, 0:4], ss32[:, :, 0:4], G_D ** -0.5, None, MUL))
                for a in (1, 0):
                    q_ = qktok[:, :, a]
                    own(tt(q_, q_, bcl(ss32[:, :, 4 * a:4 * a + 4], G_D), MUL), s_gn_n)
                tt(qE[:], qktok[:, :, 0], bcl(ex[:, 0, :, 4:8], G_D), MUL).then_inc(s_gn_n.up(), 1)
                for c in range(NC):
                    dve.wait_ge(s_gd_dec.sem, s_gd_dec.at(l, 4 * c + 4))
                    dve.wait_ge(s_gd_kq.sem, s_gd_kq.at(l, c + 1))
                    D4 = decG[:, c % 2]
                    by_row = lambda a: a.rearrange("p (a r) n -> p r a n", r=2)
                    kkqk = hi_banks[:, 2 * (c % 2):2 * (c % 2) + 2, :].rearrange("p r (k a n) -> p k r a n", k=2, a=2)
                    own(tt(by_row(attT[:, c]), by_row(D4), kkqk[:, 1], MUL), s_gd_att)
                    link(tt(D4, D4, bcl(beta[:, c, :], P), MUL))
                    own(tt(by_row(aT[:, c]), by_row(D4), kkqk[:, 0], MUL), s_gd_at)
                for c in range(NC):
                    dve.wait_ge(s_ti_m.sem, s_ti_m.at(l, c + 1))
                    own(tt(tri_t[:, c], bcm(cst("idn"), G_H), tri_t[:, c], SUB), s_ti_0)
                for b in range(B_OUT, B_OUT + 2):
                    weights_lo(b)
                for n in range(NJ):
                    v, c = n // NC, n % NC
                    dve.wait_ge(s_tx_mm.sem, s_tx_mm.at(l, n + 1))
                    if v < NLEV - 2:
                        t = halves(tri_i[:, c], v, 0)
                        tt(t, t, joined(c, v, 0), SUB).then_inc(s_t_upd.up(), 1)
                    t = halves(tri_t[:, c], v, 1)
                    tt(t, t, joined(c, v, 1), SUB).then_inc(s_tt_upd.up(), 1)
                for c in range(NC):
                    dve.wait_ge(s_vn_mm.sem, s_vn_mm.at(l, c + 1))
                    if c >= 2:
                        dve.wait_ge(s_o_mm.sem, s_o_mm.at(l, c - 1))
                        dve.wait_ge(s_st_mm.sem, s_st_mm.at(l, c - 1))
                    tt(vnew[:, c % 2].rearrange("p (a r) d -> p r a d", r=2),
                             hi_banks[:, 0:2, 0:P].rearrange("p r (a d) -> p r a d", a=2),
                             bcl(beta[:, c, :].rearrange("p (a r) -> p r a", r=2), G_D), MUL).then_inc(s_vn.up(), 1)
                    if c < NC - 1:
                        dve.wait_ge(s_st_mm.sem, s_st_mm.at(l, c + 1))
                        new_, old = (c + 1) % 2, c % 2
                        if c == 0:
                            dve.tensor_copy(stS[:, new_].rearrange("p a d -> p (a d)"), bk[0][:, 0:P]).then_inc(s_st.up(), 1)
                        else:
                            for p_ in range(2):
                                for hh in range(2):
                                    r = slice(64 * hh, 64 * hh + 64)
                                    last = stt(stS[r, new_, p_, :], stS[r, old, p_, :],
                                               ex[r, 1, c, 4 + 2 * p_ + hh:5 + 2 * p_ + hh],
                                               bk[c % 2][r, p_ * 64:p_ * 64 + 64], MUL, ADD)
                                    if p_ + hh < 2:
                                        last.then_inc(s_dve_step.up(), 1)
                            last.then_inc(s_st.up(), 1)
                        dve.wait_ge(s_st.sem, s_st.at(l, c + 1))
                        dve.wait_ge(s_dve_step.sem, s_dve_step.at(l, s_dve_step.n))
                dve.wait_ge(s_o_ev.sem, s_o_ev.at(l, NC))
                dve.wait_ge(s_zg_ev.sem, s_zg_ev.at(l, 2))
                of = otok[:].rearrange("p c h d -> p (c h d)")
                link(tt(osq[:].rearrange("p c n -> p (c n)"), of, of, MUL))
                dve.reduce_sum(ss16[:], osq[:].rearrange("p c (h d) -> p (c h) d", h=G_H), AX.X).then_inc(s_go_ss.up(), 1)
                dve.wait_ge(s_go_rs.sem, s_go_rs.at(l, 1))
                link(tt(of, of, zgt[:].rearrange("p c n -> p (c n)"), MUL))
                o16 = otok[:].rearrange("p c h d -> p (c h) d")
                tt(o16, o16, bcl(ss16[:], G_D), MUL).then_inc(s_go_n.up(), 1)
                for f in range(2):
                    n = H_MIX + 6 + f
                    dve.wait_ge(s_go_tr.sem, s_go_tr.at(l, f + 1))
                    free_htmp(n)
                    dve.tensor_scalar(htmp[:, n % 2, :], bk[2 + f], col("gng", f), None, MUL).then_inc(s_h_f32.up(), 1)
                for f in range(2):
                    split_lo(H_MIX + 6 + f)

                def mem_lo(o, j, i, par):
                    add(o, j, i, par)
                    dve.wait_ge(s_h_lo.sem, s_h_lo.at(l, o + (H_MEM - 1)))
                    dve.tensor_scalar(htmp[:, j, 0:MEM], memn[:, bass.ds(o, 1), :].rearrange("p a n -> p (a n)"),
                                      prm[:, bass.ds(o + PC["g_mem"][0], 1)], None, MUL).then_inc(s_h_f32.up(), 1)
                    dve.wait_ge(s_h_hi.sem, s_h_hi.at(l, o + (H_MEM + 1)))
                    tt(meml[:, bass.ds(o, 1), :].rearrange("p a n -> p (a n)"), htmp[:, j, 0:MEM],
                       memh[:, bass.ds(o, 1), :].rearrange("p a n -> p (a n)").bitcast(F32), SUB).then_inc(s_h_lo.up(), 1)

                add = add_out(B_OUT)
                dense(B_OUT, N_OUT, KT, mem_lo, then=KT)

                def x_lo(o, j, i, par):
                    if j == 0:
                        dve.wait_ge(s_nrm_rs.sem, s_nrm_rs.at(l, 2))
                        dve.wait_ge(s_h_lo.sem, s_h_lo.at(l, i + (H_X - 1)))
                        stt(htmp[:, par, :], xT[:, bass.ds(i, 1), :].rearrange("p a n -> p (a n)"),
                            prm[:, bass.ds(i + PC["g_x"][0], 1)], rs[:, 0, :], MUL, MUL).then_inc(s_h_f32.up(), 1)
                    else:
                        dve.wait_ge(s_h_hi.sem, s_h_hi.at(l, i + (H_X + 1)))
                        tt(h_lo[:, bass.ds(i, 1), :].rearrange("p a n -> p (a n)"), htmp[:, par, :],
                           h_hi[:, bass.ds(i, 1), :].rearrange("p a n -> p (a n)").bitcast(F32), SUB).then_inc(s_h_lo.up(), 1)

                dense(B_KV, N_KV, KT, x_lo, then=KT)
                def ck_scale(m):
                    dve.wait_ge(s_ck_rs.sem, s_ck_rs.at(l, m + 1))
                    for f in range(2):
                        t = kvT[:, 2 * m + f, :]
                        stt(t, t, col("xkg", f), rs[:, 0, 0:MEM], MUL, MUL).then_inc(s_ck_n.up(), 1)

                def cq_scale(m):
                    dve.wait_ge(s_cq_rs.sem, s_cq_rs.at(l, m + 1))
                    for f in range(2):
                        t = qcT[:, 2 * m + f, :]
                        stt(t, t, col("xqg", f), rs[:, 1, :], MUL, MUL).then_inc(s_cq_n.up(), 1)

                for t in range(N_CQ + 3):
                    if 0 <= t - 3 < N_CQ and (t - 3) % 2 == 1:
                        cq_scale((t - 3) // 2)
                    if t >= 1 and t - 1 < N_CQ:
                        weights_lo(B_CQ + t + 1)
                    if t < N_CQ and t % 2 == 1:
                        ck_scale(t // 2)

                def c_max(n):
                    dve.wait_ge(s_c_s.sem, s_c_s.at(l, n + 1))
                    link(dve.reduce_max(rr[:, n, :], bk[4 + n % 2].rearrange("p (i m) -> p i m", i=2), AX.X))
                    dve.tensor_scalar(mx[:, n, :], rr[:, n, :], -(X_D ** -0.5), None, MUL).then_inc(s_c_nm.up(), 1)

                def c_scale(n):
                    dve.wait_ge(s_c_p.sem, s_c_p.at(l, 2 * n + 2))
                    link(dve.reciprocal(rr[:, n, :], sm[:, n, :]))
                    tt(pc[:, n % 3], pc[:, n % 3], bcl(rr[:, n, :], MEM), MUL).then_inc(s_c_w.up(), 1)

                for n in range(N_CA + 3):
                    if n < N_CA:
                        c_max(n)
                    if 0 <= n - 1 < N_CA:
                        c_scale(n - 1)
                    if n >= 4 and n % 2 == 0:
                        for e in range(2):
                            split_lo(H_CA + n - 4 + e, src=bk[e])
                dense(B_CO, N_CO, KT, add_out(B_CO), then=KT)
                norm_out(2, H_FF, "g_ffn")
                b = B_FF
                for half in range(2):
                    f0 = half * FH

                    def ffn_out(i, j, b, f0):
                        if j == 0:
                            return
                        dve.wait_ge(s_f_sg.sem, s_f_sg.at(l, i + (f0 + 1)))
                        dve.wait_ge(s_blk_done.sem, s_blk_done.at(l, 2 * i + (b + 2)))
                        dve.wait_ge(s_f_hi.sem, s_f_hi.at(l, i + f0))
                        dve.wait_ge(s_f_lo.sem, s_f_lo.at(l, i + f0))
                        tt(h2[:], sgate[:], bk[1], MUL).then_inc(s_f_h2.up(), 1)
                        dve.wait_ge(s_f_hi.sem, s_f_hi.at(l, i + (f0 + 1)))
                        tt(f_lo[:, bass.ds(i, 1), :].rearrange("p a n -> p (a n)"), h2[:],
                                 f_hi[:, bass.ds(i, 1), :].rearrange("p a n -> p (a n)").bitcast(F32), SUB).then_inc(s_f_lo.up(), 1)

                    def body(q, slot, loads, i, par, b=b, f0=f0):
                        for j in range(2):
                            dve.wait_ge(s_w_hi.sem, s_w_hi.at(l, 2 * q + (b + j + 1)))
                            tt(w_lo[j][:, 0:KT, :].rearrange("p k n -> p (k n)"),
                                     raw[:, slot, j * WA:(j + 1) * WA],
                                     w_hi[j][:, 0:KT, :].rearrange("p k n -> p (k n)").bitcast(F32), SUB).then_inc(s_w_lo.up(), 1)
                            ffn_out(i, j, b, f0)
                    pair_loop(dve, b // 2, FH, body)
                    for j in range(2):
                        weights_lo(b + N_GU + j, FH)
                        ffn_out(FH - 1, j, b, f0)
                    b += N_GU
                    dense(b, N_DN, FH, add_out(b), then=KT if half == 0 else None)
                    b += N_DN

        @block.tensor
        def _(pe):
            def mm(out, lhsT, rhs, start=True, stop=True):
                return pe.matmul(out, lhsT, rhs, start=start, stop=stop)

            idn, ones, blk, tri = cst("idn"), cst("ones"), cst("blk"), cst("tri")

            pe.wait_ge(s_const_in.sem, 16)
            pe.wait_ge(s_x_in.sem, 16)
            for n in range(8):
                c, i = n // 2, n % 2
                if n >= 2:
                    pe.wait_ge(s_x_turned.sem, n - 1)
                for k in range(4):
                    last = pe.transpose(bk[2 + n % 2][:, k * P:(k + 1) * P], xtok[:, c, (4 * i + k) * P:(4 * i + k + 1) * P], idn)
                last.then_inc(s_x_tr.sem, 1)
            pe.wait_ge(s_mem_n.sem, 2)
            for n in range(4):
                c, i = n // 2, n % 2
                if n >= 2:
                    pe.wait_ge(s_m_ev.sem, n - 1)
                for k in range(4):
                    last = pe.transpose(bk[4 + n % 2][:, k * P:(k + 1) * P], mjunk[:, c, (4 * i + k) * P:(4 * i + k + 1) * P], idn)
                last.then_inc(s_m_tr.sem, 1)
            pe.wait_ge(s_c_bf.sem, 1)
            pe.wait_ge(s_x_turned.sem, 8)
            for k in range(KT):
                pe.wait_ge(s_nrm_sq.sem, k + 1)
                mm(bk[2], ones, sq[:, k % 2, :], k == 0, k == KT - 1).then_inc(s_nrm_mm.sem, 1)

            with pe.Fori(0, DEPTH) as l:
                def pass3(j, k, K, hi, lo, w):
                    mm(bk[j][:, 0:w], w_hi[j][:, k, :], hi[:, k, 0:w], k == 0, False)
                    mm(bk[j][:, 0:w], w_hi[j][:, k, :], lo[:, k, 0:w], False, False)
                    return mm(bk[j][:, 0:w], w_lo[j][:, k, :], hi[:, k, 0:w], False, k == K - 1)

                def product(j, K, hi, lo, w):
                    for k in range(K):
                        last = pass3(j, k, K, hi, lo, w)
                    last.then_inc(s_blk_done.up(), 1)

                def product_pair(n0):
                    for k in range(KT):
                        pe.wait_ge(s_h_lo.sem, s_h_lo.at(l, n0 + k + 1))
                        for j in range(2):
                            last = pass3(j, k, KT, h_hi, h_lo, SEQ)
                            if k == KT - 1:
                                last.then_inc(s_blk_done.up(), 1)

                def dense(b0, n, K, hi, lo, w, free, e0, *needs):
                    trips[0] = n // 2
                    with pe.Fori(0, n // 2) as i:
                        for j in range(2):
                            if j == 0:
                                for s, v in needs:
                                    pe.wait_ge(s.sem, s.at(l, v))
                            pe.wait_ge(s_w_lo.sem, s_w_lo.at(l, 2 * i + (b0 + j + 1)))
                            pe.wait_ge(free.sem, free.at(l, 2 * i + (e0 + j - 1)))
                            product(j, K, hi, lo, w)
                    trips[0] = 1

                def dense_x(b0, K, hi, lo, e0, g, *needs):
                    def block_x(o, j):
                        pe.wait_ge(s_w_lo.sem, s_w_lo.at(l, o + (b0 + 1)))
                        pe.wait_ge(s_evac_d.sem, s_evac_d.at(l, o + (e0 - 1)))
                        product(j, K, hi, lo, SEQ)

                    def sum_x(squares, first=False, last=False):
                        mm(bk[2], ones, squares, first, last).then_inc(s_nrm_mm.up(), 1)

                    for s, v in needs:
                        pe.wait_ge(s.sem, s.at(l, v))
                    block_x(0, 0)
                    block_x(1, 1)
                    trips[0] = 3
                    with pe.Fori(0, 3) as i:
                        for j in range(2):
                            block_x(2 * i + (2 + j), j)
                    trips[0] = 1
                    pe.wait_ge(s_nrm_acc.sem, s_nrm_acc.at(l, (g + 1) * (KT - 2)))
                    sum_x(sqsum[:], first=True)
                    pe.wait_ge(s_nrm_sq.sem, s_nrm_sq.at(l, g * KT + KT - 1))
                    sum_x(sq[:, 0, :])
                    pe.wait_ge(s_nrm_sq.sem, s_nrm_sq.at(l, (g + 1) * KT))
                    sum_x(sq[:, 1, :], last=True)

                for b in range(2):
                    pe.wait_ge(s_w_lo.sem, s_w_lo.at(l, b + 1))
                pe.wait_ge(s_evac_d.sem, s_evac_d.at(l, 0))
                product_pair(H_IN)
                pe.wait_ge(s_wsm_lo.sem, s_wsm_lo.at(l, 1))
                for k in range(KT):
                    mm(bk[7], wsm_hi[:, k, :], h_hi[:, k, :], k == 0, False)
                    mm(bk[7], wsm_hi[:, k, :], h_lo[:, k, :], False, False)
                    last = mm(bk[7], wsm_lo[:, k, :], h_hi[:, k, :], False, k == KT - 1)
                last.then_inc(s_g_mm.up(), 1)
                pe.wait_ge(s_g_out.sem, s_g_out.at(l, 1))
                for c in range(NC):
                    last = pe.transpose(bk[7][:, c * P:(c + 1) * P], gates[:, c * P:(c + 1) * P], idn)
                last.then_inc(s_g_ps.up(), 1)

                def product_in(b):
                    pe.wait_ge(s_w_lo.sem, s_w_lo.at(l, b + 1))
                    pe.wait_ge(s_evac_a.sem, s_evac_a.at(l, b - 1))

                def qk_sum(o, j):
                    pe.wait_ge(s_qk_sq.sem, s_qk_sq.at(l, o + 1))
                    mm(bk[2 + j], blk, sq[:, j, :]).then_inc(s_qk_ss.up(), 1)

                trips[0] = 3
                with pe.Fori(0, 3) as i:
                    for j in range(2):
                        product_in(2 * i + (j + 2))
                        product(j, KT, h_hi, h_lo, SEQ)
                        qk_sum(2 * i + j, j)
                trips[0] = 1
                for b in range(8, N_QK + N_V):
                    product_in(b)
                    product(b % 2, KT, h_hi, h_lo, SEQ)
                    if b - 2 < N_QK:
                        qk_sum(b - 2, b % 2)
                    if b == 10:
                        pe.wait_ge(s_g_a.sem, s_g_a.at(l, 1))
                        gaf = ga[:].rearrange("p c h -> p (c h)")
                        mm(bk[7][:, 64:96], tri, gaf)
                        mm(bk[7][:, 96:128], ones, gaf).then_inc(s_g_cum.up(), 1)

                def v_turn(c):
                    if c == 0:
                        pe.wait_ge(s_evac_a.sem, s_evac_a.at(l, N_QK + N_V))
                        pe.wait_ge(s_qk_n.sem, s_qk_n.at(l, N_QK))
                        pe.wait_ge(s_g_dk.sem, s_g_dk.at(l, 1))
                    if c == 1:
                        pe.wait_ge(s_v_ev.sem, s_v_ev.at(l, 1))
                    if c >= 2:
                        pe.wait_ge(s_da_wt.sem, s_da_wt.at(l, c - 1))
                    for h in range(DA_H):
                        last = pe.transpose(bk[2][:, h * P:(h + 1) * P], vT[:, h, c * P:(c + 1) * P], idn)
                    last.then_inc(s_v_tr.up(), 1)

                def da_scores(n):
                    h, qt = n // NC, n % NC
                    nk = (qt + 1) * P
                    if n >= 2:
                        pe.wait_ge(s_da_p.sem, s_da_p.at(l, 2 * (n - 1)))
                    for c in range(2):
                        r = slice(64 * c, 64 * c + 64)
                        b = bk[4 + 2 * (n % 2) + c]
                        mm(b[:, 0:nk], projT[r, h, qt * P:nk], projT[r, 4 + h, 0:nk], True, False)
                        last = mm(b[:, nk - P:nk], idb[:], negq[:], False, True)
                    last.then_inc(s_da_s.up(), 1)

                def da_turn(n):
                    pe.wait_ge(s_da_w.sem, s_da_w.at(l, n + 1))
                    if n >= 1:
                        pe.wait_ge(s_da_wt.sem, s_da_wt.at(l, n))
                    if n < NC:
                        pe.wait_ge(s_v_ev.sem, s_v_ev.at(l, min(n + 2, NC)))
                    for k in range(n % NC + 1):
                        last = pe.transpose(bk[2][:, k * P:(k + 1) * P], wgt[:, n % 2, k * P:(k + 1) * P], idn)
                    last.then_inc(s_da_t.up(), 1)

                def da_values(n):
                    h, qt = n // NC, n % NC
                    pe.wait_ge(s_da_wt.sem, s_da_wt.at(l, n + 1))
                    if qt == 0 and h >= 1:
                        pe.wait_ge(s_da_o.sem, s_da_o.at(l, h))
                    for k in range(qt + 1):
                        last = mm(bk[3][:, qt * P:(qt + 1) * P], vtok[:, k, h, :], wgtT[:, n % 2, k * P:(k + 1) * P],
                                  k == 0, k == qt)
                    last.then_inc(s_da_pv.up(), 1)

                for s in range(ND + 2):
                    b = N_QK + N_V + s
                    if b < N_IN:
                        product_in(b)
                        product(b % 2, KT, h_hi, h_lo, SEQ)
                    if s < NC:
                        v_turn(s)
                    if s < ND:
                        da_scores(s)
                    if 0 <= s - 1 < ND:
                        da_turn(s - 1)
                    if 0 <= s - 2:
                        da_values(s - 2)

                pe.wait_ge(s_da_o.sem, s_da_o.at(l, DA_H))
                for c in range(NC):
                    if c == 0:
                        pe.wait_ge(s_convs.sem, s_convs.at(l, 4))
                    if c >= 2:
                        pe.wait_ge(s_s_ev.sem, s_s_ev.at(l, c - 1))
                        pe.wait_ge(s_s_x.sem, s_s_x.at(l, 2 * (c - 1)))
                    for t in range(4):
                        last = pe.transpose(bk[2 + 2 * (t // 2) + c % 2][:, (t % 2) * P:(t % 2 + 1) * P],
                                            convT[:, t, c * P:(c + 1) * P], idn)
                    last.then_inc(s_s_tr.up(), 1)
                pe.wait_ge(s_s_ev.sem, s_s_ev.at(l, NC))
                pe.wait_ge(s_s_x.sem, s_s_x.at(l, 2 * NC))

                def decays(b, c, h0):
                    for h in range(4):
                        o = b[:, h * P:(h + 1) * P]
                        mm(o, ga[:, c, h0 + h:h0 + h + 1].to_broadcast([P, P]), tri, True, False)
                        last = mm(o, idb[:], negd[:], False, True)
                    return last

                def s_decays(c):
                    cs = slice(c * P, (c + 1) * P)
                    if c >= 2:
                        pe.wait_ge(s_s_dec.sem, s_s_dec.at(l, 4 * (c - 1)))
                    decays(bk[4 + c % 2], c, 0).then_inc(s_s_d.up(), 1)
                    if c >= 2:
                        pe.wait_ge(s_s_st.sem, s_s_st.at(l, c - 1))
                    for g in range(2):
                        last = mm(bk[2 + c % 2][:, g * P:(g + 1) * P], convT[:, 2 + g, cs], convT[:, 4 + g, cs])
                    last.then_inc(s_s_cb.up(), 1)

                def s_outer(c):
                    if c >= 2:
                        pe.wait_ge(s_s_hst.sem, s_s_hst.at(l, c - 1))
                    for g in range(2):
                        last = mm(bk[c % 2][:, g * P:(g + 1) * P], btok[:, c, g, :],
                                  xdd[:, c, 2 * g:2 * g + 2, :].rearrange("p h d -> p (h d)"))
                    last.then_inc(s_s_h.up(), 1)

                def on_sum(h):
                    pe.wait_ge(s_on_sq.sem, s_on_sq.at(l, h + 1))
                    if h >= 2:
                        pe.wait_ge(s_on_rs.sem, s_on_rs.at(l, h - 1))
                    mm(bk[6 + h % 2], ones, sq[:, h % 2, :]).then_inc(s_on_ss.up(), 1)

                on_sum(0)
                on_sum(1)
                s_decays(0)
                s_decays(1)
                pe.wait_ge(s_zs.sem, s_zs.at(l, 2))
                for i in range(2):
                    for c in range(2):
                        for t in range(2):
                            cc = 2 * i + c
                            last = pe.transpose(bk[i][:, (2 * c + t) * P:(2 * c + t + 1) * P],
                                                zT[:, t, cc * P:(cc + 1) * P], idn)
                    last.then_inc(s_z_tr.up(), 1)
                on_sum(2)
                on_sum(3)
                pe.wait_ge(s_z_ev.sem, s_z_ev.at(l, 2))
                s_outer(0)
                pe.wait_ge(s_on_rs.sem, s_on_rs.at(l, DA_H))
                for c in range(NC):
                    cs = slice(c * P, (c + 1) * P)
                    pe.wait_ge(s_s_st.sem, s_s_st.at(l, c + 1))
                    if c >= 1:
                        pe.wait_ge(s_s_ya.sem, s_s_ya.at(l, c))
                        pe.wait_ge(s_s_hst.sem, s_s_hst.at(l, c))
                    for h in range(S_H):
                        last = mm(bk[7][:, h * S_D:(h + 1) * S_D], scoT[:, c % 2, h, :], xd[:, c, h, :])
                    if c:
                        for g in range(2):
                            last = mm(bk[7][:, 256 + g * P:256 + (g + 1) * P], convT[:, 4 + g, cs],
                                      hst[:, c % 2, 2 * g:2 * g + 2, :].rearrange("p h d -> p (h d)"))
                    last.then_inc(s_s_y.up(), 1)
                    if c + 1 < NC - 1:
                        s_outer(c + 1)
                    if c + 2 < NC:
                        s_decays(c + 2)

                pe.wait_ge(s_s_ya.sem, s_s_ya.at(l, NC))
                for c in range(NC):
                    if c >= 2:
                        pe.wait_ge(s_gt_ev.sem, s_gt_ev.at(l, 2 * (c - 1)))
                    for t in range(6):
                        o = bk[2 + c % 2][:, t * P:(t + 1) * P] if t < 4 else bk[4 + c % 2][:, (t - 4) * P:(t - 3) * P]
                        last = pe.transpose(o, convG[:, t, c * P:(c + 1) * P], idn)
                    last.then_inc(s_gt_tr.up(), 1)

                pe.wait_ge(s_gt_ev.sem, s_gt_ev.at(l, 8))
                pe.wait_ge(s_s_yn.sem, s_s_yn.at(l, 1))
                for f in range(2):
                    for c in range(NC):
                        last = pe.transpose(bk[2 + f][:, c * P:(c + 1) * P],
                                            ysd[:, c, 2 * f:2 * f + 2, :].rearrange("p h d -> p (h d)"), idn)
                    last.then_inc(s_so_tr.up(), 1)

                pe.wait_ge(s_h_f32.sem, s_h_f32.at(l, H_MIX + 6))
                pe.wait_ge(s_gt_ev.sem, s_gt_ev.at(l, 8))
                for i in range(6):
                    which, pr = i // 2, i % 2
                    if pr == 0:
                        pe.wait_ge(s_gn_n.sem, s_gn_n.at(l, which + 1))
                    if i >= 2:
                        pe.wait_ge(s_g3_ev.sem, s_g3_ev.at(l, i - 1))
                    for c in range(NC):
                        src = (qktok[:, c, 1], qktok[:, c, 0], qE[:, c])[which]
                        last = pe.transpose(bk[2 + pr][:, c * P:(c + 1) * P],
                                            src[:, 2 * pr:2 * pr + 2, :].rearrange("p h d -> p (h d)"), idn)
                    last.then_inc(s_g3_tr.up(), 1)
                pe.wait_ge(s_g3_ev.sem, s_g3_ev.at(l, 6))
                for c in range(NC):
                    cs = slice(c * P, (c + 1) * P)
                    if c >= 2:
                        pe.wait_ge(s_gd_dec.sem, s_gd_dec.at(l, 4 * (c - 1)))
                    decays(bk[c % 2], c, 4).then_inc(s_gd_d.up(), 1)
                    if c >= 2:
                        pe.wait_ge(s_gd_at.sem, s_gd_at.at(l, c - 1))
                        pe.wait_ge(s_gd_att.sem, s_gd_att.at(l, c - 1))
                    for h in range(G_H):
                        r = slice(64 * (h % 2), 64 * (h % 2) + 64)
                        kk = tr3[r, 0, h // 2, cs]
                        o = bk[4 + 2 * (c % 2) + h % 2]
                        mm(o[:, (h // 2) * P:(h // 2 + 1) * P], kk, kk)
                        last = mm(o[:, (2 + h // 2) * P:(3 + h // 2) * P], kk, tr3[r, 1, h // 2, cs])
                    last.then_inc(s_gd_kq.up(), 1)
                for c in range(NC):
                    pe.wait_ge(s_ti_0.sem, s_ti_0.at(l, c + 1))
                    if c >= 2:
                        pe.wait_ge(s_ti_ev.sem, s_ti_ev.at(l, c - 1))
                    for h in range(G_H):
                        last = pe.transpose(bk[2 + c % 2][:, h * P:(h + 1) * P], tri_t[:, c, h, :], idn)
                    last.then_inc(s_ti_tr.up(), 1)
                def join_1(n):
                    c = n % NC
                    pe.wait_ge(s_lvl.sem, s_lvl.at(l, n + 1))
                    if n < 2:
                        pe.wait_ge(s_ti_ev.sem, s_ti_ev.at(l, n + 3))
                    else:
                        pe.wait_ge(s_m1_ev.sem, s_m1_ev.at(l, n - 1))
                    if n >= NC:
                        pe.wait_ge(s_t_upd.sem, s_t_upd.at(l, n - NC + 1))
                    for h in range(G_H):
                        last = mm(bk[2 + n % 2][:, h * P:(h + 1) * P], lvlA[:, n % 2, h, :], tri_i[:, c, h, :])
                    last.then_inc(s_m1_mm.up(), 1)

                def join_2(n):
                    v, c = n // NC, n % NC
                    pe.wait_ge(s_m1_ev.sem, s_m1_ev.at(l, n + 1))
                    if n >= NC:
                        pe.wait_ge(s_tt_upd.sem, s_tt_upd.at(l, n - NC + 1))
                    for h in range(G_H):
                        if v < NLEV - 2:
                            mm(joined(c, v, 0)[:, h], tri_t[:, c, h, :], halves(m1[:, c], v, 0)[:, h])
                        last = mm(joined(c, v, 1)[:, h], m1[:, c, h, :], halves(tri_t[:, c], v, 1)[:, h])
                    last.then_inc(s_tx_mm.up(), 1)

                join_1(0)
                for n in range(1, NJ):
                    join_1(n)
                    join_2(n - 1)
                join_2(NJ - 1)
                pe.wait_ge(s_tt_upd.sem, s_tt_upd.at(l, (NLEV - 1) * NC))
                pe.wait_ge(s_m1_ev.sem, s_m1_ev.at(l, (NLEV - 1) * NC))
                pe.wait_ge(s_kdec.sem, s_kdec.at(l, 2))
                for pr in range(2):
                    for c in range(NC):
                        for hh in range(2):
                            h = 2 * pr + hh
                            last = mm(bk[2 + pr][64 * hh:64 * hh + 64, c * P:(c + 1) * P], kE[:, c, h, :],
                                      tri_t[:, c, h, :])
                    last.then_inc(s_w_mm.up(), 1)
                pe.wait_ge(s_w_ev.sem, s_w_ev.at(l, 2))
                for c in range(NC):
                    cs = slice(c * P, (c + 1) * P)
                    if c >= 1:
                        pe.wait_ge(s_vn.sem, s_vn.at(l, c))
                        pe.wait_ge(s_st.sem, s_st.at(l, c))
                    for h in range(G_H):
                        r = slice(64 * (h % 2), 64 * (h % 2) + 64)
                        o = bk[4 + h % 2][:, (h // 2) * G_D:(h // 2 + 1) * G_D]
                        last = mm(o, tri_t[:, c, h, :], gvtok[:, c, h, :], True, c == 0)
                        if c:
                            last = mm(o, wTn[r, h // 2, cs], stS[r, c % 2, h // 2, :], False, True)
                    last.then_inc(s_vn_mm.up(), 1)
                    if c < 2:
                        pe.wait_ge(s_zs.sem, s_zs.at(l, 4))
                        for cc in (2 * c, 2 * c + 1):
                            for t in range(2):
                                last = pe.transpose(bk[2 + c][:, (2 * (cc % 2) + t) * P:(2 * (cc % 2) + t + 1) * P],
                                                    zT[:, 2 + t, cc * P:(cc + 1) * P], idn)
                        last.then_inc(s_zg_tr.up(), 1)
                    pe.wait_ge(s_vn.sem, s_vn.at(l, c + 1))
                    if c < NC - 1:
                        for h in range(G_H):
                            r = slice(64 * (h % 2), 64 * (h % 2) + 64)
                            last = mm(bk[c % 2][r, (h // 2) * G_D:(h // 2 + 1) * G_D], kgt[:, c, h, :], vnew[:, c % 2, h, :])
                        last.then_inc(s_st_mm.up(), 1)
                    if c >= 1:
                        pe.wait_ge(s_o_ev.sem, s_o_ev.at(l, c))
                    for h in range(G_H):
                        r = slice(64 * (h % 2), 64 * (h % 2) + 64)
                        o = bk[6 + h % 2][:, (h // 2) * G_D:(h // 2 + 1) * G_D]
                        if c:
                            mm(o, tr3[r, 2, h // 2, cs], stS[r, c % 2, h // 2, :], True, False)
                        last = mm(o, attT[:, c, h, :], vnew[:, c % 2, h, :], c == 0, True)
                    last.then_inc(s_o_mm.up(), 1)
                pe.wait_ge(s_zg_ev.sem, s_zg_ev.at(l, 2))
                pe.wait_ge(s_go_n.sem, s_go_n.at(l, 1))
                for f in range(2):
                    for c in range(NC):
                        last = pe.transpose(bk[2 + f][:, c * P:(c + 1) * P],
                                            otok[:, c, 2 * f:2 * f + 2, :].rearrange("p h d -> p (h d)"), idn)
                    last.then_inc(s_go_tr.up(), 1)

                dense_x(B_OUT, KT, h_hi, h_lo, ED_OUT, 0, (s_h_lo, H_MIX + KT))
                dense(B_KV, N_KV, KT, memh, meml, MEM, s_evac_a, EA_KV, (s_h_lo, H_MEM + KT), (s_evac_d, ED_OUT + N_OUT))
                def cq_sum(t):
                    pe.wait_ge(s_cq_sq.sem, s_cq_sq.at(l, t + 1))
                    if t % 2 == 0 and t:
                        pe.wait_ge(s_cq_rs.sem, s_cq_rs.at(l, t // 2))
                    mm(bk[2], ones, sq[:, t % 2, :], t % 2 == 0, t % 2 == 1).then_inc(s_cq_ss.up(), 1)

                def ck_sum(m):
                    pe.wait_ge(s_ck_sq.sem, s_ck_sq.at(l, 2 * m + 2))
                    if m:
                        pe.wait_ge(s_ck_rs.sem, s_ck_rs.at(l, m))
                    for f in range(2):
                        last = mm(bk[3][:, 0:MEM], ones, ksq[:, f, :], f == 0, f == 1)
                    last.then_inc(s_ck_ss.up(), 1)

                for t in range(N_CQ):
                    pe.wait_ge(s_w_lo.sem, s_w_lo.at(l, B_CQ + t + 1))
                    pe.wait_ge(s_h_lo.sem, s_h_lo.at(l, H_X + KT))
                    pe.wait_ge(s_evac_a.sem, s_evac_a.at(l, EA_CQ + t - 1))
                    product(t % 2, KT, h_hi, h_lo, SEQ)
                    if t >= 2:
                        cq_sum(t - 2)
                    if t % 2 == 0:
                        ck_sum(t // 2)
                    else:
                        g = t // 2
                        for i in range(4):
                            last = pe.transpose(bk[4 + g][:, i * P:(i + 1) * P],
                                                kvT[:, 8 + 4 * (g % 2) + i, (g // 2) * P:(g // 2 + 1) * P], idn)
                        last.then_inc(s_cv_tr.up(), 1)
                for t in (N_CQ - 2, N_CQ - 1):
                    cq_sum(t)

                def c_scores(n):
                    h, qp = n // 2, n % 2
                    pe.wait_ge(s_cq_n.sem, s_cq_n.at(l, 2 * h + 2))
                    pe.wait_ge(s_ck_n.sem, s_ck_n.at(l, 2 * h + 2))
                    if n < 2:
                        pe.wait_ge(s_cv_ev.sem, s_cv_ev.at(l, n + 1))
                    else:
                        pe.wait_ge(s_c_p.sem, s_c_p.at(l, 2 * (n - 1)))
                    for i in range(2):
                        q0 = (2 * qp + i) * P
                        for f in range(2):
                            last = mm(bk[4 + n % 2][:, i * MEM:(i + 1) * MEM], qcT[:, 2 * h + f, q0:q0 + P],
                                      kvT[:, 2 * h + f, :], f == 0, f == 1)
                    last.then_inc(s_c_s.up(), 1)

                def c_turn(n):
                    pe.wait_ge(s_c_w.sem, s_c_w.at(l, n + 1))
                    if n < 2:
                        pe.wait_ge(s_cv_ev.sem, s_cv_ev.at(l, n + 3))
                    else:
                        pe.wait_ge(s_c_pt.sem, s_c_pt.at(l, n - 1))
                    for i in range(2):
                        for m in range(2):
                            last = pe.transpose(bk[6 + n % 2][:, m * 256 + i * P:m * 256 + (i + 1) * P],
                                                pc[:, n % 3, i, m * P:(m + 1) * P], idn)
                    last.then_inc(s_c_t.up(), 1)

                def c_values(h):
                    pe.wait_ge(s_c_pt.sem, s_c_pt.at(l, 2 * h + 2))
                    for e in range(2):
                        if h == 0:
                            pe.wait_ge(s_evac_a.sem, s_evac_a.at(l, EA_CQ + N_CQ))
                        else:
                            pe.wait_ge(s_h_lo.sem, s_h_lo.at(l, H_CA + 2 * (h - 1) + e + 1))
                        for m in range(2):
                            last = mm(bk[e], vmt[:, m, h * X_D + e * P:h * X_D + (e + 1) * P], pT[:, h % 2, m, :],
                                      m == 0, m == 1)
                        last.then_inc(s_c_pv.up(), 1)

                for n in range(N_CA + 3):
                    if n < N_CA:
                        c_scores(n)
                    if n >= 4 and n % 2 == 0:
                        c_values(n // 2 - 2)
                    if 0 <= n - 2 < N_CA:
                        c_turn(n - 2)
                dense_x(B_CO, KT, h_hi, h_lo, ED_CO, 1, (s_h_lo, H_CA + KT))
                b = B_FF
                for half in range(2):
                    f0, e0 = half * FH, ED_DN + half * N_DN
                    if half == 0:
                        pe.wait_ge(s_w_lo.sem, s_w_lo.at(l, b + 2))
                        pe.wait_ge(s_evac_d.sem, s_evac_d.at(l, e0))
                        product_pair(H_FF)
                    done = 1 - half
                    trips[0] = FH - done
                    with pe.Fori(0, FH - done) as i:
                        pe.wait_ge(s_evac_d.sem, s_evac_d.at(l, e0))
                        for j, free in enumerate((s_f_sg, s_f_h2)):
                            pe.wait_ge(s_w_lo.sem, s_w_lo.at(l, 2 * i + (b + 2 * done + j + 1)))
                            pe.wait_ge(free.sem, free.at(l, i + (f0 + done)))
                            product(j, KT, h_hi, h_lo, SEQ)
                    trips[0] = 1
                    b += N_GU
                    if half == 0:
                        dense(b, N_DN, FH, f_hi, f_lo, SEQ, s_evac_d, e0, (s_f_sg, f0 + FH), (s_f_lo, f0 + FH))
                    else:
                        dense_x(b, FH, f_hi, f_lo, e0, 2, (s_f_sg, f0 + FH), (s_f_lo, f0 + FH))
                    b += N_DN
            for n in range(8):
                c, i = n // 2, n % 2
                if n == 0:
                    pe.wait_ge(s_evac_d.sem, s_evac_d.at(DEPTH, 0))
                if n >= 2:
                    pe.wait_ge(s_y_ready.sem, n - 1)
                for k in range(4):
                    last = pe.transpose(bk[2 + n % 2][:, k * P:(k + 1) * P], xT[:, 4 * i + k, c * P:(c + 1) * P], idn)
                last.then_inc(s_y_tr.sem, 1)

        got = {k: v for k, v in ((k, s.n) for k, s in signals.items()) if v}
        if got != PER_LAYER:
            if strict:
                raise AssertionError(f"PER_LAYER = {got}")
        return got


def layout(inp):
    f = lambda n: np.ascontiguousarray(np.asarray(inp[n]))
    L = DEPTH
    w_in = f("w_in")
    o = np.cumsum([0, 512, 512, 512, 256, 768, 4, 768, 256, 4, 4])
    part = {n: w_in[:, :, o[i]:o[i + 1]] for i, n in enumerate(("qa", "ka", "va", "zs", "xbc", "dt", "qkv", "zg", "b", "a"))}
    big = np.concatenate([part[n] for n in ("qa", "ka", "va", "xbc", "qkv", "zs", "zg")], axis=2)
    small = np.concatenate([part[n] for n in ("dt", "a", "b")], axis=2)

    def blocks(w, k):
        Lw, K, N = w.shape
        return w.reshape(Lw, k, P, N // P, P).transpose(0, 3, 2, 1, 4).reshape(Lw, N // P, P, k * P)

    gu = blocks(f("w_gate_up"), KT)
    gu = np.stack([gu[:, :FT], gu[:, FT:]], axis=2).reshape(L, 2 * FT, P, WA)
    wa = np.concatenate([blocks(big, KT), blocks(f("w_out"), KT), blocks(f("w_ckv"), KT), blocks(f("w_cq"), KT),
                         blocks(f("w_co"), KT), gu], axis=1)
    wa = wa.reshape(L, PAIRS_A, 2, P, WA).transpose(0, 1, 3, 2, 4).reshape(L * PAIRS_A, P, 2 * WA)
    dn = f("w_down").reshape(L, 2, FH * P, D_MODEL)
    wd = np.stack([blocks(dn[:, h], FH) for h in range(2)], axis=1)
    wd = wd.reshape(L, PAIRS_D, 2, P, WD).transpose(0, 1, 3, 2, 4).reshape(L * PAIRS_D, P, 2 * WD)
    wsm = small.reshape(L, KT, P, 12).transpose(0, 2, 1, 3).reshape(L, P, KT * 12)

    rows = lambda a: np.broadcast_to(a[:, None, :], (L, P, a.shape[-1]))
    tiles = lambda a: a.reshape(L, -1, P).transpose(0, 2, 1)
    twice = lambda a: np.concatenate([a, a], axis=-1)[:, :, None]
    cw = np.concatenate([f("ssd_conv_w"), f("gdn_conv_w")], axis=2)
    cw = cw.reshape(L, 4, 12, P).transpose(0, 3, 2, 1).reshape(L, P, 48)
    cb = tiles(np.concatenate([f("ssd_conv_b"), np.zeros((L, 768), np.float32)], axis=1))
    li = np.array([0.8 - 0.6 * math.exp(-0.3 * l) for l in range(L)], np.float32)
    lamv = np.concatenate([f("da_lambda_q1"), f("da_lambda_k1"), f("da_lambda_q2"), f("da_lambda_k2")], axis=1)
    gng = twice(f("gdn_norm_g"))
    prm = np.concatenate([
        tiles(f("norm_mix_g")), tiles(f("norm_x_g")), tiles(f("norm_mem_g")), tiles(f("norm_ffn_g")),
        *([twice(f("da_q_norm_g"))] * 4), *([twice(f("da_k_norm_g"))] * 4), f("da_sub_norm_g")[:, :, None], cw, cb,
        rows(np.concatenate([f("ssd_dt_bias"), f("gdn_dt_bias")], axis=1)),
        rows(np.concatenate([f("ssd_A_log"), f("gdn_A_log")], axis=1)),
        rows(f("ssd_D")), tiles(f("ssd_norm_g")), gng, gng, tiles(f("xq_norm_g")), tiles(f("xk_norm_g")),
        rows(li[:, None]), rows(np.array([1.0 - (0.8 - 0.6 * math.exp(-0.3 * l)) for l in range(L)], np.float32)[:, None]),
        rows(lamv)], axis=2)
    i = np.arange(P)
    con = np.zeros((P, NCON), np.float32)
    put = lambda n, a: con.__setitem__((slice(None), slice(*CC[n])), a)
    put("idn", np.eye(P))
    put("ones", 1.0)
    put("blk", i[:, None] // 64 == i[None, :] // 64)
    put("tri", i[:, None] <= i[None, :])
    put("negq", np.where(i[None, :] > i[:, None], -1e30, 0.0))
    put("negd", np.where(i[None, :] < i[:, None], -1e30, 0.0))
    levels = []
    for v in range(NLEV):
        b = 1 << v
        same = (i[:, None] // (2 * b)) == (i[None, :] // (2 * b))
        levels.append(same & (i[:, None] % (2 * b) < b) & (i[None, :] % (2 * b) >= b))
    put("lev", np.concatenate(levels, axis=1))
    c = np.ascontiguousarray
    return {"x": c(f("x")[0]), "mem": c(f("mem")[0]), "wa": c(wa), "wd": c(wd), "wsm": c(wsm), "prm": c(prm), "con": con}


def kernel(**inputs):
    import concourse.bacc as _bacc
    from concourse.bass_utils import run_bass_kernel_spmd as _run

    nc = _bacc.Bacc("TRN2", target_bir_lowering=False, num_devices=1)
    arrays = layout(inputs)
    args = [nc.dram_tensor(f"in_{n}", a.shape, mybir.dt.from_np(a.dtype), kind="ExternalInput").ap()
            for n, a in arrays.items()]
    out = nc.dram_tensor("out_x", (SEQ, D_MODEL), F32, kind="ExternalOutput").ap()
    trunk(nc, *args, out)
    r = _run(nc, [{f"in_{n}": a for n, a in arrays.items()}], core_ids=[0])
    return r.results[0]["out_x"].reshape(1, SEQ, D_MODEL)
```
